# Optimizing a Trainium2 kernel written in Bass

```python
import math
import jax
import jax.numpy as jnp
from jax import lax
import numpy as np

D_MODEL = 2048
BATCH = 1
SEQ = 256
DEPTH = 1
DEC_BATCH = 8
DEC_SEQ = 4
PAST_LEN = 2048
PAGE_SIZE = 128

HEAD_DIM = 64
A_WINDOW = 128
A_Q_HEADS = 16
A_KV_HEADS = 2
A_GROUP = A_Q_HEADS // A_KV_HEADS
B_PATTERNS = ((128, 1), (512, 4), (2048, 16))
B_N_GROUPS = 3
B_HEADS = 8
N_HEADS_TOTAL = A_Q_HEADS + B_N_GROUPS * B_HEADS
NUM_BUCKETS = 32
REL_MAX_DIST = 2048
BLOCK = 128
D_FF = -(-8 * D_MODEL // (3 * 256)) * 256
ALPHA = (2 * DEPTH) ** 0.25
BETA = (8 * DEPTH) ** -0.25
SCALE = HEAD_DIM ** -0.5
LN_EPS = 1e-5
A_OUT_W = A_Q_HEADS * HEAD_DIM
A_KV_W = A_KV_HEADS * HEAD_DIM
B_QKV_W = B_N_GROUPS * B_HEADS * HEAD_DIM
B_OUT_W = B_HEADS * HEAD_DIM
SPLIT_POINTS = (A_OUT_W, A_OUT_W + A_KV_W, A_OUT_W + 2 * A_KV_W, A_OUT_W + 2 * A_KV_W + B_QKV_W, A_OUT_W + 2 * A_KV_W + 2 * B_QKV_W, A_OUT_W + 2 * A_KV_W + 3 * B_QKV_W, A_OUT_W + 2 * A_KV_W + 3 * B_QKV_W + D_MODEL)
IN_W = A_OUT_W + 2 * A_KV_W + 3 * B_QKV_W + 2 * D_MODEL

kernel_name = 'hybrid_swa_sink_dilated_gated_step'

def rel_bucket(dist):
    max_exact = NUM_BUCKETS // 2
    d = jnp.maximum(dist, 0)
    ratio = jnp.maximum(d, max_exact).astype(jnp.float32) / max_exact
    large = max_exact + (jnp.log(ratio) / math.log(REL_MAX_DIST / max_exact) * (NUM_BUCKETS - max_exact)).astype(jnp.int32)
    return jnp.where(d < max_exact, d, jnp.minimum(large, NUM_BUCKETS - 1))

def rel_bias_for(rel_bias, dist, h0, nh):
    return jnp.moveaxis(rel_bias[rel_bucket(dist), h0:h0 + nh], -1, 0).astype(jnp.float32)

def softmax_weights(s, sink):
    m = jnp.max(s, axis=-1, keepdims=True)
    if sink is not None:
        m = jnp.maximum(m, sink)
    p = jnp.exp(s - m)
    l = jnp.sum(p, axis=-1, keepdims=True)
    if sink is not None:
        l = l + jnp.exp(sink - m)
    return p / l, (m + jnp.log(l))[..., 0]

def layer_norm(x, g, b):
    xf = x.astype(jnp.float32)
    mu = jnp.mean(xf, axis=-1, keepdims=True)
    var = jnp.mean(jnp.square(xf - mu), axis=-1, keepdims=True)
    return ((xf - mu) * lax.rsqrt(var + LN_EPS) * g.astype(jnp.float32) + b.astype(jnp.float32)).astype(x.dtype)

def in_proj(x, w):
    b, s = x.shape[:2]
    h = jnp.einsum('bsd,de->bse', x, w)
    qa, ka, va, qb, kb, vb, ga, gb = jnp.split(h, SPLIT_POINTS, axis=-1)
    return (qa.reshape(b, s, A_KV_HEADS, A_GROUP, HEAD_DIM),
            ka.reshape(b, s, A_KV_HEADS, HEAD_DIM),
            va.reshape(b, s, A_KV_HEADS, HEAD_DIM),
            qb.reshape(b, s, B_N_GROUPS, B_HEADS, HEAD_DIM),
            kb.reshape(b, s, B_N_GROUPS, B_HEADS, HEAD_DIM),
            vb.reshape(b, s, B_N_GROUPS, B_HEADS, HEAD_DIM),
            ga, gb)

def banded_attention(q, k, v, max_dist, dist_scale, rel_bias, h0, sink):
    n, L, kvh, g, dh = q.shape
    nb = -(-L // BLOCK)
    pad = nb * BLOCK - L
    qb = jnp.pad(q, ((0, 0), (0, pad), (0, 0), (0, 0), (0, 0))).reshape(n, nb, BLOCK, kvh, g, dh)

    def band(t):
        t = jnp.pad(t, ((0, 0), (BLOCK, pad), (0, 0), (0, 0))).reshape(n, nb + 1, BLOCK, kvh, dh)
        return jnp.concatenate([t[:, :-1], t[:, 1:]], axis=2)

    kb, vb = band(k), band(v)
    dist = jnp.arange(BLOCK)[:, None] + BLOCK - jnp.arange(2 * BLOCK)[None, :]
    key_pos = jnp.arange(nb)[:, None, None] * BLOCK + jnp.arange(2 * BLOCK)[None, None, :] - BLOCK
    valid = (dist >= 0) & (dist <= max_dist) & (key_pos >= 0)
    bias = rel_bias_for(rel_bias, dist * dist_scale, h0, kvh * g).reshape(kvh, g, BLOCK, 2 * BLOCK)
    s = jnp.einsum('nbqkgd,nbckd->nbkgqc', qb, kb, preferred_element_type=jnp.float32) * SCALE + bias
    s = jnp.where(valid[None, :, None, None], s, -jnp.inf)
    sink_b = None if sink is None else sink[None, None, :, :, None, None].astype(jnp.float32)
    p, lse = softmax_weights(s, sink_b)
    o = jnp.einsum('nbkgqc,nbckd->nbqkgd', p.astype(v.dtype), vb).reshape(n, nb * BLOCK, kvh, g, dh)[:, :L]
    lse = jnp.transpose(lse, (0, 1, 4, 2, 3)).reshape(n, nb * BLOCK, kvh, g)[:, :L]
    return o, lse

def to_residues(t, d):
    b, s = t.shape[:2]
    return jnp.moveaxis(t.reshape(b, s // d, d, *t.shape[2:]), 2, 1).reshape(b * d, s // d, *t.shape[2:])

def from_residues(t, d, b):
    n, m = t.shape[:2]
    return jnp.moveaxis(t.reshape(b, d, m, *t.shape[2:]), 1, 2).reshape(b, m * d, *t.shape[2:])

def dilated_attention_prompt(q, k, v, win, dil, rel_bias, h0):
    b = q.shape[0]
    o, lse = banded_attention(to_residues(q, dil)[:, :, :, None], to_residues(k, dil), to_residues(v, dil),
                              win // dil, dil, rel_bias, h0, None)
    return from_residues(o[:, :, :, 0], dil, b), from_residues(lse[..., 0], dil, b)

def window_attention_step(q, k, v, cache, rel_bias, sink):
    t = q.shape[1]
    lc = cache.shape[1]
    kv_all = jnp.concatenate([cache, jnp.stack([k, v], axis=2)], axis=1)
    dist = (lc + jnp.arange(t))[:, None] - jnp.arange(lc + t)[None, :]
    valid = (dist >= 0) & (dist < A_WINDOW)
    bias = rel_bias_for(rel_bias, dist, 0, A_Q_HEADS).reshape(A_KV_HEADS, A_GROUP, t, lc + t)
    s = jnp.einsum('btkgd,bckd->bkgtc', q, kv_all[:, :, 0], preferred_element_type=jnp.float32) * SCALE + bias
    s = jnp.where(valid, s, -jnp.inf)
    p, _ = softmax_weights(s, sink[None, :, :, None, None].astype(jnp.float32))
    o = jnp.einsum('bkgtc,bckd->btkgd', p.astype(v.dtype), kv_all[:, :, 1])
    return o, kv_all[:, t:]

def dilated_attention_step(q, k, v, cache, win, dil, rel_bias, h0):
    t = q.shape[1]
    lc = cache.shape[1]
    n_keys = win // dil + 1
    kv_all = jnp.concatenate([cache, jnp.stack([k, v], axis=2)], axis=1)
    idx = lc + jnp.arange(t)[:, None] - jnp.arange(n_keys)[None, :] * dil
    valid = idx >= 0
    kvg = jnp.take(kv_all, jnp.maximum(idx, 0), axis=1)
    bias = rel_bias_for(rel_bias, jnp.arange(n_keys) * dil, h0, B_HEADS)
    s = jnp.einsum('bthd,btjhd->bhtj', q, kvg[:, :, :, 0], preferred_element_type=jnp.float32) * SCALE + bias[:, None, :]
    s = jnp.where(valid, s, -jnp.inf)
    p, lse = softmax_weights(s, None)
    o = jnp.einsum('bhtj,btjhd->bthd', p.astype(v.dtype), kvg[:, :, :, 1])
    return o, jnp.moveaxis(lse, 1, 2), kv_all[:, t:]

def combine_dilations(outs, lses):
    w = jax.nn.softmax(jnp.stack(lses, axis=0), axis=0)
    o = jnp.einsum('gbsh,gbshd->bshd', w, jnp.stack(outs, axis=0).astype(jnp.float32))
    return o.reshape(o.shape[0], o.shape[1], B_OUT_W).astype(outs[0].dtype)

def merge_and_ffn(x, oa, ob, ga, gb, w_oa, w_ob, w_out, ln1_g, ln1_b, w_ffn_in, w_ffn_out, ln2_g, ln2_b):
    b, s = x.shape[:2]
    pa = oa.reshape(b, s, A_OUT_W) @ w_oa
    pb = ob @ w_ob
    mix = (jax.nn.sigmoid(ga) * pa + jax.nn.sigmoid(gb) * pb) @ w_out
    h = layer_norm(ALPHA * x + mix, ln1_g, ln1_b)
    gate, up = jnp.split(h @ w_ffn_in, 2, axis=-1)
    f = (jax.nn.silu(gate) * up) @ w_ffn_out
    return layer_norm(ALPHA * h + f, ln2_g, ln2_b)

def setup_inputs(seed: int = 0) -> dict:
    key = jax.random.key(seed)
    ks = jax.random.split(key, 20)

    def nrm(k, shape, scale=1.0):
        return jax.random.normal(k, shape, jnp.float32) * scale

    return {
        'x_prompt': nrm(ks[0], (BATCH, SEQ, D_MODEL)),
        'x_sample': nrm(ks[1], (DEC_BATCH, DEC_SEQ, D_MODEL)),
        'cache_a': nrm(ks[2], (DEPTH, DEC_BATCH, min(A_WINDOW, PAST_LEN), 2, A_KV_HEADS, HEAD_DIM)),
        'cache_b1': nrm(ks[3], (DEPTH, DEC_BATCH, min(B_PATTERNS[0][0], PAST_LEN), 2, B_HEADS, HEAD_DIM)),
        'cache_b2': nrm(ks[4], (DEPTH, DEC_BATCH, min(B_PATTERNS[1][0], PAST_LEN), 2, B_HEADS, HEAD_DIM)),
        'cache_b3': nrm(ks[5], (DEPTH, DEC_BATCH, min(B_PATTERNS[2][0], PAST_LEN), 2, B_HEADS, HEAD_DIM)),
        'rel_bias': nrm(ks[6], (NUM_BUCKETS, N_HEADS_TOTAL), 0.5),
        'w_in': nrm(ks[7], (DEPTH, D_MODEL, IN_W), D_MODEL ** -0.5),
        'a_sink': nrm(ks[8], (DEPTH, A_Q_HEADS), 0.5),
        'w_oa': nrm(ks[9], (DEPTH, A_OUT_W, D_MODEL), A_OUT_W ** -0.5),
        'w_ob': nrm(ks[10], (DEPTH, B_OUT_W, D_MODEL), B_OUT_W ** -0.5),
        'w_out': nrm(ks[11], (DEPTH, D_MODEL, D_MODEL), BETA * D_MODEL ** -0.5),
        'ln1_g': 1.0 + nrm(ks[12], (DEPTH, D_MODEL), 0.05),
        'ln1_b': nrm(ks[13], (DEPTH, D_MODEL), 0.02),
        'w_ffn_in': nrm(ks[14], (DEPTH, D_MODEL, 2 * D_FF), D_MODEL ** -0.5),
        'w_ffn_out': nrm(ks[15], (DEPTH, D_FF, D_MODEL), BETA * D_FF ** -0.5),
        'ln2_g': 1.0 + nrm(ks[16], (DEPTH, D_MODEL), 0.05),
        'ln2_b': nrm(ks[17], (DEPTH, D_MODEL), 0.02),
    }

def reference(x_prompt, x_sample, cache_a, cache_b1, cache_b2, cache_b3, rel_bias, w_in, a_sink, w_oa, w_ob,
              w_out, ln1_g, ln1_b, w_ffn_in, w_ffn_out, ln2_g, ln2_b):
    caches_b = (cache_b1, cache_b2, cache_b3)
    xp, xs = x_prompt, x_sample
    new_a_p, new_a_s = [], []
    new_b_p = [[], [], []]
    new_b_s = [[], [], []]
    for l in range(DEPTH):
        sink = a_sink[l].reshape(A_KV_HEADS, A_GROUP)
        ffn_args = (w_oa[l], w_ob[l], w_out[l], ln1_g[l], ln1_b[l], w_ffn_in[l], w_ffn_out[l], ln2_g[l], ln2_b[l])

        qa, ka, va, qb, kb, vb, ga, gb = in_proj(xp, w_in[l])
        seq = xp.shape[1]
        oa, _ = banded_attention(qa, ka, va, A_WINDOW - 1, 1, rel_bias, 0, sink)
        la = min(A_WINDOW, seq)
        new_a_p.append(jnp.stack([ka[:, seq - la:], va[:, seq - la:]], axis=2))
        outs, lses = [], []
        for g, (win, dil) in enumerate(B_PATTERNS):
            o, lse = dilated_attention_prompt(qb[:, :, g], kb[:, :, g], vb[:, :, g], win, dil, rel_bias,
                                              A_Q_HEADS + g * B_HEADS)
            outs.append(o)
            lses.append(lse)
            lb = min(win, seq)
            new_b_p[g].append(jnp.stack([kb[:, seq - lb:, g], vb[:, seq - lb:, g]], axis=2))
        ob = combine_dilations(outs, lses)
        xp_next = merge_and_ffn(xp, oa, ob, ga, gb, *ffn_args)

        qa, ka, va, qb, kb, vb, ga, gb = in_proj(xs, w_in[l])
        oa, buf_a = window_attention_step(qa, ka, va, cache_a[l], rel_bias, sink)
        new_a_s.append(buf_a)
        outs, lses = [], []
        for g, (win, dil) in enumerate(B_PATTERNS):
            o, lse, buf_b = dilated_attention_step(qb[:, :, g], kb[:, :, g], vb[:, :, g], caches_b[g][l], win, dil,
                                                   rel_bias, A_Q_HEADS + g * B_HEADS)
            outs.append(o)
            lses.append(lse)
            new_b_s[g].append(buf_b)
        ob = combine_dilations(outs, lses)
        xs_next = merge_and_ffn(xs, oa, ob, ga, gb, *ffn_args)
        xp, xs = xp_next, xs_next

    return (xp, xs,
            jnp.stack(new_a_p, axis=0), jnp.stack(new_b_p[0], axis=0), jnp.stack(new_b_p[1], axis=0), jnp.stack(new_b_p[2], axis=0),
            jnp.stack(new_a_s, axis=0), jnp.stack(new_b_s[0], axis=0), jnp.stack(new_b_s[1], axis=0), jnp.stack(new_b_s[2], axis=0))


_drawn_inputs = setup_inputs


def setup_inputs(seed=0):
    import zlib

    import numpy as np

    out = dict(_drawn_inputs(seed))
    spreads = {}
    factors = {'a_sink': 26.102, 'ln1_b': 2.672, 'ln2_b': 2.83}
    for name, (base, spread) in spreads.items():
        noise = np.random.default_rng([zlib.crc32(name.encode()), seed]).standard_normal(out[name].shape)
        drawn = base * np.exp(spread * noise) if base else spread * noise
        out[name] = jnp.asarray(drawn.astype(out[name].dtype))
    for name, factor in factors.items():
        out[name] = (out[name] * factor).astype(out[name].dtype)
    return out
```

```python
import math
from contextlib import ExitStack

import numpy as np

import concourse.bass as bass
from concourse import mybir

F32 = mybir.dt.float32
F32R = mybir.dt.float32r
ALU = mybir.AluOpType
ACT = mybir.ActivationFunctionType
AX = mybir.AxisListType.X

P = 128
D = 2048
SEQ = 256
DB, DS = 8, 4
NS = DB * DS
T = SEQ + NS
KT = D // P
DH = 64
QH, KVH = 16, 2
BH, BG = 8, 3
DIL = (1, 4, 16)
WIN = (128, 512, 2048)
FF = 5632
FT_HALF = FF // P // 2
NH = QH + BG * BH
BUCKETS = 32
ALPHA = 2.0 ** 0.25
SCALE = DH ** -0.5
EPS = 1e-5
NEG = -1e30
LOW = -3.0e38
C_QA, C_KVA, C_QB, C_GATE = 0, 1024, 1280, 5888
IN_W = 9984
CK = 1024
RING = 4
AHEAD = 3
NKEY_B = 3 * P + 3 * NS
NKEY_A = P + NS


def bucket(dist):
    d = max(int(dist), 0)
    if d < 16:
        return d
    return min(16 + int(math.log(d / 16) / math.log(2048 / 16) * 16), 31)


def constants():
    ohp = np.zeros((BUCKETS, 384), np.float32)
    maskp = np.full((NH, 384), NEG, np.float32)
    for i in range(384):
        dist = 255 - i
        ohp[bucket(dist), i] = 1
        if 0 <= dist < 128:
            maskp[:QH, i] = 0
        for g in range(BG):
            if 0 <= dist <= WIN[g] and dist % DIL[g] == 0:
                maskp[QH + g * BH:QH + (g + 1) * BH, i] = 0
    ohb = np.zeros((P, NKEY_B), np.float32)
    oha = np.zeros((P, NKEY_A), np.float32)
    maskb = np.zeros((P, 2, NKEY_B), np.float32)
    maska = np.zeros((P, 2, 2, NKEY_A), np.float32)
    for t in range(DS):
        for n in range(P):
            ohb[32 * t + bucket(128 + t - n), n] = 1
            ohb[32 * t + bucket(4 * (128 - n)), P + n] = 1
            ohb[32 * t + bucket(16 * (128 - n)), 2 * P + n] = 1
            oha[32 * t + bucket(128 + t - n), n] = 1
        for k in range(NS):
            oha[32 * t + bucket(t - k % DS), P + k] = 1
            for g in range(BG):
                ohb[32 * t + bucket(t - k % DS), 3 * P + NS * g + k] = 1
    for r in range(P):
        b4, t = r // 32, r % DS
        for bb in range(2):
            b = bb * 4 + b4
            for n in range(P):
                if 128 + t - n > 128:
                    maskb[r, bb, n] = NEG
                if 128 + t - n > 127:
                    maska[r, bb, :, n] = NEG
            for k in range(NS):
                kb, kt = k // DS, k % DS
                if kb != b or kt > t:
                    maska[r, bb, :, P + k] = NEG
                    maskb[r, bb, 3 * P + k] = NEG
                if kb != b or kt != t:
                    maskb[r, bb, 3 * P + NS + k] = NEG
                    maskb[r, bb, 3 * P + 2 * NS + k] = NEG
    return {"ohp": ohp, "maskp": maskp, "ohb": ohb, "oha": oha, "maskb": maskb, "maska": maska,
            "ident": np.eye(P, dtype=np.float32),
            "rowsel": (np.arange(P)[None, :] // DS % 8 == np.arange(8)[:, None]).astype(np.float32)}


class Phase:

    def __init__(self, chunk0, tile0, set0, groups, chunks, tiles=4, sets=1):
        self.chunk0, self.tile0, self.set0, self.groups, self.chunks = chunk0, tile0, set0, groups, chunks
        self.tiles, self.sets = tiles, sets

    def after(self, groups, chunks, tiles=4, sets=1):
        return Phase(self.chunk0 + self.groups * self.chunks, self.tile0 + self.groups * self.tiles * self.sets,
                     self.set0 + self.groups * (self.tiles - 1) * self.sets, groups, chunks, tiles, sets)

    def tile_done(self, i, set_, m, last_chunk):
        if m == self.tiles - 1:
            return 1, self.chunk0 + self.chunks * i + last_chunk + 1
        return 0, self.set0 + (self.tiles - 1) * (self.sets * i + set_) + m + 1


PH_QB = Phase(0, 0, 0, 3, 8)
PH_KB = PH_QB.after(3, 8)
PH_VB = PH_KB.after(3, 8)
PH_QA = PH_VB.after(2, 8)
PH_KVA = PH_QA.after(1, 4, 2)
PH_GATE = PH_KVA.after(8, 8)
PH_MERGE = PH_GATE.after(2, 12, 4, 2)
PH_OUT = PH_MERGE.after(4, 8)
PH_F1 = [PH_OUT.after(11, 8, 2, 2), None]
PH_F2 = [PH_F1[0].after(1, 44, 4, 4), None]
PH_F1[1] = PH_F2[0].after(11, 8, 2, 2)
PH_F2[1] = PH_F1[1].after(1, 44, 4, 4)
CHUNKS = PH_F2[1].chunk0 + 44
FREE0 = PH_GATE.tile0

UNITS = [[(h, "a", h, 0)] for h in range(QH)] + \
        [[(QH + BG * h + g, "b", h, g) for g in range(BG)] for h in range(BH)]
TABLE_ROWS = [h for h in range(QH)] + [QH + BH * g + h for h in range(BH) for g in range(BG)]


def build(nc, x_prompt, x_sample, cache_a, cache_b1, cache_b2, cache_b3, rel_bias, w_in, a_sink, w_oa,
          w_ob, w_out, ln1_g, ln1_b, w_ffn_in, w_ffn_out, ln2_g, ln2_b,
          ohp, maskp, ohb, oha, maskb, maska, ident_in, rowsel,
          y_p, y_s, na_p, nb1_p, nb2_p, nb3_p, na_s, nb1_s, nb2_s, nb3_s):
    caches = (cache_b1, cache_b2, cache_b3)
    nb_p, nb_s = (nb1_p, nb2_p, nb3_p), (nb1_s, nb2_s, nb3_s)
    tok_dram = nc.dram_tensor("tok_scratch", [3, BG, NS, 512], F32, kind="Internal").ap()
    toka_dram = nc.dram_tensor("toka_scratch", [2, NS, P], F32, kind="Internal").ap()
    tz_dram = nc.dram_tensor("bias_scratch", [NH, 384], F32, kind="Internal").ap()

    with ExitStack() as ctx:
        base = (nc.sbuf_base + 63) // 64 * 64

        def at(name, shape, offset, dt=F32):
            return nc.alloc_sbuf_tensor_at(name, shape, dt, offset=base + offset)

        TB = T * 4
        raw = [at(f"raw{s}", [P, CK], 4096 * s) for s in range(RING)]
        whi = [at(f"whi{s}", [P, CK], 16384 + 4096 * s, F32R) for s in range(RING)]
        wlo = [at(f"wlo{s}", [P, CK], 32768 + 4096 * s, F32R) for s in range(RING)]
        XH = at("XH", [P, KT, T], 49152, F32R)
        XL = at("XL", [P, KT, T], 67584, F32R)
        R1 = 86016
        xs_p = at("xs_p", [P, 2, D], R1)
        xs_s = at("xs_s", [NS, D], R1 + 16384)
        QB = at("QB", [P, 12, T], R1)
        KB = at("KB", [P, 12, T], R1 + 12 * TB)
        QA = at("QA", [P, 8, T], R1 + 24 * TB)
        KD = at("KD", [P, 2, T], R1 + 32 * TB)
        GT = at("GT", [P, 32, T], R1)
        R2 = 125184
        VTOK = at("VTOK", [P, 2, BG, 512], R2)
        VAT = at("VAT", [P, 2, P], R2 + 12288)
        PTB = at("PTB", [P, BG, 2, P], R2)
        PTN = at("PTN", [96, 2, P], R2 + 3072)
        PTA = at("PTA", [P, 2, 2, P], R2 + 4096)
        PTNA = at("PTNA", [NS, 2, 2, P], R2 + 6144)
        C1 = at("C1", [P, 2, 512], R2 + 8192)
        CA = at("CA", [P, 2, P], R2 + 12288)
        R3 = 138496
        KTOK = at("KTOK", [P, 2, BG, 512], R3)
        KAT = at("KAT", [P, 2, P], R3 + 12288)
        BIAS = at("BIAS", [P, 4, 256], R3)
        SP_ = at("SP_", [P, 2, BG, 384], R3 + 4096)
        PT = at("PT", [P, 3, 384], R3 + 13312)
        QBD = at("QBD", [P, BG, 4, DB, 32], R3)
        KTS = at("KTS", [P, 2, 512], R3 + 12288)
        R4 = 156416
        OT = at("OT", [P, 12, T], R4)
        TOKS = at("TOKS", [NS, BG, 512], R4)
        TOKA = at("TOKA", [NS, 2, P], R4 + 6144)
        FT = at("FT", [P, 4, T], R4 + 7168)
        KAF = at("KAF", [P, T], R4 + 7168 + 4 * TB)
        R5 = 170240
        KST = at("KST", [P, 2, 2, 512], R5)
        QST = at("QST", [P, 2, 2, 512], R5 + 8192)
        PROD = at("PROD", [P, 1024], R5 + 16384)
        OHP = at("OHP", [BUCKETS, 384], R5)
        TZ = at("TZ", [NH, 384], R5 + 1536)
        VST = at("VST", [P, 2, DS, 512], R5)
        OHB = at("OHB", [P, NKEY_B], R5)
        OHA = at("OHA", [P, NKEY_A], R5 + 1920)
        RELT = at("RELT", [P, 5, P], R5 + 2560)
        BIB = at("BIB", [P, 2, NKEY_B], R5 + 16384)
        ST = at("ST", [P, 2, 256], 190720)
        VN = at("VN", [96, 512], 192768)
        VNA = at("VNA", [NS, P], 194816)
        QAS = at("QAS", [64, 2, DB, 8, DS], 195328)
        SRB = at("SRB", [P, 2, NKEY_B], 197376)
        SRA = at("SRA", [P, 2, 2, NKEY_A], 201216)
        BIA = at("BIA", [P, 2, 2, NKEY_A], 203776)
        OTH = at("OTH", [P, 12, T], R2, F32R)
        OTL = at("OTL", [P, 12, T], R2 + 13824, F32R)
        MT = at("MT", [P, 3, T], R2 + 27648)
        MH = at("MH", [P, KT, T], R5, F32R)
        ML = at("ML", [P, KT, T], R5 + 18432, F32R)
        U = at("U", [P, KT, T], R1)
        SUM = at("SUM", [P, T], R1 + 18432)
        MU = at("MU", [P, T], R1 + 19584)
        RS = at("RS", [P, T], R1 + 20736)
        SQ = at("SQ", [P, 4, T], R1 + 21888)
        X1H = at("X1H", [P, KT, T], 49152, F32R)
        X1L = at("X1L", [P, KT, T], 67584, F32R)
        HH = at("HH", [P, FT_HALF, T], R2, F32R)
        HL = at("HL", [P, FT_HALF, T], R2 + 25344, F32R)
        SG = at("SG", [P, 2, T], R2 + 50688)
        HT = at("HT", [P, 2, T], R2 + 52992)
        HF = at("HF", [P, 2, T], R2 + 55296)
        YT = at("YT", [P, 2, D], R2)
        YTS = at("YTS", [NS, D], R2 + 16384)
        R6 = 208704
        ident = at("ident", [P, P], R6)
        ones = at("ones", [P, P], R6 + 512)
        LNP = at("LNP", [P, 4, KT], R6 + 1024)
        REL4 = at("REL4", [P, NH], R6 + 1280)
        SINKB = at("SINKB", [P, QH], R6 + 1440)
        SINKR = at("SINKR", [P, 2], R6 + 1504)
        NM = at("NM", [P, 2, 2], R6 + 1536)
        MX = at("MX", [P, 2, 2, BG], R6 + 1568)
        LS = at("LS", [P, 2, 2], R6 + 1632)
        ES = at("ES", [P, 2, 2], R6 + 1664)
        RL = at("RL", [P, 2, 2], R6 + 1696)
        SMX = at("SMX", [P, 6], R6 + 1728)
        SNM = at("SNM", [P, 6], R6 + 1760)
        SLS = at("SLS", [P, 6], R6 + 1792)
        SES = at("SES", [P, 6], R6 + 1824)
        SRL = at("SRL", [P, 6], R6 + 1856)
        EPSC = at("EPSC", [P, 1], R6 + 1888)
        lnrow = at("lnrow", [64, P], R6 + 1920)
        ROWSEL = at("ROWSEL", [8, P], R6 + 2432)
        QLO = at("QLO", [64, 8, NS], R6 + 3072)
        SINK2 = at("SINK2", [8, 2], R6 + 2944)

        bank = [ctx.enter_context(nc.psum_tensor(f"bank{i}", [P, 512], F32)) for i in range(8)]

        def sem(name):
            return ctx.enter_context(nc.semaphore(name))

        x_in = sem("x_in"); const_in = sem("const_in"); ln_in = sem("ln_in")
        raw_in = [sem(f"raw_in{s}") for s in range(RING)]
        hi_done, lo_done, chunk_used = sem("hi_done"), sem("lo_done"), sem("chunk_used")
        tile_ready, tile_free = sem("tile_ready"), sem("tile_free")
        pb_ready, pb_free = sem("pb_ready"), sem("pb_free")
        xt_ready, xh_done, xl_done = sem("xt_ready"), sem("xh_done"), sem("xl_done")
        setup_pe, setup_dve = sem("setup_pe"), sem("setup_dve")
        tz_out = sem("tz_out")
        ft_ready, ft_turned, ft_copied, tok_ready = sem("ft_ready"), sem("ft_turned"), sem("ft_copied"), sem("tok_ready")
        tok_out = sem("tok_out"); toka_out = sem("toka_out"); kv_out = sem("kv_out")
        new_out = sem("new_out"); copy_out = sem("copy_out")
        unit_in = [sem("unit_in0"), sem("unit_in1")]
        unit_done = sem("unit_done"); prod_done = sem("prod_done")
        kd_in = sem("kd_in"); qas_in = sem("qas_in"); qas_own = sem("qas_own")
        bias_in = [sem(f"bias_in{i}") for i in range(4)]
        s_ready, s_read, m_ready, nm_ready, e_ready, p_ready = (
            sem("s_ready"), sem("s_read"), sem("m_ready"), sem("nm_ready"), sem("e_ready"), sem("p_ready"))
        t_ready, pt_ready, pt_used, o_read = sem("t_ready"), sem("pt_ready"), sem("pt_used"), sem("o_read")
        chain = sem("chain")
        relt_zero, relt_done, qbd_zero, qbd_done = sem("relt_zero"), sem("relt_done"), sem("qbd_zero"), sem("qbd_done")
        samp_in = sem("samp_in"); vn_in = sem("vn_in")
        rowbias_pe, rowbias_done = sem("rowbias_pe"), sem("rowbias_done")
        ck_in = [sem("ck_in0"), sem("ck_in1")]
        kts_pe = sem("kts_pe"); kts_ready = sem("kts_ready"); kts_used = sem("kts_used")
        rows_ready, rows_m, rows_e, rows_p = sem("rows_ready"), sem("rows_m"), sem("rows_e"), sem("rows_p")
        rt_pe, rt_done = sem("rt_pe"), sem("rt_done")
        v_in = [sem("v_in0"), sem("v_in1")]
        v_used = sem("v_used"); cv_in = [sem("cv_in0"), sem("cv_in1")]; cv_used = sem("cv_used")
        os_read = sem("os_read")
        oth_done, otl_done = sem("oth_done"), sem("otl_done")
        mix_done, mh_done, ml_done = sem("mix_done"), sem("mh_done"), sem("ml_done")
        sum_done, sum_pe, mu_done, cen_done, sq_done, sq_used, sd_done, rs_done, nrm_done, y_done, x1h_done, x1l_done = (
            sem("sum_done"), sem("sum_pe"), sem("mu_done"), sem("cen_done"), sem("sq_done"), sem("sq_used"),
            sem("sd_done"), sem("rs_done"), sem("nrm_done"), sem("y_done"), sem("x1h_done"), sem("x1l_done"))
        sg_done, hh_done, hl_done = sem("sg_done"), sem("hh_done"), sem("hl_done")
        yt_pe, yt_done, y_out = sem("yt_pe"), sem("yt_done"), sem("y_out")

        block = ctx.enter_context(nc.Block())

        def loop(eng, ph, body):
            start = 0
            if ph.chunk0 == 0:
                body(0)
                start = 1
            if ph.groups - start == 1:
                body(start)
            else:
                with eng.Fori(start, ph.groups) as i:
                    body(i)

        def known_below(value, limit):
            return isinstance(value, int) and value < limit

        @block.sync
        def _(sp):
            sp.dma_start(xs_p[:, :, :], x_prompt[0].rearrange("(n p) d -> p n d", p=P)).then_inc(x_in, 16)
            sp.dma_start(xs_s[:, :], x_sample.rearrange("b t d -> (b t) d")).then_inc(x_in, 16)
            sp.dma_start(ident[:, :], ident_in).then_inc(x_in, 16)

            def chunk(ph, i, k, src, shape=None):
                c = ph.chunk0 + ph.chunks * i + k
                if not known_below(c, RING):
                    sp.wait_ge(lo_done, c - RING + 1)
                dst = raw[k % RING][:, :]
                if shape:
                    dst = dst.rearrange(*shape[0], **shape[1])
                sp.dma_start(dst, src).then_inc(raw_in[k % RING], 16)

            def rows(w):
                return w.rearrange("(k p) e -> p k e", p=P)

            two = (("p (k e) -> p k e",), {"k": 2})
            four = (("p (k e) -> p k e",), {"k": 4})
            win = rows(w_in[0])
            for ph, col in ((PH_QB, C_QB), (PH_KB, C_QB + 1536), (PH_VB, C_QB + 3072), (PH_QA, C_QA)):
                def body(i, ph=ph, col=col):
                    for k in range(8):
                        chunk(ph, i, k, win[:, 2 * k:2 * k + 2, bass.ds(col + 512 * i, 512)], two)
                loop(sp, ph, body)
            for k in range(4):
                chunk(PH_KVA, 0, k, win[:, 4 * k:4 * k + 4, C_KVA:C_KVA + 256], four)
                if k == 0:
                    sp.dma_start(lnrow[0:16, :], ln1_g[0].rearrange("(k p) -> k p", p=P)).then_inc(ln_in, 16)
                    sp.dma_start(lnrow[16:32, :], ln1_b[0].rearrange("(k p) -> k p", p=P)).then_inc(ln_in, 16)
                    sp.dma_start(lnrow[32:48, :], ln2_g[0].rearrange("(k p) -> k p", p=P)).then_inc(ln_in, 16)
                    sp.dma_start(lnrow[48:64, :], ln2_b[0].rearrange("(k p) -> k p", p=P)).then_inc(ln_in, 16)

            def gates(i):
                for k in range(8):
                    chunk(PH_GATE, i, k, win[:, 2 * k:2 * k + 2, bass.ds(C_GATE + 512 * i, 512)], two)
            loop(sp, PH_GATE, gates)

            def merge(i):
                for s in range(2):
                    cols = bass.ds(1024 * i + 512 * s, 512)
                    for k in range(4):
                        chunk(PH_MERGE, i, 6 * s + k, rows(w_oa[0])[:, 2 * k:2 * k + 2, cols], two)
                    for k in range(2):
                        chunk(PH_MERGE, i, 6 * s + 4 + k, rows(w_ob[0])[:, 2 * k:2 * k + 2, cols], two)
            loop(sp, PH_MERGE, merge)

            def outp(i):
                for k in range(8):
                    chunk(PH_OUT, i, k, rows(w_out[0])[:, 2 * k:2 * k + 2, bass.ds(512 * i, 512)], two)
            loop(sp, PH_OUT, outp)
            f1 = w_ffn_in[0].rearrange("(k p) (u e) -> p k u e", p=P, u=2)
            f2 = rows(w_ffn_out[0])
            for half in range(2):
                def ffn_in(i, half=half):
                    for k in range(8):
                        chunk(PH_F1[half], i, k,
                              f1[:, 4 * (k // 2):4 * (k // 2) + 4, k % 2, bass.ds(FT_HALF * P * half + 256 * i, 256)], four)
                loop(sp, PH_F1[half], ffn_in)
                for j in range(4):
                    for k in range(11):
                        k0 = FT_HALF * half + 2 * k
                        chunk(PH_F2[half], 0, 11 * j + k, f2[:, k0:k0 + 2, 512 * j:512 * j + 512], two)
            sp.wait_ge(yt_done, KT)
            sp.dma_start(y_p[0].rearrange("(n p) d -> p n d", p=P), YT[:, :, :]).then_inc(y_out, 16)
            sp.dma_start(y_s.rearrange("b t d -> (b t) d"), YTS[:, :]).then_inc(y_out, 16)
            sp.wait_ge(y_out, 32)

        @block.gpsimd
        def _(pool):
            for t in range(DS):
                pool.dma_start(REL4[32 * t:32 * t + 32, :], rel_bias).then_inc(const_in, 16)
            pool.dma_start(OHP[:, :], ohp).then_inc(const_in, 16)
            pool.dma_start(TZ[:, :], maskp).then_inc(const_in, 16)
            pool.dma_start(SINKB[:, :], bass.AP(a_sink.tensor, 0, [[0, P], [1, QH]])).then_inc(const_in, 16)
            pool.dma_start(ROWSEL[:, :], rowsel).then_inc(const_in, 16)
            for kv in range(2):
                pool.dma_start(SINK2[:, kv:kv + 1], bass.AP(a_sink.tensor, 8 * kv, [[1, 8], [1, 1]])).then_inc(const_in, 16)
            pool.wait_ge(setup_dve, 1)
            pool.dma_start(tz_dram, TZ[:, :]).then_inc(tz_out, 16)
            def shift(new, old, first, n, pieces):
                row = old.shape[2] * old.shape[3] * old.shape[4]
                src = old.rearrange("b r k h d -> b (r k h d)")[:, bass.ds(first + DS * row, n)]
                dst = new.rearrange("b r k h d -> b (r k h d)")[:, bass.ds(first, n)]
                pool.dma_start(dst.rearrange("b (x y) -> x b y", x=pieces),
                               src.rearrange("b (x y) -> x b y", x=pieces)).then_inc(copy_out, 16)

            shift(na_s[0], cache_a[0], 0, 124 * 256, 16)
            shift(nb1_s[0], cache_b1[0], 0, 124 * 1024, 16)
            pool.wait_ge(tz_out, 16)

            def token_rows(kind, g):
                pool.dma_start(tok_dram[kind, g], TOKS[:, g, :]).then_inc(tok_out, 16)
                pool.wait_ge(tok_out, 16 * (3 * kind + g + 1))
                if kind:
                    w = WIN[g]
                    pool.dma_start(nb_s[g][0, :, w - 4:w, kind - 1].rearrange("b t h d -> b t (h d)"),
                                   tok_dram[kind, g].rearrange("(b t) f -> b t f", b=DB)).then_inc(new_out, 16)

            def unit_loads(b):
                for j in range(4):
                    g, t0 = 1 + j // 2, 2 * (j % 2)
                    if not known_below(4 * b + j, 2):
                        pool.wait_ge(unit_done, 4 * b + j - 1)
                    keys = caches[g][0].rearrange("b (n r) k h d -> n b r k (h d)", r=DIL[g])
                    pool.dma_start(KST[:, j % 2], keys[:, b, t0:t0 + 2, 0, :]).then_inc(unit_in[j % 2], 16)
                    q = tok_dram[0, g, 4 * b + t0:4 * b + t0 + 2, :].rearrange("t f -> (t f)")
                    pool.dma_start(QST[:, j % 2].rearrange("p t f -> p (t f)"), q.partition_broadcast(P)
                                   ).then_inc(unit_in[j % 2], 16)

            def copy_b2(b):
                shift(nb2_s[0, bass.ds(b, 1)], cache_b2[0, bass.ds(b, 1)], 0, 508 * 1024, 32)

            def copy_b3(n):
                shift(nb3_s[0], cache_b3[0], n * (73 * 1024), 73 * 1024, 16)

            for g in range(BG):
                pool.wait_ge(tok_ready, 4 * (g + 1))
                token_rows(0, g)
            for b in range(8):
                unit_loads(b)
                copy_b2(b)
                if b < 6:
                    pool.wait_ge(tok_ready, 4 * (b + 4))
                    token_rows(1 + b // 3, b % 3)
                if b == 2 or b == 5:
                    kv, src = (0, KTOK) if b == 2 else (1, VTOK)
                    pool.dma_start(nb1_p[0, 0, :, kv].rearrange("p h d -> p (h d)"), src[:, 1, 0, :]).then_inc(kv_out, 16)
                    for g in (1, 2):
                        pool.dma_start(nb_p[g][0, 0, :, kv].rearrange("(n p) h d -> p n (h d)", p=P),
                                       src[:, :, g, :]).then_inc(kv_out, 16)
            pool.dma_start(VN[:, :], tok_dram[2].rearrange("g n f -> (g n) f")).then_inc(vn_in, 16)
            pool.wait_ge(ft_copied, 32)
            pool.dma_start(QLO[:, :, :], QA[64:128, :, SEQ:T]).then_inc(qas_in, 16)
            pool.wait_ge(ft_ready, 45)
            pool.dma_start(KD[0:64, 1, :], KAF[64:128, :]).then_inc(kd_in, 16)
            pool.dma_start(KD[64:128, 0, :], KAF[0:64, :]).then_inc(kd_in, 16)
            pool.dma_start(KD[0:64, 0, :], KAF[0:64, :]).then_inc(kd_in, 16)
            pool.dma_start(KD[64:128, 1, :], KAF[64:128, :]).then_inc(kd_in, 16)
            pool.wait_ge(tok_ready, 38)
            for kv, src in ((0, KAT), (1, VAT)):
                pool.dma_start(na_p[0, 0, :, kv].rearrange("p h d -> p (h d)"), src[:, 1, :]).then_inc(kv_out, 16)
                pool.dma_start(toka_dram[kv], TOKA[:, kv, :]).then_inc(toka_out, 16)
            pool.wait_ge(toka_out, 32)
            for kv in range(2):
                pool.dma_start(na_s[0, :, 124:128, kv].rearrange("b t h d -> b t (h d)"),
                               toka_dram[kv].rearrange("(b t) f -> b t f", b=DB)).then_inc(new_out, 16)
            pool.dma_start(VNA[:, :], toka_dram[1]).then_inc(vn_in, 16)
            pool.wait_ge(kv_out, 16 * 8)
            for n, row in enumerate(TABLE_ROWS):
                if n >= 4:
                    pool.wait_ge(s_read, n - 3)
                pool.dma_start(BIAS[:, n % 4, :], bass.AP(tz_dram.tensor, row * 384, [[1, P], [1, 256]])
                               ).then_inc(bias_in[n % 4], 16)
            pool.wait_ge(unit_done, 32)
            pool.dma_start(OHB[:, :], ohb).then_inc(samp_in, 16)
            pool.dma_start(OHA[:, :], oha).then_inc(samp_in, 16)
            pool.dma_start(BIB[:, :, :], maskb).then_inc(samp_in, 16)
            pool.dma_start(BIA[:, :, :, :], maska).then_inc(samp_in, 16)
            nc.gpsimd.memset(RELT[:, :, :], 0.0).then_inc(relt_zero, 1)
            pool.wait_ge(relt_zero, 1)
            for s, h0 in enumerate((QH, QH + BH, QH + 2 * BH, 0, BH)):
                for t in range(DS):
                    q = slice(32 * t, 32 * t + 32)
                    dst = RELT[q, s, :].rearrange("p (b h t) -> p b h t", b=4, t=DS)[:, :, :, t]
                    nc.gpsimd.tensor_copy(dst, REL4[q, h0:h0 + 8].unsqueeze(1).broadcast_to([32, 4, 8])
                                          ).then_inc(relt_done, 1)
            pool.wait_ge(relt_done, 20)
            pool.wait_ge(pt_used, 40)
            nc.gpsimd.memset(QBD[:, :, :, :, :], 0.0).then_inc(qbd_zero, 1)
            pool.wait_ge(qbd_zero, 1)
            for g in range(BG):
                for pr in range(4):
                    for hf in range(2):
                        q = slice(64 * hf, 64 * hf + 64)
                        h = 2 * pr + hf
                        nc.gpsimd.tensor_copy(QBD[q, g, pr, :, 4 * h:4 * h + 4],
                                              QB[q, 4 * g + pr, SEQ:T].rearrange("p (b t) -> p b t", t=DS)
                                              ).then_inc(qbd_done, 1)
            for b in range(DB):
                if b >= 2:
                    pool.wait_ge(kts_pe, b - 1)
                pool.dma_start(C1[:, b % 2, :], cache_b1[0, b, :, 0].rearrange("p h d -> p (h d)")).then_inc(ck_in[b % 2], 16)
                pool.dma_start(CA[:, b % 2, :], cache_a[0, b, :, 0].rearrange("p h d -> p (h d)")).then_inc(ck_in[b % 2], 16)
            for b in range(DB):
                if b == 0:
                    pool.wait_ge(rowbias_done, 2)
                    pool.wait_ge(kts_pe, 8)
                for g in (1, 2):
                    if b >= 1:
                        pool.wait_ge(v_used, 2 * b + g - 2)
                    pool.dma_start(VST[:, g - 1], caches[g][0, b].rearrange("(n r) k h d -> n r k (h d)", r=DIL[g])[:, 0:4, 1, :]
                                   ).then_inc(v_in[g - 1], 16)
                if b >= 2:
                    pool.wait_ge(cv_used, b - 1)
                pool.dma_start(C1[:, b % 2, :], cache_b1[0, b, :, 1].rearrange("p h d -> p (h d)")).then_inc(cv_in[b % 2], 16)
                pool.dma_start(CA[:, b % 2, :], cache_a[0, b, :, 1].rearrange("p h d -> p (h d)")).then_inc(cv_in[b % 2], 16)

            def slab_after(ph, n0):
                def body(i):
                    pool.wait_ge(chunk_used, ph.chunk0 + ph.chunks * i + 1)
                    copy_b3(i + n0)
                loop(pool, ph, body)
            slab_after(PH_MERGE, 0)
            slab_after(PH_OUT, 2)
            slab_after(PH_F1[0], 6)
            slab_after(PH_F1[1], 17)
            pool.wait_ge(copy_out, 16 * (2 + 8 + 28))
            pool.wait_ge(kv_out, 16 * 8)
            pool.wait_ge(new_out, 16 * 8)

        @block.scalar
        def _(act):
            def split(ph, i, k):
                c = ph.chunk0 + ph.chunks * i + k + AHEAD
                if isinstance(c, int) and c >= CHUNKS:
                    return
                s = (k + AHEAD) % RING
                act.wait_ge(raw_in[s], 16 * (ph.chunk0 // RING + ph.chunks // RING * i + (k + AHEAD) // RING + 1))
                if not known_below(c, RING):
                    act.wait_ge(chunk_used, c - RING + 1)
                nc.scalar.activation(whi[s][:, :], raw[s][:, :], ACT.Copy).then_inc(hi_done, 1)

            for k in range(KT):
                act.wait_ge(xt_ready, k + 1)
                nc.scalar.activation(XH[:, k, :], bank[4 + k % 4][:, 0:T], ACT.Copy).then_inc(xh_done, 1)
                if k >= KT - 3:
                    c = k - KT + 3
                    act.wait_ge(raw_in[c], 16)
                    nc.scalar.activation(whi[c][:, :], raw[c][:, :], ACT.Copy).then_inc(hi_done, 1)

            def tile(ph, i, m):
                which, value = ph.tile_done(i, 0, m, ph.chunks - 1)
                act.wait_ge((tile_ready, chunk_used)[which], value)
                return bank[m]

            def project(kind, ph, i):
                n0 = ph.tile0 + 4 * i

                def evacuate(m):
                    src = tile(ph, i, m)
                    if not known_below(n0 + m, 4):
                        act.wait_ge(ft_turned, 36 if kind == "qa" else n0 + m - 3)
                        act.wait_ge(ft_copied, {"q": n0 + m - 3, "k": n0 + m - 3, "v": 24, "qa": 4 * i + m + 21}[kind])
                    nc.scalar.activation(FT[:, m, :], src[:, 0:T], ACT.Copy,
                                         scale=SCALE if kind in ("q", "qa") else 1.0)\
                        .then_inc(ft_ready, 1)

                def token_rows(m):
                    act.wait_ge(ft_turned, n0 + m + 1)
                    b = bank[4 + m]
                    if kind in ("k", "v"):
                        dst = (KTOK if kind == "k" else VTOK)[:, :, bass.ds(i, 1), m * P:m * P + P]
                        nc.scalar.activation(dst.rearrange("p n g f -> p (n g) f"),
                                             b[:, 0:256].rearrange("p (n f) -> p n f", n=2), ACT.Copy)
                    nc.scalar.activation(TOKS[:, bass.ds(i, 1), m * P:m * P + P].rearrange("p g f -> p (g f)"),
                                         b[0:NS, 256:384], ACT.Copy).then_inc(tok_ready, 1)

                for k in range(8):
                    split(ph, i, k)
                evacuate(0)
                for m in range(1, 4):
                    evacuate(m)
                    if kind != "qa":
                        token_rows(m - 1)
                if kind != "qa":
                    token_rows(3)

            loop(act, PH_QB, lambda i: project("q", PH_QB, i))
            act.wait_ge(tok_out, 16 * 3)
            loop(act, PH_KB, lambda i: project("k", PH_KB, i))
            act.wait_ge(tok_out, 16 * 6)
            loop(act, PH_VB, lambda i: project("v", PH_VB, i))
            loop(act, PH_QA, lambda i: project("qa", PH_QA, i))
            for k in range(4):
                split(PH_KVA, 0, k)
            tile(PH_KVA, 0, 0)
            nc.scalar.activation(KAF[:, :], bank[0][:, 0:T], ACT.Copy).then_inc(ft_ready, 1)
            tile(PH_KVA, 0, 1)
            act.wait_ge(ft_copied, 29)
            nc.scalar.activation(FT[:, 0, :], bank[1][:, 0:T], ACT.Copy).then_inc(ft_ready, 1)
            for m in range(2):
                act.wait_ge(ft_turned, 36 + m + 1)
                nc.scalar.activation((KAT, VAT)[m][:, :, :], bank[4 + m][:, 0:256].rearrange("p (n f) -> p n f", n=2), ACT.Copy)
                nc.scalar.activation(TOKA[:, m, :], bank[4 + m][0:NS, 256:384], ACT.Copy).then_inc(tok_ready, 1)

            def exponentials(u):
                blocks, s = UNITS[u], u % 2
                act.wait_ge(nm_ready, u + 1)
                for qb in range(2):
                    cols = slice(0, 128) if qb == 0 else slice(128, 384)
                    v = SP_[:, s, 0:len(blocks), cols]
                    ins = nc.scalar.activation(v, v, ACT.Exp, bias=NM[:, s, qb:qb + 1], accum_out=LS[:, s, qb:qb + 1])
                    ins.then_inc(e_ready, 1)
                if len(blocks) == 1:
                    nc.scalar.activation(ES[:, s, :], NM[:, s, :], ACT.Exp, bias=SINKB[:, u:u + 1]).then_inc(e_ready, 1)

            def turned(n):
                act.wait_ge(t_ready, n + 1)
                if n >= 3:
                    act.wait_ge(pt_used, n - 2)
                nc.scalar.activation(PT[:, n % 3, :], bank[3 + n % 2][:, 0:384], ACT.Copy).then_inc(pt_ready, 1)

            exponentials(0)
            for u in range(len(UNITS)):
                if u + 1 < len(UNITS):
                    exponentials(u + 1)
                for n, *_ in UNITS[u]:
                    turned(n)

            for b in range(DB):
                act.wait_ge(kts_pe, b + 1)
                if b >= 1:
                    act.wait_ge(kts_used, b)
                nc.scalar.activation(KTS[:, 0, :], bank[4][:, 0:512], ACT.Copy)
                nc.scalar.activation(KTS[0:64, 1, 0:256], bank[5][0:64, 0:256], ACT.Copy).then_inc(kts_ready, 1)
            for r in range(2):
                act.wait_ge(rows_m, r + 1)
                nc.scalar.activation(SRB[:, r, :], SRB[:, r, :], ACT.Exp, bias=SNM[:, r:r + 1],
                                     accum_out=SLS[:, r:r + 1]).then_inc(rows_e, 1)
            act.wait_ge(rows_m, 6)
            for r in range(2, 6):
                v = SRA[:, (r - 2) // 2, r % 2, :]
                nc.scalar.activation(v, v, ACT.Exp, bias=SNM[:, r:r + 1], accum_out=SLS[:, r:r + 1]).then_inc(rows_e, 1)
                nc.scalar.activation(SES[:, r:r + 1], SNM[:, r:r + 1], ACT.Exp,
                                     bias=SINKR[:, r % 2:r % 2 + 1]).then_inc(rows_e, 1)
            act.wait_ge(rt_pe, 1)
            nc.scalar.activation(PTB[:, :, 0, :], bank[4][:, 0:384].rearrange("p (g r) -> p g r", g=3), ACT.Copy)
            nc.scalar.activation(PTB[:, :, 1, :], bank[5][:, 0:384].rearrange("p (g r) -> p g r", g=3), ACT.Copy)
            nc.scalar.activation(PTN[:, 0, :], bank[4][0:96, 384:512], ACT.Copy)
            nc.scalar.activation(PTN[:, 1, :], bank[5][0:96, 384:512], ACT.Copy)
            act.wait_ge(rt_pe, 2)
            nc.scalar.activation(PTA[:, :, :, :], bank[6][:, :].rearrange("p (b k r) -> p k b r", b=2, k=2), ACT.Copy)
            nc.scalar.activation(PTNA[:, :, :, :], bank[7][0:NS, :].rearrange("p (b k r) -> p k b r", b=2, k=2),
                                 ACT.Copy).then_inc(rt_done, 1)

            def gates(i):
                for k in range(8):
                    split(PH_GATE, i, k)
                for m in range(4):
                    src = tile(PH_GATE, i, m)
                    nc.scalar.activation(GT[:, bass.ds(4 * i + m, 1), :].rearrange("p n t -> p (n t)"), src[:, 0:T],
                                         ACT.Sigmoid).then_inc(tile_free, 1)
            loop(act, PH_GATE, gates)

            for n in range(3):
                act.wait_ge(os_read, 1)
                nc.scalar.activation(OTH[:, 4 * n:4 * n + 4, :], OT[:, 4 * n:4 * n + 4, :], ACT.Copy).then_inc(oth_done, 1)

            def merge(i):
                for k in range(12):
                    split(PH_MERGE, i, k)
                    if k % 6 == 5:
                        s = k // 6
                        for m in range(4):
                            n = 8 * i + 4 * s + m
                            act.wait_ge(mix_done, n + 1)
                            nc.scalar.activation(MH[:, bass.ds(n, 1), :].rearrange("p n t -> p (n t)"), MT[:, 2, :],
                                                 ACT.Copy).then_inc(mh_done, 1)
            loop(act, PH_MERGE, merge)

            def outp(i):
                for k in range(8):
                    split(PH_OUT, i, k)
            loop(act, PH_OUT, outp)

            def norm(which):
                act.wait_ge(sum_pe, 2 * which + 1)
                nc.scalar.activation(MU[:, :], bank[4][:, 0:T], ACT.Copy, scale=1.0 / D).then_inc(mu_done, 1)
                for n in range(4):
                    act.wait_ge(cen_done, 4 * which + n + 1)
                    if n:
                        act.wait_ge(sq_used, 3 * which + n)
                    nc.scalar.activation(SQ[:, :, :], U[:, 4 * n:4 * n + 4, :], ACT.Square).then_inc(sq_done, 1)
                act.wait_ge(sum_pe, 2 * which + 2)
                nc.scalar.activation(MU[:, :], bank[5][:, 0:T], ACT.Sqrt, bias=EPSC[:, 0:1], scale=1.0 / D).then_inc(sd_done, 1)
                for k in range(KT):
                    if k % 4 == 0:
                        act.wait_ge(nrm_done, 4 * which + k // 4 + 1)
                    nc.scalar.activation(U[:, k, :], U[:, k, :], ACT.Identity, scale=LNP[:, 2 * which, k:k + 1],
                                         bias=LNP[:, 2 * which + 1, k:k + 1]).then_inc(y_done, 1)
                    if which == 0:
                        act.wait_ge(y_done, k + 1)
                        nc.scalar.activation(X1H[:, k, :], U[:, k, :], ACT.Copy).then_inc(x1h_done, 1)

            norm(0)
            for half in range(2):
                def ffn_in(i, half=half):
                    ph = PH_F1[half]
                    for k in range(8):
                        split(ph, i, k)
                    n = 22 * half + 2 * i
                    for j in range(2):
                        which, value = ph.tile_done(i, 0, j, 6)
                        act.wait_ge((tile_ready, chunk_used)[which], value)
                        src = bank[j]
                        nc.scalar.activation(SG[:, j, :], src[:, 0:T], ACT.Sigmoid).then_inc(sg_done, 1)
                    for j in range(2):
                        act.wait_ge(tile_free, ph.tile0 - FREE0 + 4 * i + 2 + j + 1)
                        nc.scalar.activation(HH[:, bass.ds(2 * i + j, 1), :].rearrange("p n t -> p (n t)"), HF[:, j, :],
                                             ACT.Copy).then_inc(hh_done, 1)
                loop(act, PH_F1[half], ffn_in)
                for k in range(44):
                    split(PH_F2[half], 0, k)
            norm(1)
            for k in range(KT):
                act.wait_ge(yt_pe, k + 1)
                b = bank[6 + k % 2]
                nc.scalar.activation(YT[:, :, k * P:k * P + P], b[:, 0:256].rearrange("p (n f) -> p n f", n=2), ACT.Copy)
                nc.scalar.activation(YTS[:, k * P:k * P + P], b[0:NS, 256:384], ACT.Copy).then_inc(yt_done, 1)

        @block.vector
        def _(dve):
            count = [0]

            def link(ins):
                count[0] += 1
                ins.then_inc(chain, 1)
                dve.wait_ge(chain, count[0])

            def split(ph, i, k):
                c = ph.chunk0 + ph.chunks * i + k + AHEAD
                if isinstance(c, int) and c >= CHUNKS:
                    return
                s = (k + AHEAD) % RING
                dve.wait_ge(hi_done, c + 1)
                nc.vector.tensor_tensor(wlo[s][:, :], raw[s][:, :], whi[s][:, :].bitcast(F32), ALU.subtract).then_inc(lo_done, 1)

            link(nc.vector.memset(ones[:, :], 1.0))
            link(nc.vector.memset(EPSC[:, :], EPS))
            for k in range(KT):
                dve.wait_ge(xh_done, k + 1)
                nc.vector.tensor_tensor(XL[:, k, :], bank[4 + k % 4][:, 0:T], XH[:, k, :].bitcast(F32),
                                        ALU.subtract).then_inc(xl_done, 1)
                if k >= KT - 3:
                    c = k - KT + 3
                    dve.wait_ge(hi_done, c + 1)
                    nc.vector.tensor_tensor(wlo[c][:, :], raw[c][:, :], whi[c][:, :].bitcast(F32), ALU.subtract).then_inc(lo_done, 1)
            dve.wait_ge(setup_pe, 1)
            dve.wait_ge(const_in, 16 * 10)
            nc.vector.tensor_tensor(TZ[:, :], bank[3][0:NH, 0:384], TZ[:, :], ALU.add).then_inc(setup_dve, 1)
            link(nc.vector.tensor_copy(SINKR[:, :], bank[3][:, 400:402]))

            def unit(b, j):
                n = 4 * b + j
                g, t0 = 1 + j // 2, 2 * (j % 2)
                dve.wait_ge(unit_in[j % 2], 64 * b + 32 * (j // 2) + 32)
                if not known_below(n, 1):
                    dve.wait_ge(unit_done, n)
                nc.vector.tensor_tensor(PROD[:, :], KST[:, j % 2].rearrange("p t f -> p (t f)"),
                                        QST[:, j % 2].rearrange("p t f -> p (t f)"), ALU.mult).then_inc(prod_done, 1)
                dve.wait_ge(prod_done, n + 1)
                dst = ST[:, g - 1, bass.ds(32 * b, 32)].rearrange("p (h t) -> p t h", t=DS)[:, t0:t0 + 2, :]
                nc.vector.tensor_reduce(dst, PROD[:, :].rearrange("p (t h d) -> p t h d", t=2, h=BH),
                                        AX, ALU.add).then_inc(unit_done, 1)

            def project(kind, ph, i):
                n0 = ph.tile0 + 4 * i
                b = None if kind == "q" else i + {"k": 0, "v": 3, "qa": 6}[kind]
                for k in range(8):
                    split(ph, i, k)
                    if b is not None and k % 2 == 1:
                        unit(b, k // 2)
                if kind != "v":
                    dst = {"q": QB, "k": KB, "qa": QA}[kind]
                    for m in range(4):
                        dve.wait_ge(ft_ready, n0 + m + 1)
                        d = dst[:, bass.ds(4 * i + m, 1), :].rearrange("p n t -> p (n t)")
                        if kind == "k":
                            nc.vector.tensor_copy(d, FT[:, m, :]).then_inc(ft_copied, 1)
                        else:
                            nc.vector.tensor_copy(d[:, 0:SEQ].rearrange("p (n c) -> p n c", n=2),
                                                  FT[:, m, 0:SEQ].rearrange("p (n c) -> p n c", n=2)[:, :, ::-1])
                            nc.vector.tensor_copy(d[:, SEQ:T], FT[:, m, SEQ:T]).then_inc(ft_copied, 1)

            loop(dve, PH_QB, lambda i: project("q", PH_QB, i))
            loop(dve, PH_KB, lambda i: project("k", PH_KB, i))
            loop(dve, PH_VB, lambda i: project("v", PH_VB, i))
            loop(dve, PH_QA, lambda i: project("qa", PH_QA, i))
            dve.wait_ge(ft_copied, 32)
            for par in range(2):
                if par:
                    dve.wait_ge(qas_in, 16)
                src = QLO[:, :, :] if par else QA[0:64, :, SEQ:T]
                for kv in range(2):
                    nc.vector.tensor_copy(QAS[:, kv, :, par:8:2, :].rearrange("p b g t -> p g b t"),
                                          src[:, 4 * kv:4 * kv + 4, :].rearrange("p g (b t) -> p g b t", t=DS)).then_inc(qas_own, 1)
            for k in range(4):
                split(PH_KVA, 0, k)

            def logits(u):
                blocks, s = UNITS[u], u % 2
                if u >= 2:
                    dve.wait_ge(t_ready, UNITS[u - 2][-1][0] + 1)
                if u == 0:
                    dve.wait_ge(kv_out, 16 * 8)
                for j, (n, *_) in enumerate(blocks):
                    dve.wait_ge(s_ready, n + 1)
                    dve.wait_ge(bias_in[n % 4], 16 * (n // 4 + 1))
                    b = bank[n % 3]
                    nc.vector.tensor_tensor_reduce(SP_[:, s, j, 0:128], b[:, 0:128], BIAS[:, n % 4, 128:256], 1.0, LOW,
                                                   ALU.add, ALU.max, MX[:, s, 0, j:j + 1]).then_inc(m_ready, 1)
                    nc.vector.tensor_tensor_reduce(SP_[:, s, j, 128:384], b[:, 128:384], BIAS[:, n % 4, :], 1.0, LOW,
                                                   ALU.add, ALU.max, MX[:, s, 1, j:j + 1]).then_inc(s_read, 1)
                dve.wait_ge(m_ready, blocks[-1][0] + 1)
                dve.wait_ge(s_read, blocks[-1][0] + 1)
                if len(blocks) == 1:
                    nc.vector.tensor_scalar(NM[:, s, :], MX[:, s, :, 0], SINKB[:, u:u + 1], -1.0, ALU.max, ALU.mult)\
                        .then_inc(nm_ready, 1)
                else:
                    nc.vector.tensor_reduce(NM[:, s, :], MX[:, s, :, :], AX, ALU.max, negate=True).then_inc(nm_ready, 1)

            def normalise(u):
                blocks, s = UNITS[u], u % 2
                dve.wait_ge(e_ready, 3 * (u + 1) if u < QH else 3 * QH + 2 * (u - QH + 1))
                if len(blocks) == 1:
                    link(nc.vector.tensor_tensor(LS[:, s, :], LS[:, s, :], ES[:, s, :], ALU.add))
                link(nc.vector.reciprocal(RL[:, s, :], LS[:, s, :]))
                for qb in range(2):
                    cols = slice(0, 128) if qb == 0 else slice(128, 384)
                    v = SP_[:, s, 0:len(blocks), cols]
                    ins = nc.vector.tensor_scalar(v, v, RL[:, s, qb:qb + 1], None, ALU.mult)
                    ins.then_inc(p_ready, 1)

            def output(pair):
                dve.wait_ge(pt_used, UNITS[2 * pair + 1][-1][0] + 1)
                nc.vector.tensor_copy(OT[:, pair, 0:SEQ].rearrange("p (n c) -> p n c", n=2),
                                      bank[5 + pair % 2][:, 0:SEQ].rearrange("p (n c) -> p n c", n=2)[:, :, ::-1])\
                    .then_inc(o_read, 1)

            dve.wait_ge(const_in, 16 * 10)
            logits(0)
            for u in range(len(UNITS)):
                if u + 1 < len(UNITS):
                    logits(u + 1)
                normalise(u)
                if u % 2 == 0 and u:
                    if u == 2:
                        dve.wait_ge(toka_out, 32)
                        dve.wait_ge(tok_out, 16 * 9)
                        dve.wait_ge(kd_in, 64)
                    output(u // 2 - 1)
            output(len(UNITS) // 2 - 1)

            dve.wait_ge(samp_in, 64)
            dve.wait_ge(rowbias_pe, 1)
            for bb in range(2):
                ins = nc.vector.tensor_tensor(BIB[:, bb, :], bank[6][:, 0:NKEY_B], BIB[:, bb, :], ALU.add)
                if bb == 1:
                    ins.then_inc(rowbias_done, 1)
            for bb in range(2):
                ins = nc.vector.tensor_tensor(BIA[:, bb, :, :], bank[7][:, 0:2 * NKEY_A].rearrange("p (k n) -> p k n", k=2),
                                              BIA[:, bb, :, :], ALU.add)
                if bb == 1:
                    ins.then_inc(rowbias_done, 1)
            dve.wait_ge(rowbias_done, 2)
            for bb in range(2):
                dve.wait_ge(rows_ready, 1)
                link(nc.vector.tensor_tensor_reduce(SRB[:, bb, :], bank[bb][:, 0:NKEY_B], BIB[:, bb, :], 1.0, LOW,
                                                    ALU.add, ALU.max, SMX[:, bb:bb + 1]))
                nc.vector.tensor_scalar(SNM[:, bb:bb + 1], SMX[:, bb:bb + 1], -1.0, None, ALU.mult).then_inc(rows_m, 1)
            for r in range(2, 6):
                bb, kv = (r - 2) // 2, r % 2
                link(nc.vector.tensor_tensor_reduce(SRA[:, bb, kv, :], bank[2 + bb][:, kv * NKEY_A:kv * NKEY_A + NKEY_A],
                                                    BIA[:, bb, kv, :], 1.0, LOW, ALU.add, ALU.max, SMX[:, r:r + 1]))
                nc.vector.tensor_scalar(SNM[:, r:r + 1], SMX[:, r:r + 1], SINKR[:, kv:kv + 1], -1.0, ALU.max, ALU.mult)\
                    .then_inc(rows_m, 1)
            dve.wait_ge(rows_e, 10)
            link(nc.vector.tensor_tensor(SLS[:, 2:6], SLS[:, 2:6], SES[:, 2:6], ALU.add))
            link(nc.vector.reciprocal(SRL[:, :], SLS[:, :]))
            for r in range(6):
                v = SRB[:, r, :] if r < 2 else SRA[:, (r - 2) // 2, r % 2, :]
                nc.vector.tensor_scalar(v, v, SRL[:, r:r + 1], None, ALU.mult).then_inc(rows_p, 1)

            def gates(i):
                for k in range(8):
                    split(PH_GATE, i, k)
            loop(dve, PH_GATE, gates)
            dve.wait_ge(v_used, 16)
            for hf in range(2):
                q = slice(64 * hf, 64 * hf + 64)
                nc.vector.tensor_copy(OT[q, 8:12, SEQ:T], bank[4][q, 0:256].rearrange("p (r h n) -> p r h n", r=4, h=2)[:, :, hf, :])
                ins = nc.vector.tensor_copy(OT[q, 0:8, SEQ:T], bank[5][q, 0:256].rearrange("p (r n) -> p r n", r=8))
            ins.then_inc(os_read, 1)
            for n in range(3):
                dve.wait_ge(oth_done, n + 1)
                nc.vector.tensor_tensor(OTL[:, 4 * n:4 * n + 4, :], OT[:, 4 * n:4 * n + 4, :],
                                        OTH[:, 4 * n:4 * n + 4, :].bitcast(F32), ALU.subtract).then_inc(otl_done, 1)

            def one(buf, n):
                return buf[:, bass.ds(n, 1), :].rearrange("p n t -> p (n t)")

            def merge(i):
                for k in range(12):
                    split(PH_MERGE, i, k)
                    if k % 6 == 5:
                        s = k // 6
                        for m in range(4):
                            n = 8 * i + 4 * s + m
                            which, value = PH_MERGE.tile_done(i, s, m, 6 * s + 3)
                            dve.wait_ge((tile_ready, chunk_used)[which], value)
                            nc.vector.tensor_tensor(MT[:, 0, :], bank[m][:, 0:T], one(GT, n), ALU.mult).then_inc(tile_free, 1)
                            if m < 3:
                                dve.wait_ge(pb_ready, 6 * i + 3 * s + m + 1)
                            else:
                                dve.wait_ge(chunk_used, PH_MERGE.chunk0 + 12 * i + 6 * s + 6)
                            nc.vector.tensor_tensor(MT[:, 1, :], bank[4 + m][:, 0:T], one(GT, n + 16), ALU.mult).then_inc(pb_free, 1)
                            dve.wait_ge(pb_free, n + 1)
                            nc.vector.tensor_tensor(MT[:, 2, :], MT[:, 0, :], MT[:, 1, :], ALU.add).then_inc(mix_done, 1)
                            dve.wait_ge(mh_done, n + 1)
                            nc.vector.tensor_tensor(one(ML, n), MT[:, 2, :], one(MH, n).bitcast(F32), ALU.subtract).then_inc(ml_done, 1)
            loop(dve, PH_MERGE, merge)

            nc.vector.memset(SUM[:, :], 0.0).then_inc(sum_done, 1)

            def outp(i):
                for k in range(8):
                    split(PH_OUT, i, k)
                for m in range(4):
                    n = 4 * i + m
                    which, value = PH_OUT.tile_done(i, 0, m, 7)
                    dve.wait_ge((tile_ready, chunk_used)[which], value)
                    nc.vector.scalar_tensor_tensor(out=one(U, n), in0=one(XH, n).bitcast(F32), scalar=ALPHA,
                                                   in1=bank[m][:, 0:T], op0=ALU.mult, op1=ALU.add).then_inc(tile_free, 1)
                    dve.wait_ge(tile_free, PH_OUT.tile0 - FREE0 + n + 1)
                    nc.vector.scalar_tensor_tensor(out=one(U, n), in0=one(XL, n).bitcast(F32), scalar=ALPHA,
                                                   in1=one(U, n), op0=ALU.mult, op1=ALU.add).then_inc(sum_done, 1)
                    dve.wait_ge(sum_done, 2 * n + 2)
                    nc.vector.tensor_tensor(SUM[:, :], SUM[:, :], one(U, n), ALU.add).then_inc(sum_done, 1)
            loop(dve, PH_OUT, outp)

            def norm(which):
                dve.wait_ge(mu_done, which + 1)
                for n in range(4):
                    v = U[:, 4 * n:4 * n + 4, :]
                    nc.vector.tensor_tensor(v, v, MU[:, :].unsqueeze(1).broadcast_to([P, 4, T]), ALU.subtract).then_inc(cen_done, 1)
                dve.wait_ge(sd_done, which + 1)
                nc.vector.reciprocal(RS[:, :], MU[:, :]).then_inc(rs_done, 1)
                dve.wait_ge(rs_done, which + 1)
                for n in range(4):
                    v = U[:, 4 * n:4 * n + 4, :]
                    nc.vector.tensor_tensor(v, v, RS[:, :].unsqueeze(1).broadcast_to([P, 4, T]), ALU.mult).then_inc(nrm_done, 1)
                if which == 0:
                    for k in range(KT):
                        dve.wait_ge(x1h_done, k + 1)
                        nc.vector.tensor_tensor(X1L[:, k, :], U[:, k, :], X1H[:, k, :].bitcast(F32), ALU.subtract).then_inc(x1l_done, 1)

            dve.wait_ge(setup_pe, 2)
            link(nc.vector.tensor_copy(LNP[:, :, :], bank[7][:, 0:64].rearrange("p (a k) -> p a k", a=4)))
            norm(0)
            for half in range(2):
                def ffn_in(i, half=half):
                    ph = PH_F1[half]
                    for k in range(8):
                        split(ph, i, k)
                    n = 22 * half + 2 * i
                    t0 = ph.tile0 + 4 * i
                    for j in range(2):
                        dve.wait_ge(sg_done, n + j + 1)
                        nc.vector.tensor_tensor(HT[:, j, :], bank[j][:, 0:T], SG[:, j, :], ALU.mult).then_inc(tile_free, 1)
                    for j in range(2):
                        dve.wait_ge(tile_free, t0 - FREE0 + j + 1)
                        which, value = ph.tile_done(i, 1, j, 7)
                        dve.wait_ge((tile_ready, chunk_used)[which], value)
                        nc.vector.tensor_tensor(HF[:, j, :], bank[2 + j][:, 0:T], HT[:, j, :], ALU.mult).then_inc(tile_free, 1)
                    for j in range(2):
                        dve.wait_ge(hh_done, n + j + 1)
                        nc.vector.tensor_tensor(one(HL, 2 * i + j), HF[:, j, :], one(HH, 2 * i + j).bitcast(F32),
                                                ALU.subtract).then_inc(hl_done, 1)
                loop(dve, PH_F1[half], ffn_in)
                for k in range(44):
                    split(PH_F2[half], 0, k)
                    if k % 11 == 10:
                        j = k // 11
                        for m in range(4):
                            n = 4 * j + m
                            which, value = PH_F2[half].tile_done(0, j, m, k)
                            dve.wait_ge((tile_ready, chunk_used)[which], value)
                            nc.vector.scalar_tensor_tensor(out=U[:, n, :], in0=U[:, n, :], scalar=ALPHA if half == 0 else 1.0,
                                                           in1=bank[m][:, 0:T], op0=ALU.mult, op1=ALU.add).then_inc(tile_free, 1)
                            if half == 1:
                                dve.wait_ge(tile_free, PH_F2[half].tile0 - FREE0 + n + 1)
                                if n == 0:
                                    link(nc.vector.tensor_copy(SUM[:, :], U[:, 0, :]))
                                elif n < KT - 1:
                                    link(nc.vector.tensor_tensor(SUM[:, :], SUM[:, :], U[:, n, :], ALU.add))
                                else:
                                    nc.vector.tensor_tensor(SUM[:, :], SUM[:, :], U[:, n, :], ALU.add).then_inc(sum_done, 1)
            norm(1)

        @block.tensor
        def _(pe):
            def mm(out, lhsT, rhs, start, stop, **kw):
                return nc.tensor.matmul(out, lhsT, rhs, start=start, stop=stop, **kw)

            def turn(out, in_, n=P):
                return nc.tensor.transpose(out, in_, ident[0:n, 0:n])

            def chunk_products(ph, i, k, k0, hi, lo, banks, first, last, free_wait=None, after=None, kk=2, m_n=4, ready=None):
                c = ph.chunk0 + ph.chunks * i + k
                s = k % RING
                pe.wait_ge(lo_done, c + 1)
                w = CK // kk
                for m in range(m_n):
                    if first and free_wait:
                        free_wait(m)
                    for q in range(kk):
                        a = whi[s][:, q * w + m * P:q * w + m * P + P]
                        b = wlo[s][:, q * w + m * P:q * w + m * P + P]
                        out = bank[banks + m][:, 0:T]
                        st, sp_ = first and q == 0, last and q == kk - 1
                        mm(out, a, hi[:, k0 + q, :], st, False)
                        mm(out, a, lo[:, k0 + q, :], False, False)
                        ins = mm(out, b, hi[:, k0 + q, :], False, sp_)
                    if last and m < m_n - 1:
                        ins.then_inc(ready or tile_ready, 1)
                    if last and after and m:
                        after(m - 1)
                ins.then_inc(chunk_used, 1)
                if last and after:
                    after(m_n - 1)

            pe.wait_ge(x_in, 48)
            for k in range(KT):
                if k >= 4:
                    pe.wait_ge(xl_done, k - 3)
                b = bank[4 + k % 4]
                turn(b[:, 0:P], xs_p[:, 0, k * P:k * P + P])
                turn(b[:, P:2 * P], xs_p[:, 1, k * P:k * P + P])
                turn(b[:, 2 * P:T], xs_s[:, k * P:k * P + P], NS).then_inc(xt_ready, 1)
            pe.wait_ge(const_in, 16 * 10)
            mm(bank[3][:, 400:402], ROWSEL[:, :], SINK2[:, :], True, True)
            mm(bank[3][0:NH, 0:384], REL4[0:32, :], OHP[:, :], True, True).then_inc(setup_pe, 1)
            pe.wait_ge(chain, 3)
            pe.wait_ge(xl_done, KT)

            def free_wait(ph, i, s=0):
                def wait(m):
                    n = ph.tile0 + ph.tiles * (ph.sets * i + s) + m
                    if ph.chunk0 < PH_GATE.chunk0:
                        if not known_below(n, 4):
                            pe.wait_ge(ft_ready, n - 3)
                    elif not known_below(n, FREE0 + 4):
                        pe.wait_ge(tile_free, n - FREE0 - 3)
                return wait

            def project(kind, ph, i):
                n0 = ph.tile0 + 4 * i

                def rows(m):
                    pe.wait_ge(ft_ready, n0 + m + 1)
                    if not known_below(n0, 4):
                        pe.wait_ge(tok_ready, n0 + m - 3)
                    b = bank[4 + m]
                    if kind in ("k", "v"):
                        turn(b[:, 0:P], FT[:, m, 0:P])
                        turn(b[:, P:2 * P], FT[:, m, P:2 * P])
                    turn(b[0:NS, 256:384], FT[:, m, SEQ:T]).then_inc(ft_turned, 1)

                for k in range(8):
                    chunk_products(ph, i, k, 2 * k, XH, XL, 0, k == 0, k == 7, free_wait(ph, i),
                                   rows if kind != "qa" else None)

            loop(pe, PH_QB, lambda i: project("q", PH_QB, i))
            loop(pe, PH_KB, lambda i: project("k", PH_KB, i))
            loop(pe, PH_VB, lambda i: project("v", PH_VB, i))
            loop(pe, PH_QA, lambda i: project("qa", PH_QA, i))
            for k in range(4):
                chunk_products(PH_KVA, 0, k, 4 * k, XH, XL, 0, k == 0, k == 3, free_wait(PH_KVA, 0), None, 4, 2)
            for m in range(2):
                pe.wait_ge(ft_ready, 44 + m + 1)
                if m == 0:
                    pe.wait_ge(tok_ready, 36)
                b = bank[4 + m]
                f = KAF[:, :] if m == 0 else FT[:, 0, :]
                turn(b[:, 0:P], f[:, 0:P])
                turn(b[:, P:2 * P], f[:, P:2 * P])
                turn(b[0:NS, 256:384], f[:, SEQ:T]).then_inc(ft_turned, 1)

            def scores(u):
                for n, kind, h, g in UNITS[u]:
                    if n >= 3:
                        pe.wait_ge(s_read, n - 2)
                    q = slice(64 * (h % 2), 64 * (h % 2) + 64)
                    if kind == "a":
                        qt, kt = QA[q, h // 2, :], KD[q, h // 8, :]
                    else:
                        qt, kt = QB[q, 4 * g + h // 2, :], KB[q, 4 * g + h // 2, :]
                    b = bank[n % 3]
                    mm(b[:, 0:128], qt[:, 0:128], kt[:, 0:128], True, True)
                    mm(b[:, 128:384], qt[:, 128:256], kt[:, 0:256], True, True).then_inc(s_ready, 1)

            def turns(u, n, j):
                pe.wait_ge(p_ready, 2 * u + 2)
                if n >= 2:
                    pe.wait_ge(pt_ready, n - 1)
                b, s = bank[3 + n % 2], SP_[:, u % 2, j, :]
                turn(b[:, 0:128], s[:, 0:128])
                turn(b[:, 128:256], s[:, 128:256])
                turn(b[:, 256:384], s[:, 256:384]).then_inc(t_ready, 1)

            def values(u, n, kind, h, g, first, last):
                pe.wait_ge(pt_ready, n + 1)
                pair = u // 2
                if first and u % 2 == 0 and pair >= 2:
                    pe.wait_ge(o_read, pair - 1)
                q = slice(64 * (h % 2), 64 * (h % 2) + 64)
                o = bank[5 + pair % 2]
                if kind == "a":
                    v = [VAT[:, blk, 64 * (h // 8):64 * (h // 8) + 64] for blk in range(2)]
                else:
                    v = [VTOK[:, blk, g, 64 * h:64 * h + 64] for blk in range(2)]
                mm(o[q, 0:256], v[0], PT[:, n % 3, 0:256], first, False, skip_group_check=True)
                ins = mm(o[q, 128:256], v[1], PT[:, n % 3, 256:384], False, last, skip_group_check=True)
                ins.then_inc(pt_used, 1)
                return ins

            pe.wait_ge(kd_in, 64)
            pe.wait_ge(tok_ready, 38)
            pe.wait_ge(ft_copied, 32)
            scores(0)
            todo = None
            for u in range(len(UNITS)):
                if u + 1 < len(UNITS):
                    scores(u + 1)
                for j, (n, kind, h, g) in enumerate(UNITS[u]):
                    turns(u, n, j)
                    if todo:
                        values(*todo)
                    todo = (u, n, kind, h, g, j == 0, j == len(UNITS[u]) - 1)
            values(*todo)

            pe.wait_ge(samp_in, 64)
            pe.wait_ge(relt_done, 20)
            pe.wait_ge(o_read, 12)
            for g in range(BG):
                mm(bank[6][:, g * P:g * P + P], RELT[:, g, :], OHB[:, g * P:g * P + P], True, True)
                mm(bank[6][:, 3 * P + NS * g:3 * P + NS * g + NS], RELT[:, g, :],
                   OHB[:, 3 * P + NS * g:3 * P + NS * g + NS], True, True)
            for kv in range(2):
                ins = mm(bank[7][:, kv * NKEY_A:kv * NKEY_A + NKEY_A], RELT[:, 3 + kv, :], OHA[:, :], True, True)
            ins.then_inc(rowbias_pe, 1)
            pe.wait_ge(qbd_done, 24)
            pe.wait_ge(qas_own, 4)
            pe.wait_ge(pt_ready, 40)
            for b in range(DB):
                pe.wait_ge(ck_in[b % 2], 32 * (b // 2 + 1))
                if b >= 1:
                    pe.wait_ge(kts_ready, b)
                for pr in range(4):
                    turn(bank[4][:, pr * P:pr * P + P], C1[:, b % 2, pr * P:pr * P + P])
                for kv in range(2):
                    ins = turn(bank[5][0:64, kv * P:kv * P + P], CA[:, b % 2, 64 * kv:64 * kv + 64])
                ins.then_inc(kts_pe, 1)
                pe.wait_ge(kts_ready, b + 1)
                r, bb = slice(32 * (b % 4), 32 * (b % 4) + 32), b // 4
                for pr in range(4):
                    mm(bank[bb][r, 0:P], QBD[:, 0, pr, b, :], KTS[:, 0, pr * P:pr * P + P], pr == 0, pr == 3)
                for kv in range(2):
                    qs = QAS[:, kv, b].rearrange("p g t -> p (g t)")
                    ins = mm(bank[2 + bb][r, kv * NKEY_A:kv * NKEY_A + P], qs, KTS[0:64, 1, kv * P:kv * P + P], True, True)
                ins.then_inc(kts_used, 1)
            pe.wait_ge(unit_done, 32)
            for bb in range(2):
                for g in (1, 2):
                    turn(bank[bb][:, g * P:g * P + P], ST[:, g - 1, P * bb:P * bb + P])
                for g in range(BG):
                    for pr in range(4):
                        mm(bank[bb][:, 3 * P + NS * g:3 * P + NS * g + NS],
                           QBD[:, g, pr, 4 * bb:4 * bb + 4, :].rearrange("p b r -> p (b r)"),
                           KB[:, 4 * g + pr, SEQ:T], pr == 0, pr == 3)
                for kv in range(2):
                    qs = QAS[:, kv, 4 * bb:4 * bb + 4].rearrange("p b g t -> p (b g t)")
                    ins = mm(bank[2 + bb][:, kv * NKEY_A + P:(kv + 1) * NKEY_A], qs, KD[0:64, kv, SEQ:T], True, True)
            ins.then_inc(rows_ready, 1)
            pe.wait_ge(rows_p, 6)
            for bb in range(2):
                for g in range(BG):
                    turn(bank[4 + bb][:, g * P:g * P + P], SRB[:, bb, g * P:g * P + P])
                ins = turn(bank[4 + bb][0:96, 384:512], SRB[:, bb, 384:480])
            ins.then_inc(rt_pe, 1)
            for bb in range(2):
                for kv in range(2):
                    n = 2 * bb + kv
                    turn(bank[6][:, n * P:n * P + P], SRA[:, bb, kv, 0:P])
                    ins = turn(bank[7][0:NS, n * P:n * P + P], SRA[:, bb, kv, P:NKEY_A])
            ins.then_inc(rt_pe, 1)
            pe.wait_ge(rt_done, 1)
            pe.wait_ge(vn_in, 32)
            for pr in range(4):
                mm(bank[4][:, 64 * pr:64 * pr + 64].rearrange("p (h b t) -> p h b t", h=2, t=DS),
                   VN[:, P * pr:P * pr + P],
                   PTN[:, :, :].rearrange("p c (b h t) -> p h (c b) t", b=4, t=DS)[:, 2 * pr:2 * pr + 2],
                   pr == 0, False, skip_group_check=True)
            for par in range(2):
                for kv in range(2):
                    mm(bank[5][64 * par:64 * par + 64, 128 * kv:128 * kv + 128]
                       .rearrange("p (g b t) -> p g b t", g=4, t=DS),
                       VNA[:, 64 * kv:64 * kv + 64],
                       PTNA[:, kv].rearrange("p c (b g t) -> p g (c b) t", b=4, t=DS)[:, par:8:2],
                       kv == 0, False, skip_group_check=True)

            def cached_values(b):
                c, bb, b4 = slice(4 * b, 4 * b + 4), b // 4, b % 4
                pe.wait_ge(cv_in[b % 2], 32 * (b // 2 + 1))
                for pr in range(4):
                    mm(bank[4][:, 64 * pr:64 * pr + 64].rearrange("p (h n) -> p h n", h=2)[:, :, c],
                       C1[:, b % 2, P * pr:P * pr + P],
                       PTB[:, 0, bb, 32 * b4 + 8 * pr:32 * b4 + 8 * pr + 8].rearrange("p (h t) -> p h t", t=DS),
                       False, False, skip_group_check=True)
                for par in range(2):
                    for kv in range(2):
                        ins = mm(bank[5][64 * par:64 * par + 64, 128 * kv:128 * kv + 128].rearrange("p (g n) -> p g n", g=4)[:, :, c],
                                 CA[:, b % 2, 64 * kv:64 * kv + 64],
                                 PTA[:, kv, bb, 32 * b4:32 * b4 + 32].rearrange("p (g t) -> p g t", t=DS)[:, par:8:2],
                                 False, b == DB - 1, skip_group_check=True)
                ins.then_inc(cv_used, 1)
                for g in (1, 2):
                    pe.wait_ge(v_in[g - 1], 16 * (b + 1))
                    for t in range(DS):
                        for pr in range(4):
                            ins = mm(bank[4][:, 64 * pr:64 * pr + 64].rearrange("p (h n) -> p h n", h=2)[:, :, 4 * b + t],
                                     VST[:, g - 1, t, P * pr:P * pr + P],
                                     PTB[:, g, bb, 32 * b4 + 8 * pr:32 * b4 + 8 * pr + 8].rearrange("p (h t) -> p h t", t=DS)[:, :, t],
                                     False, b == DB - 1 and g == 2, skip_group_check=True)
                    ins.then_inc(v_used, 1)

            for i in range(8):
                for k in range(8):
                    chunk_products(PH_GATE, i, k, 2 * k, XH, XL, 0, k == 0, k == 7, free_wait(PH_GATE, i))
                cached_values(i)

            pe.wait_ge(otl_done, 3)

            def merge(i):
                for s in range(2):
                    n0 = 8 * i + 4 * s

                    def pb_wait(m):
                        if not known_below(n0 + m, 4):
                            pe.wait_ge(pb_free, n0 + m - 3)

                    for k in range(4):
                        chunk_products(PH_MERGE, i, 6 * s + k, 2 * k, OTH, OTL, 0, k == 0, k == 3, free_wait(PH_MERGE, i, s))
                    for k in range(2):
                        chunk_products(PH_MERGE, i, 6 * s + 4 + k, 8 + 2 * k, OTH, OTL, 4, k == 0, k == 1, pb_wait,
                                       ready=pb_ready)
            for i in range(2):
                merge(i)

            pe.wait_ge(ml_done, KT)

            def outp(i):
                for k in range(8):
                    chunk_products(PH_OUT, i, k, 2 * k, MH, ML, 0, k == 0, k == 7, free_wait(PH_OUT, i))
            loop(pe, PH_OUT, outp)

            def norm(which):
                pe.wait_ge(sum_done, 33 if which == 0 else 34)
                mm(bank[4][:, 0:T], ones[:, :], SUM[:, :], True, True).then_inc(sum_pe, 1)
                for n in range(4):
                    pe.wait_ge(sq_done, 4 * which + n + 1)
                    for k in range(4):
                        ins = mm(bank[5][:, 0:T], ones[:, :], SQ[:, k, :], n == 0 and k == 0, n == 3 and k == 3)
                    ins.then_inc(sum_pe if n == 3 else sq_used, 1)

            pe.wait_ge(ln_in, 64)
            turn(bank[7][:, 0:64], lnrow[:, :], 64).then_inc(setup_pe, 1)
            norm(0)
            for half in range(2):
                def ffn_in(i, half=half):
                    for k in range(8):
                        pe.wait_ge(x1l_done, 4 * (k // 2) + 4)
                        chunk_products(PH_F1[half], i, k, 4 * (k // 2), X1H, X1L, 2 * (k % 2), k < 2, k >= 6,
                                       free_wait(PH_F1[half], i, k % 2), None, 4, 2)
                loop(pe, PH_F1[half], ffn_in)
                pe.wait_ge(hl_done, 22 * half + 22)
                for j in range(4):
                    for k in range(11):
                        chunk_products(PH_F2[half], 0, 11 * j + k, 2 * k, HH, HL, 0, k == 0, k == 10, free_wait(PH_F2[half], 0, j))
            norm(1)
            for k in range(KT):
                pe.wait_ge(y_done, KT + k + 1)
                if k >= 2:
                    pe.wait_ge(yt_done, k - 1)
                b = bank[6 + k % 2]
                turn(b[:, 0:P], U[:, k, 0:P])
                turn(b[:, P:2 * P], U[:, k, P:2 * P])
                turn(b[0:NS, 256:384], U[:, k, SEQ:T]).then_inc(yt_pe, 1)


_INS = ["x_prompt", "x_sample", "cache_a", "cache_b1", "cache_b2", "cache_b3", "rel_bias", "w_in", "a_sink",
        "w_oa", "w_ob", "w_out", "ln1_g", "ln1_b", "w_ffn_in", "w_ffn_out", "ln2_g", "ln2_b"]
_CONSTS = ["ohp", "maskp", "ohb", "oha", "maskb", "maska", "ident", "rowsel"]
_OUTS = [(1, 256, 2048), (8, 4, 2048), (1, 1, 128, 2, 2, 64), (1, 1, 128, 2, 8, 64), (1, 1, 256, 2, 8, 64),
         (1, 1, 256, 2, 8, 64), (1, 8, 128, 2, 2, 64), (1, 8, 128, 2, 8, 64), (1, 8, 512, 2, 8, 64),
         (1, 8, 2048, 2, 8, 64)]


def kernel(**inputs):
    import numpy as _np
    import concourse.bacc as _bacc
    from concourse import mybir as _mybir
    from concourse.bass_utils import run_bass_kernel_spmd as _run

    nc = _bacc.Bacc("TRN2", target_bir_lowering=False, num_devices=1)
    arrays, args = {}, []
    consts = constants()
    for name in _INS + _CONSTS:
        a = _np.ascontiguousarray(consts[name] if name in consts else inputs[name])
        arrays[f"in_{name}_dram"] = a
        args.append(nc.dram_tensor(f"in_{name}_dram", a.shape, _mybir.dt.from_np(a.dtype), kind="ExternalInput").ap())
    for i, shape in enumerate(_OUTS):
        args.append(nc.dram_tensor(f"out_{i}_dram", shape, _mybir.dt.float32, kind="ExternalOutput").ap())
    build(nc, *args)
    r = _run(nc, [arrays], core_ids=[0])
    return tuple(r.results[0][f"out_{i}_dram"] for i in range(len(_OUTS)))
```

```python
import math
from contextlib import ExitStack

import numpy as np

import concourse.bass as bass
from concourse import mybir

F32 = mybir.dt.float32
F32R = mybir.dt.float32r
ALU = mybir.AluOpType
ACT = mybir.ActivationFunctionType
AX = mybir.AxisListType.X

P = 128
D = 2048
SEQ = 256
DB, DS = 8, 4
NS = DB * DS
T = SEQ + NS
KT = D // P
DH = 64
QH, KVH = 16, 2
BH, BG = 8, 3
DIL = (1, 4, 16)
WIN = (128, 512, 2048)
FF = 5632
FT_HALF = FF // P // 2
NH = QH + BG * BH
BUCKETS = 32
ALPHA = 2.0 ** 0.25
SCALE = DH ** -0.5
EPS = 1e-5
NEG = -1e30
LOW = -3.0e38
C_QA, C_KVA, C_QB, C_GATE = 0, 1024, 1280, 5888
IN_W = 9984
CK = 1024
RING = 4
AHEAD = 3
NKEY_B = 3 * P + 3 * NS
NKEY_A = P + NS


def bucket(dist):
    d = max(int(dist), 0)
    if d < 16:
        return d
    return min(16 + int(math.log(d / 16) / math.log(2048 / 16) * 16), 31)


def constants():
    ohp = np.zeros((BUCKETS, 384), np.float32)
    maskp = np.full((NH, 384), NEG, np.float32)
    for i in range(384):
        dist = 255 - i
        ohp[bucket(dist), i] = 1
        if 0 <= dist < 128:
            maskp[:QH, i] = 0
        for g in range(BG):
            if 0 <= dist <= WIN[g] and dist % DIL[g] == 0:
                maskp[QH + g * BH:QH + (g + 1) * BH, i] = 0
    ohb = np.zeros((P, NKEY_B), np.float32)
    oha = np.zeros((P, NKEY_A), np.float32)
    maskb = np.zeros((P, 2, NKEY_B), np.float32)
    maska = np.zeros((P, 2, 2, NKEY_A), np.float32)
    for t in range(DS):
        for n in range(P):
            ohb[32 * t + bucket(128 + t - n), n] = 1
            ohb[32 * t + bucket(4 * (128 - n)), P + n] = 1
            ohb[32 * t + bucket(16 * (128 - n)), 2 * P + n] = 1
            oha[32 * t + bucket(128 + t - n), n] = 1
        for k in range(NS):
            oha[32 * t + bucket(t - k % DS), P + k] = 1
            for g in range(BG):
                ohb[32 * t + bucket(t - k % DS), 3 * P + NS * g + k] = 1
    for r in range(P):
        b4, t = r // 32, r % DS
        for bb in range(2):
            b = bb * 4 + b4
            for n in range(P):
                if 128 + t - n > 128:
                    maskb[r, bb, n] = NEG
                if 128 + t - n > 127:
                    maska[r, bb, :, n] = NEG
            for k in range(NS):
                kb, kt = k // DS, k % DS
                if kb != b or kt > t:
                    maska[r, bb, :, P + k] = NEG
                    maskb[r, bb, 3 * P + k] = NEG
                if kb != b or kt != t:
                    maskb[r, bb, 3 * P + NS + k] = NEG
                    maskb[r, bb, 3 * P + 2 * NS + k] = NEG
    return {"ohp": ohp, "maskp": maskp, "ohb": ohb, "oha": oha, "maskb": maskb, "maska": maska,
            "ident": np.eye(P, dtype=np.float32),
            "rowsel": (np.arange(P)[None, :] // DS % 8 == np.arange(8)[:, None]).astype(np.float32)}


class Phase:

    def __init__(self, chunk0, tile0, set0, groups, chunks, tiles=4, sets=1):
        self.chunk0, self.tile0, self.set0, self.groups, self.chunks = chunk0, tile0, set0, groups, chunks
        self.tiles, self.sets = tiles, sets

    def after(self, groups, chunks, tiles=4, sets=1):
        return Phase(self.chunk0 + self.groups * self.chunks, self.tile0 + self.groups * self.tiles * self.sets,
                     self.set0 + self.groups * (self.tiles - 1) * self.sets, groups, chunks, tiles, sets)

    def tile_done(self, i, set_, m, last_chunk):
        if m == self.tiles - 1:
            return 1, self.chunk0 + self.chunks * i + last_chunk + 1
        return 0, self.set0 + (self.tiles - 1) * (self.sets * i + set_) + m + 1


PH_QB = Phase(0, 0, 0, 3, 8)
PH_KB = PH_QB.after(3, 8)
PH_VB = PH_KB.after(3, 8)
PH_QA = PH_VB.after(2, 8)
PH_KVA = PH_QA.after(1, 4, 2)
PH_GATE = PH_KVA.after(8, 8)
PH_MERGE = PH_GATE.after(2, 12, 4, 2)
PH_OUT = PH_MERGE.after(4, 8)
PH_F1 = [PH_OUT.after(11, 8, 2, 2), None]
PH_F2 = [PH_F1[0].after(1, 44, 4, 4), None]
PH_F1[1] = PH_F2[0].after(11, 8, 2, 2)
PH_F2[1] = PH_F1[1].after(1, 44, 4, 4)
CHUNKS = PH_F2[1].chunk0 + 44
FREE0 = PH_GATE.tile0

UNITS = [[(h, "a", h, 0)] for h in range(QH)] + \
        [[(QH + BG * h + g, "b", h, g) for g in range(BG)] for h in range(BH)]
TABLE_ROWS = [h for h in range(QH)] + [QH + BH * g + h for h in range(BH) for g in range(BG)]


def build(nc, x_prompt, x_sample, cache_a, cache_b1, cache_b2, cache_b3, rel_bias, w_in, a_sink, w_oa,
          w_ob, w_out, ln1_g, ln1_b, w_ffn_in, w_ffn_out, ln2_g, ln2_b,
          ohp, maskp, ohb, oha, maskb, maska, ident_in, rowsel,
          y_p, y_s, na_p, nb1_p, nb2_p, nb3_p, na_s, nb1_s, nb2_s, nb3_s):
    caches = (cache_b1, cache_b2, cache_b3)
    nb_p, nb_s = (nb1_p, nb2_p, nb3_p), (nb1_s, nb2_s, nb3_s)
    tok_dram = nc.dram_tensor("tok_scratch", [3, BG, NS, 512], F32, kind="Internal").ap()
    toka_dram = nc.dram_tensor("toka_scratch", [2, NS, P], F32, kind="Internal").ap()
    tz_dram = nc.dram_tensor("bias_scratch", [NH, 384], F32, kind="Internal").ap()

    with ExitStack() as ctx:
        base = (nc.sbuf_base + 63) // 64 * 64

        def at(name, shape, offset, dt=F32):
            return nc.alloc_sbuf_tensor_at(name, shape, dt, offset=base + offset)

        TB = T * 4
        raw = [at(f"raw{s}", [P, CK], 4096 * s) for s in range(RING)]
        whi = [at(f"whi{s}", [P, CK], 16384 + 4096 * s, F32R) for s in range(RING)]
        wlo = [at(f"wlo{s}", [P, CK], 32768 + 4096 * s, F32R) for s in range(RING)]
        XH = at("XH", [P, KT, T], 49152, F32R)
        XL = at("XL", [P, KT, T], 67584, F32R)
        R1 = 86016
        xs_p = at("xs_p", [P, 2, D], R1)
        xs_s = at("xs_s", [NS, D], R1 + 16384)
        QB = at("QB", [P, 12, T], R1)
        KB = at("KB", [P, 12, T], R1 + 12 * TB)
        QA = at("QA", [P, 8, T], R1 + 24 * TB)
        KD = at("KD", [P, 2, T], R1 + 32 * TB)
        GT = at("GT", [P, 32, T], R1)
        R2 = 125184
        VTOK = at("VTOK", [P, 2, BG, 512], R2)
        VAT = at("VAT", [P, 2, P], R2 + 12288)
        PTB = at("PTB", [P, BG, 2, P], R2)
        PTN = at("PTN", [96, 2, P], R2 + 3072)
        PTA = at("PTA", [P, 2, 2, P], R2 + 4096)
        PTNA = at("PTNA", [NS, 2, 2, P], R2 + 6144)
        C1 = at("C1", [P, 2, 512], R2 + 8192)
        CA = at("CA", [P, 2, P], R2 + 12288)
        R3 = 138496
        KTOK = at("KTOK", [P, 2, BG, 512], R3)
        KAT = at("KAT", [P, 2, P], R3 + 12288)
        BIAS = at("BIAS", [P, 4, 256], R3)
        R5 = 170240
        SPS = [at(f"SP{s}", [P, BG, 384], o) for s, o in enumerate((R3 + 4096, R3 + 8704, R5 + 5120, R5 + 9728))]
        PT = at("PT", [P, 3, 384], R3 + 13312)
        QBD = at("QBD", [P, BG, 4, DB, 32], R3)
        KTS = [at("KTS0", [P, 2, 512], R3 + 12288), at("KTS1", [P, 2, 512], R5 + 5120)]
        R4 = 156416
        OT = at("OT", [P, 12, T], R4)
        TOKS = at("TOKS", [NS, BG, 512], R4)
        TOKA = at("TOKA", [NS, 2, P], R4 + 6144)
        FT = at("FT", [P, 4, T], R4 + 7168)
        KAF = at("KAF", [P, T], R4 + 7168 + 4 * TB)
        KST = at("KST", [P, 2, 2, 512], R5)
        QST = at("QST", [P, 2, 2, 512], R5 + 8192)
        PROD = at("PROD", [P, 1024], R5 + 16384)
        OHP = at("OHP", [BUCKETS, 384], R5)
        TZ = at("TZ", [NH, 384], R5 + 1536)
        VST = at("VST", [P, 2, DS, 512], R5)
        OHB = at("OHB", [P, NKEY_B], R5)
        OHA = at("OHA", [P, NKEY_A], R5 + 1920)
        RELT = at("RELT", [P, 5, P], R5 + 2560)
        BIB = at("BIB", [P, 2, NKEY_B], R5 + 16384)
        ST = at("ST", [P, 2, 256], 190720)
        VN = at("VN", [96, 512], 192768)
        VNA = at("VNA", [NS, P], 194816)
        QAS = at("QAS", [64, 2, DB, 8, DS], 195328)
        SRB = at("SRB", [P, 2, NKEY_B], 197376)
        SRA = at("SRA", [P, 2, 2, NKEY_A], 201216)
        BIA = at("BIA", [P, 2, 2, NKEY_A], 203776)
        OTH = at("OTH", [P, 12, T], R2, F32R)
        OTL = at("OTL", [P, 12, T], R2 + 13824, F32R)
        MT = at("MT", [P, 8, T], R2 + 27648)
        MH = at("MH", [P, KT, T], R5, F32R)
        ML = at("ML", [P, KT, T], R5 + 18432, F32R)
        U = at("U", [P, KT, T], R1)
        SUMS = at("SUMS", [P, 2, T], R1 + 18432)
        MU = at("MU", [P, T], R1 + 20736)
        RS = at("RS", [P, T], R1 + 21888)
        VAR = at("VAR", [P, T], R1 + 23040)
        SQ = at("SQ", [P, 4, T], R1 + 24192)
        X1H = at("X1H", [P, KT, T], 49152, F32R)
        X1L = at("X1L", [P, KT, T], 67584, F32R)
        HH = at("HH", [P, FT_HALF, T], R2, F32R)
        HL = at("HL", [P, FT_HALF, T], R2 + 25344, F32R)
        SG = at("SG", [P, 2, T], R2 + 50688)
        HT = at("HT", [P, 2, T], R2 + 52992)
        HF = at("HF", [P, 2, T], R2 + 55296)
        YT = at("YT", [P, 2, D], R2)
        YTS = at("YTS", [NS, D], R2 + 16384)
        R6 = 208704
        ident = at("ident", [P, P], R6)
        ones = at("ones", [P, P], R6 + 512)
        LNP = at("LNP", [P, 4, KT], R6 + 1024)
        REL4 = at("REL4", [P, NH], R6 + 1280)
        SINKB = at("SINKB", [P, QH], R6 + 1440)
        SINKR = at("SINKR", [P, 2], R6 + 1504)
        NM = at("NM", [P, 4, 2], R6 + 1536)
        MX = at("MX", [P, 4, 2, BG], R6 + 2976)
        LS = at("LS", [P, 4, 2], R6 + 1632)
        ES = at("ES", [P, 4, 2], R6 + 1664)
        RL = at("RL", [P, 4, 2], R6 + 1696)
        SMX = at("SMX", [P, 6], R6 + 1728)
        SNM = at("SNM", [P, 6], R6 + 1760)
        SLS = at("SLS", [P, 6], R6 + 1792)
        SES = at("SES", [P, 6], R6 + 1824)
        SRL = at("SRL", [P, 6], R6 + 1856)
        WARM = at("WARM", [P, 1], R6 + 1888)
        lnrow = at("lnrow", [64, P], R6 + 1920)
        ROWSEL = at("ROWSEL", [8, P], R6 + 2432)
        QLO = at("QLO", [64, 8, NS], R6 + 3072)
        SINK2 = at("SINK2", [8, 2], R6 + 2944)

        bank = [ctx.enter_context(nc.psum_tensor(f"bank{i}", [P, 512], F32)) for i in range(8)]

        def sem(name):
            return ctx.enter_context(nc.semaphore(name))

        x_in = [sem(f"x_in{q}") for q in range(4)]; const_in = sem("const_in"); ln_in = sem("ln_in")
        raw_in = [sem(f"raw_in{s}") for s in range(RING)]
        hi_done, lo_done, chunk_used = sem("hi_done"), sem("lo_done"), sem("chunk_used")
        tile_ready, tile_free = sem("tile_ready"), sem("tile_free")
        pb_ready, pb_free = sem("pb_ready"), sem("pb_free")
        xt_ready, xh_done, xl_done = sem("xt_ready"), sem("xh_done"), sem("xl_done")
        setup_pe, setup_dve = sem("setup_pe"), sem("setup_dve")
        tz_out = sem("tz_out")
        ft_ready, ft_turned, ft_copied, tok_ready = sem("ft_ready"), sem("ft_turned"), sem("ft_copied"), sem("tok_ready")
        tok_out = sem("tok_out"); toka_out = sem("toka_out"); kv_out = sem("kv_out")
        new_out = sem("new_out"); copy_out = sem("copy_out")
        unit_in = [sem("unit_in0"), sem("unit_in1")]
        unit_done = sem("unit_done"); prod_done = sem("prod_done")
        kd_in = sem("kd_in"); qas_in = sem("qas_in"); qas_own = sem("qas_own")
        bias_in = [sem(f"bias_in{i}") for i in range(4)]
        s_ready, s_read, m_ready, nm_ready, e_ready, p_ready = (
            sem("s_ready"), sem("s_read"), sem("m_ready"), sem("nm_ready"), sem("e_ready"), sem("p_ready"))
        t_ready, pt_ready, pt_used, o_read = sem("t_ready"), sem("pt_ready"), sem("pt_used"), sem("o_read")
        chain = sem("chain")
        relt_zero, relt_done, qbd_zero, qbd_done = sem("relt_zero"), sem("relt_done"), sem("qbd_zero"), sem("qbd_done")
        samp_in = sem("samp_in"); vn_in = sem("vn_in")
        rowbias_pe, rowbias_done = sem("rowbias_pe"), sem("rowbias_done")
        ck_in = [sem("ck_in0"), sem("ck_in1")]
        kts_pe = sem("kts_pe"); kts_ready = sem("kts_ready"); kts_used = sem("kts_used")
        rows_ready, rows_m, rows_e, rows_p = sem("rows_ready"), sem("rows_m"), sem("rows_e"), sem("rows_p")
        rt_pe, rt_done = sem("rt_pe"), sem("rt_done")
        v_in = [sem("v_in0"), sem("v_in1")]
        v_used = sem("v_used"); cv_in = [sem("cv_in0"), sem("cv_in1")]; cv_used = sem("cv_used")
        os_read = sem("os_read")
        oth_done, otl_done = sem("oth_done"), sem("otl_done")
        mix_done, mh_done, ml_done = sem("mix_done"), sem("mh_done"), sem("ml_done")
        ax_done, sq_done, sum_done, sum_pe, mu_done, cen_done, var_done, sd_done, nrm_done, y_done, x1h_done, x1l_done, x1l_rest = (
            sem("ax_done"), sem("sq_done"), sem("sum_done"), sem("sum_pe"), sem("mu_done"), sem("cen_done"), sem("var_done"),
            sem("sd_done"), sem("nrm_done"), sem("y_done"), sem("x1h_done"), sem("x1l_done"), sem("x1l_rest"))
        sg_done, hh_done, hl_done = sem("sg_done"), sem("hh_done"), sem("hl_done")
        yt_pe, yt_done, y_out = sem("yt_pe"), sem("yt_done"), sem("y_out")

        block = ctx.enter_context(nc.Block())

        def loop(eng, ph, body):
            start = 0
            if ph.chunk0 == 0:
                body(0)
                start = 1
            if ph.groups - start == 1:
                body(start)
            else:
                with eng.Fori(start, ph.groups) as i:
                    body(i)

        def u_made(eng, which, n):
            eng.wait_ge(tile_free, (PH_OUT, PH_F2[1])[which].tile0 - FREE0 + n + 1)

        def known_below(value, limit):
            return isinstance(value, int) and value < limit

        @block.sync
        def _(sp):
            def x_piece(q):
                c = slice(512 * q, 512 * q + 512)
                sp.dma_start(xs_p[:, :, c], x_prompt[0].rearrange("(n p) d -> p n d", p=P)[:, :, c]).then_inc(x_in[q], 16)
                sp.dma_start(xs_s[:, c], x_sample.rearrange("b t d -> (b t) d")[:, c]).then_inc(x_in[q], 16)

            sp.dma_start(ident[:, :], ident_in).then_inc(x_in[0], 16)
            x_piece(0)
            x_piece(1)

            def chunk(ph, i, k, src, shape=None):
                c = ph.chunk0 + ph.chunks * i + k
                if not known_below(c, RING):
                    sp.wait_ge(lo_done, c - RING + 1)
                dst = raw[k % RING][:, :]
                if shape:
                    dst = dst.rearrange(*shape[0], **shape[1])
                sp.dma_start(dst, src).then_inc(raw_in[k % RING], 16)

            def rows(w):
                return w.rearrange("(k p) e -> p k e", p=P)

            two = (("p (k e) -> p k e",), {"k": 2})
            four = (("p (k e) -> p k e",), {"k": 4})
            win = rows(w_in[0])
            for ph, col in ((PH_QB, C_QB), (PH_KB, C_QB + 1536), (PH_VB, C_QB + 3072), (PH_QA, C_QA)):
                def body(i, ph=ph, col=col):
                    for k in range(8):
                        if known_below(ph.chunk0 + ph.chunks * i, 1) and k in (1, 2):
                            x_piece(k + 1)
                        chunk(ph, i, k, win[:, 2 * k:2 * k + 2, bass.ds(col + 512 * i, 512)], two)
                loop(sp, ph, body)
            for k in range(4):
                chunk(PH_KVA, 0, k, win[:, 4 * k:4 * k + 4, C_KVA:C_KVA + 256], four)
                if k == 0:
                    sp.dma_start(lnrow[0:16, :], ln1_g[0].rearrange("(k p) -> k p", p=P)).then_inc(ln_in, 16)
                    sp.dma_start(lnrow[16:32, :], ln1_b[0].rearrange("(k p) -> k p", p=P)).then_inc(ln_in, 16)
                    sp.dma_start(lnrow[32:48, :], ln2_g[0].rearrange("(k p) -> k p", p=P)).then_inc(ln_in, 16)
                    sp.dma_start(lnrow[48:64, :], ln2_b[0].rearrange("(k p) -> k p", p=P)).then_inc(ln_in, 16)

            def gates(i):
                for k in range(8):
                    chunk(PH_GATE, i, k, win[:, 2 * k:2 * k + 2, bass.ds(C_GATE + 512 * i, 512)], two)
            loop(sp, PH_GATE, gates)

            def merge(i):
                for s in range(2):
                    cols = bass.ds(1024 * i + 512 * s, 512)
                    for k in range(4):
                        chunk(PH_MERGE, i, 6 * s + k, rows(w_oa[0])[:, 2 * k:2 * k + 2, cols], two)
                    for k in range(2):
                        chunk(PH_MERGE, i, 6 * s + 4 + k, rows(w_ob[0])[:, 2 * k:2 * k + 2, cols], two)
            loop(sp, PH_MERGE, merge)

            def outp(i):
                for k in range(8):
                    chunk(PH_OUT, i, k, rows(w_out[0])[:, 2 * k:2 * k + 2, bass.ds(512 * i, 512)], two)
            loop(sp, PH_OUT, outp)
            f1 = w_ffn_in[0].rearrange("(k p) (u e) -> p k u e", p=P, u=2)
            f2 = rows(w_ffn_out[0])
            for half in range(2):
                def ffn_in(i, half=half):
                    for k in range(8):
                        chunk(PH_F1[half], i, k,
                              f1[:, 4 * (k // 2):4 * (k // 2) + 4, k % 2, bass.ds(FT_HALF * P * half + 256 * i, 256)], four)
                loop(sp, PH_F1[half], ffn_in)
                for j in range(4):
                    for k in range(11):
                        k0 = FT_HALF * half + 2 * k
                        chunk(PH_F2[half], 0, 11 * j + k, f2[:, k0:k0 + 2, 512 * j:512 * j + 512], two)
            for q in range(4):
                c = slice(512 * q, 512 * q + 512)
                sp.wait_ge(yt_done, 4 * q + 4)
                sp.dma_start(y_p[0].rearrange("(n p) d -> p n d", p=P)[:, :, c], YT[:, :, c]).then_inc(y_out, 16)
                sp.dma_start(y_s.rearrange("b t d -> (b t) d")[:, c], YTS[:, c]).then_inc(y_out, 16)
            sp.wait_ge(y_out, 128)

        @block.gpsimd
        def _(pool):
            for t in range(DS):
                pool.dma_start(REL4[32 * t:32 * t + 32, :], rel_bias).then_inc(const_in, 16)
            pool.dma_start(OHP[:, :], ohp).then_inc(const_in, 16)
            pool.dma_start(TZ[:, :], maskp).then_inc(const_in, 16)
            pool.dma_start(SINKB[:, :], bass.AP(a_sink.tensor, 0, [[0, P], [1, QH]])).then_inc(const_in, 16)
            pool.dma_start(ROWSEL[:, :], rowsel).then_inc(const_in, 16)
            for kv in range(2):
                pool.dma_start(SINK2[:, kv:kv + 1], bass.AP(a_sink.tensor, 8 * kv, [[1, 8], [1, 1]])).then_inc(const_in, 16)
            pool.wait_ge(setup_dve, 1)
            pool.dma_start(tz_dram, TZ[:, :]).then_inc(tz_out, 16)
            def shift(new, old, first, n, pieces):
                row = old.shape[2] * old.shape[3] * old.shape[4]
                src = old.rearrange("b r k h d -> b (r k h d)")[:, bass.ds(first + DS * row, n)]
                dst = new.rearrange("b r k h d -> b (r k h d)")[:, bass.ds(first, n)]
                pool.dma_start(dst.rearrange("b (x y) -> x b y", x=pieces),
                               src.rearrange("b (x y) -> x b y", x=pieces)).then_inc(copy_out, 16)

            shift(na_s[0], cache_a[0], 0, 124 * 256, 16)
            shift(nb1_s[0], cache_b1[0], 0, 124 * 1024, 16)
            pool.wait_ge(tz_out, 16)

            def token_rows(kind, g):
                pool.dma_start(tok_dram[kind, g], TOKS[:, g, :]).then_inc(tok_out, 16)
                pool.wait_ge(tok_out, 16 * (3 * kind + g + 1))
                if kind:
                    w = WIN[g]
                    pool.dma_start(nb_s[g][0, :, w - 4:w, kind - 1].rearrange("b t h d -> b t (h d)"),
                                   tok_dram[kind, g].rearrange("(b t) f -> b t f", b=DB)).then_inc(new_out, 16)

            def unit_load(b, j):
                g, t0 = 1 + j // 2, 2 * (j % 2)
                if not known_below(4 * b + j, 2):
                    pool.wait_ge(unit_done, 4 * b + j - 1)
                keys = caches[g][0].rearrange("b (n r) k h d -> b n r k (h d)", r=DIL[g])
                pool.dma_start(KST[:, j % 2], keys[b, :, t0:t0 + 2, 0, :]).then_inc(unit_in[j % 2], 16)
                q = tok_dram[0, g, 4 * b + t0:4 * b + t0 + 2, :].rearrange("t f -> (t f)")
                pool.dma_start(QST[:, j % 2].rearrange("p t f -> p (t f)"), q.partition_broadcast(P)
                               ).then_inc(unit_in[j % 2], 16)

            def copy_b2(b):
                shift(nb2_s[0, bass.ds(b, 1)], cache_b2[0, bass.ds(b, 1)], 0, 508 * 1024, 32)

            def copy_b3(n):
                shift(nb3_s[0], cache_b3[0], n * (73 * 1024), 73 * 1024, 16)

            for g in range(BG):
                pool.wait_ge(tok_ready, 4 * (g + 1))
                token_rows(0, g)
            unit_load(0, 0)
            unit_load(0, 1)
            for b in range(8):
                unit_load(b, 2)
                unit_load(b, 3)
                if b < 7:
                    unit_load(b + 1, 0)
                    unit_load(b + 1, 1)
                copy_b2(b)
                if b < 6:
                    pool.wait_ge(tok_ready, 4 * (b + 4))
                    token_rows(1 + b // 3, b % 3)
                if b == 2 or b == 5:
                    kv, src = (0, KTOK) if b == 2 else (1, VTOK)
                    pool.dma_start(nb1_p[0, 0, :, kv].rearrange("p h d -> p (h d)"), src[:, 1, 0, :]).then_inc(kv_out, 16)
                    for g in (1, 2):
                        pool.dma_start(nb_p[g][0, 0, :, kv].rearrange("(n p) h d -> p n (h d)", p=P),
                                       src[:, :, g, :]).then_inc(kv_out, 16)
            pool.dma_start(VN[:, :], tok_dram[2].rearrange("g n f -> (g n) f")).then_inc(vn_in, 16)
            pool.wait_ge(ft_copied, 32)
            pool.dma_start(QLO[:, :, :], QA[64:128, :, SEQ:T]).then_inc(qas_in, 16)
            pool.wait_ge(ft_ready, 45)
            pool.dma_start(KD[0:64, 1, :], KAF[64:128, :]).then_inc(kd_in, 16)
            pool.dma_start(KD[64:128, 0, :], KAF[0:64, :]).then_inc(kd_in, 16)
            pool.dma_start(KD[0:64, 0, :], KAF[0:64, :]).then_inc(kd_in, 16)
            pool.dma_start(KD[64:128, 1, :], KAF[64:128, :]).then_inc(kd_in, 16)
            pool.wait_ge(tok_ready, 38)
            for kv, src in ((0, KAT), (1, VAT)):
                pool.dma_start(na_p[0, 0, :, kv].rearrange("p h d -> p (h d)"), src[:, 1, :]).then_inc(kv_out, 16)
                pool.dma_start(toka_dram[kv], TOKA[:, kv, :]).then_inc(toka_out, 16)
            pool.wait_ge(toka_out, 32)
            for kv in range(2):
                pool.dma_start(na_s[0, :, 124:128, kv].rearrange("b t h d -> b t (h d)"),
                               toka_dram[kv].rearrange("(b t) f -> b t f", b=DB)).then_inc(new_out, 16)
            pool.dma_start(VNA[:, :], toka_dram[1]).then_inc(vn_in, 16)
            pool.wait_ge(kv_out, 16 * 8)
            for n, row in enumerate(TABLE_ROWS):
                if n >= 4:
                    pool.wait_ge(s_read, n - 3)
                pool.dma_start(BIAS[:, n % 4, :], bass.AP(tz_dram.tensor, row * 384, [[1, P], [1, 256]])
                               ).then_inc(bias_in[n % 4], 16)
            pool.wait_ge(unit_done, 32)
            pool.dma_start(OHB[:, :], ohb).then_inc(samp_in, 16)
            pool.dma_start(OHA[:, :], oha).then_inc(samp_in, 16)
            pool.dma_start(BIB[:, :, :], maskb).then_inc(samp_in, 16)
            pool.dma_start(BIA[:, :, :, :], maska).then_inc(samp_in, 16)
            nc.gpsimd.memset(RELT[:, :, :], 0.0).then_inc(relt_zero, 1)
            pool.wait_ge(relt_zero, 1)
            for s, h0 in enumerate((QH, QH + BH, QH + 2 * BH, 0, BH)):
                for t in range(DS):
                    q = slice(32 * t, 32 * t + 32)
                    dst = RELT[q, s, :].rearrange("p (b h t) -> p b h t", b=4, t=DS)[:, :, :, t]
                    nc.gpsimd.tensor_copy(dst, REL4[q, h0:h0 + 8].unsqueeze(1).broadcast_to([32, 4, 8])
                                          ).then_inc(relt_done, 1)
            pool.wait_ge(relt_done, 20)
            pool.wait_ge(s_read, 40)
            pool.wait_ge(t_ready, UNITS[21][-1][0] + 1)
            for g in range(BG):
                if g:
                    pool.wait_ge(qbd_done, 8 * g)
                nc.gpsimd.memset(QBD[:, g], 0.0).then_inc(qbd_zero, 1)
                pool.wait_ge(qbd_zero, g + 1)
                for pr in range(4):
                    for hf in range(2):
                        q = slice(64 * hf, 64 * hf + 64)
                        h = 2 * pr + hf
                        nc.gpsimd.tensor_copy(QBD[q, g, pr, :, 4 * h:4 * h + 4],
                                              QB[q, 4 * g + pr, SEQ:T].rearrange("p (b t) -> p b t", t=DS)
                                              ).then_inc(qbd_done, 1)
            pool.wait_ge(pt_used, 40)
            for b in range(DB):
                if b >= 2:
                    pool.wait_ge(kts_pe, b - 1)
                pool.dma_start(C1[:, b % 2, :], cache_b1[0, b, :, 0].rearrange("p h d -> p (h d)")).then_inc(ck_in[b % 2], 16)
                pool.dma_start(CA[:, b % 2, :], cache_a[0, b, :, 0].rearrange("p h d -> p (h d)")).then_inc(ck_in[b % 2], 16)
            for b in range(DB):
                if b == 0:
                    pool.wait_ge(rowbias_done, 2)
                    pool.wait_ge(kts_used, 8)
                for g in (1, 2):
                    if b >= 1:
                        pool.wait_ge(v_used, 2 * b + g - 2)
                    pool.dma_start(VST[:, g - 1], caches[g][0, b].rearrange("(n r) k h d -> n r k (h d)", r=DIL[g])[:, 0:4, 1, :]
                                   ).then_inc(v_in[g - 1], 16)
                if b >= 2:
                    pool.wait_ge(cv_used, b - 1)
                pool.dma_start(C1[:, b % 2, :], cache_b1[0, b, :, 1].rearrange("p h d -> p (h d)")).then_inc(cv_in[b % 2], 16)
                pool.dma_start(CA[:, b % 2, :], cache_a[0, b, :, 1].rearrange("p h d -> p (h d)")).then_inc(cv_in[b % 2], 16)

            def slab_after(ph, n0):
                def body(i):
                    pool.wait_ge(chunk_used, ph.chunk0 + ph.chunks * i + 1)
                    copy_b3(i + n0)
                loop(pool, ph, body)
            slab_after(PH_MERGE, 0)
            slab_after(PH_OUT, 2)
            for k in range(4, KT):
                pool.wait_ge(y_done, k + 1)
                nc.gpsimd.tensor_tensor(X1L[:, k, :], U[:, k, :], X1H[:, k, :].bitcast(F32), ALU.subtract)\
                    .then_inc(x1l_rest, 1)
            slab_after(PH_F1[0], 6)
            slab_after(PH_F1[1], 17)
            pool.wait_ge(copy_out, 16 * (2 + 8 + 28))
            pool.wait_ge(kv_out, 16 * 8)
            pool.wait_ge(new_out, 16 * 8)

        @block.scalar
        def _(act):
            def split(ph, i, k):
                c = ph.chunk0 + ph.chunks * i + k + AHEAD
                if isinstance(c, int) and c >= CHUNKS:
                    return
                s = (k + AHEAD) % RING
                act.wait_ge(raw_in[s], 16 * (ph.chunk0 // RING + ph.chunks // RING * i + (k + AHEAD) // RING + 1))
                if not known_below(c, RING):
                    act.wait_ge(chunk_used, c - RING + 1)
                nc.scalar.activation(whi[s][:, :], raw[s][:, :], ACT.Copy).then_inc(hi_done, 1)

            for k in range(KT):
                act.wait_ge(xt_ready, k + 1)
                nc.scalar.activation(XH[:, k, :], bank[4 + k % 4][:, 0:T], ACT.Copy).then_inc(xh_done, 1)
                if k >= 7 and k % 4 == 3:
                    c = (k - 7) // 4
                    act.wait_ge(raw_in[c], 16)
                    nc.scalar.activation(whi[c][:, :], raw[c][:, :], ACT.Copy).then_inc(hi_done, 1)

            def tile(ph, i, m):
                which, value = ph.tile_done(i, 0, m, ph.chunks - 1)
                act.wait_ge((tile_ready, chunk_used)[which], value)
                return bank[m]

            def project(kind, ph, i):
                n0 = ph.tile0 + 4 * i

                def evacuate(m):
                    src = tile(ph, i, m)
                    if not known_below(n0 + m, 4):
                        act.wait_ge(ft_turned, 36 if kind == "qa" else n0 + m - 3)
                        act.wait_ge(ft_copied, {"q": n0 + m - 3, "k": n0 + m - 3, "v": 24, "qa": 4 * i + m + 21}[kind])
                    nc.scalar.activation(FT[:, m, :], src[:, 0:T], ACT.Copy,
                                         scale=SCALE if kind in ("q", "qa") else 1.0)\
                        .then_inc(ft_ready, 1)

                def token_rows(m):
                    act.wait_ge(ft_turned, n0 + m + 1)
                    b = bank[4 + m]
                    if kind in ("k", "v"):
                        dst = (KTOK if kind == "k" else VTOK)[:, :, bass.ds(i, 1), m * P:m * P + P]
                        nc.scalar.activation(dst.rearrange("p n g f -> p (n g) f"),
                                             b[:, 0:256].rearrange("p (n f) -> p n f", n=2), ACT.Copy)
                    nc.scalar.activation(TOKS[:, bass.ds(i, 1), m * P:m * P + P].rearrange("p g f -> p (g f)"),
                                         b[0:NS, 256:384], ACT.Copy).then_inc(tok_ready, 1)

                for k in range(8):
                    split(ph, i, k)
                evacuate(0)
                for m in range(1, 4):
                    evacuate(m)
                    if kind != "qa":
                        token_rows(m - 1)
                if kind != "qa":
                    token_rows(3)

            loop(act, PH_QB, lambda i: project("q", PH_QB, i))
            act.wait_ge(tok_out, 16 * 3)
            loop(act, PH_KB, lambda i: project("k", PH_KB, i))
            act.wait_ge(tok_out, 16 * 6)
            loop(act, PH_VB, lambda i: project("v", PH_VB, i))
            loop(act, PH_QA, lambda i: project("qa", PH_QA, i))
            for k in range(4):
                split(PH_KVA, 0, k)
            tile(PH_KVA, 0, 0)
            nc.scalar.activation(KAF[:, :], bank[0][:, 0:T], ACT.Copy).then_inc(ft_ready, 1)
            tile(PH_KVA, 0, 1)
            act.wait_ge(ft_copied, 29)
            nc.scalar.activation(FT[:, 0, :], bank[1][:, 0:T], ACT.Copy).then_inc(ft_ready, 1)
            for m in range(2):
                act.wait_ge(ft_turned, 36 + m + 1)
                nc.scalar.activation((KAT, VAT)[m][:, :, :], bank[4 + m][:, 0:256].rearrange("p (n f) -> p n f", n=2), ACT.Copy)
                nc.scalar.activation(TOKA[:, m, :], bank[4 + m][0:NS, 256:384], ACT.Copy).then_inc(tok_ready, 1)

            def exponentials(u):
                blocks, s = UNITS[u], u % 4
                act.wait_ge(nm_ready, u + 1)
                for qb in range(2):
                    cols = slice(0, 128) if qb == 0 else slice(128, 384)
                    v = SPS[s][:, 0:len(blocks), cols]
                    ins = nc.scalar.activation(v, v, ACT.Exp, bias=NM[:, s, qb:qb + 1], accum_out=LS[:, s, qb:qb + 1])
                    ins.then_inc(e_ready, 1)
                if len(blocks) == 1:
                    nc.scalar.activation(ES[:, s, :], NM[:, s, :], ACT.Exp, bias=SINKB[:, u:u + 1]).then_inc(e_ready, 1)

            def turned(n):
                act.wait_ge(t_ready, n + 1)
                if n >= 3:
                    act.wait_ge(pt_used, n - 2)
                nc.scalar.activation(PT[:, n % 3, :], bank[3 + n % 2][:, 0:384], ACT.Copy).then_inc(pt_ready, 1)

            exponentials(0)
            exponentials(1)
            for u in range(len(UNITS)):
                for n, *_ in UNITS[u]:
                    turned(n)
                if u + 2 < len(UNITS):
                    exponentials(u + 2)

            for b in range(DB):
                act.wait_ge(kts_pe, b + 1)
                if b >= 2:
                    act.wait_ge(kts_used, b - 1)
                kt, b0 = KTS[b % 2], 4 + 2 * (b % 2)
                nc.scalar.activation(kt[:, 0, :], bank[b0][:, 0:512], ACT.Copy)
                nc.scalar.activation(kt[0:64, 1, 0:256], bank[b0 + 1][0:64, 0:256], ACT.Copy).then_inc(kts_ready, 1)
            for r in range(2):
                act.wait_ge(rows_m, r + 1)
                nc.scalar.activation(SRB[:, r, :], SRB[:, r, :], ACT.Exp, bias=SNM[:, r:r + 1],
                                     accum_out=SLS[:, r:r + 1]).then_inc(rows_e, 1)
            act.wait_ge(rows_m, 6)
            for r in range(2, 6):
                v = SRA[:, (r - 2) // 2, r % 2, :]
                nc.scalar.activation(v, v, ACT.Exp, bias=SNM[:, r:r + 1], accum_out=SLS[:, r:r + 1]).then_inc(rows_e, 1)
                nc.scalar.activation(SES[:, r:r + 1], SNM[:, r:r + 1], ACT.Exp,
                                     bias=SINKR[:, r % 2:r % 2 + 1]).then_inc(rows_e, 1)
            act.wait_ge(rt_pe, 1)
            nc.scalar.activation(PTB[:, :, 0, :], bank[4][:, 0:384].rearrange("p (g r) -> p g r", g=3), ACT.Copy)
            nc.scalar.activation(PTB[:, :, 1, :], bank[5][:, 0:384].rearrange("p (g r) -> p g r", g=3), ACT.Copy)
            nc.scalar.activation(PTN[:, 0, :], bank[4][0:96, 384:512], ACT.Copy)
            nc.scalar.activation(PTN[:, 1, :], bank[5][0:96, 384:512], ACT.Copy)
            act.wait_ge(rt_pe, 2)
            nc.scalar.activation(PTA[:, :, :, :], bank[6][:, :].rearrange("p (b k r) -> p k b r", b=2, k=2), ACT.Copy)
            nc.scalar.activation(PTNA[:, :, :, :], bank[7][0:NS, :].rearrange("p (b k r) -> p k b r", b=2, k=2),
                                 ACT.Copy).then_inc(rt_done, 1)

            def gates(i):
                for k in range(8):
                    split(PH_GATE, i, k)
                for m in range(4):
                    src = tile(PH_GATE, i, m)
                    nc.scalar.activation(GT[:, bass.ds(4 * i + m, 1), :].rearrange("p n t -> p (n t)"), src[:, 0:T],
                                         ACT.Sigmoid).then_inc(tile_free, 1)
            loop(act, PH_GATE, gates)

            for n in range(3):
                act.wait_ge(os_read, 1)
                nc.scalar.activation(OTH[:, 4 * n:4 * n + 4, :], OT[:, 4 * n:4 * n + 4, :], ACT.Copy).then_inc(oth_done, 1)

            def merge(i):
                for k in range(12):
                    split(PH_MERGE, i, k)
                    if k % 6 == 5:
                        s = k // 6
                        for m in range(4):
                            n = 8 * i + 4 * s + m
                            act.wait_ge(mix_done, n + 1)
                            nc.scalar.activation(MH[:, bass.ds(n, 1), :].rearrange("p n t -> p (n t)"), MT[:, m, :],
                                                 ACT.Copy).then_inc(mh_done, 1)
            loop(act, PH_MERGE, merge)

            def squares(which, n0):
                for m in range(4):
                    u_made(act, which, n0 + m)
                    nc.scalar.activation(SQ[:, m, :], U[:, bass.ds(n0 + m, 1), :].rearrange("p n t -> p (n t)"), ACT.Square)\
                        .then_inc(sq_done, 1)

            def outp(i):
                for k in range(8):
                    split(PH_OUT, i, k)
                squares(0, 4 * i)
            loop(act, PH_OUT, outp)

            def norm(which):
                nc.scalar.activation(WARM[:, :], ones[:, 0:1], ACT.Sqrt)
                act.wait_ge(sum_pe, 2 * which + 1)
                nc.scalar.activation(MU[:, :], bank[4][:, 0:T], ACT.Copy).then_inc(mu_done, 1)
                nc.scalar.activation(RS[:, :], bank[4][:, 0:T], ACT.Square).then_inc(mu_done, 1)
                act.wait_ge(var_done, 2 * which + 1)
                nc.scalar.activation(VAR[:, :], VAR[:, :], ACT.Sqrt).then_inc(sd_done, 1)
                for k in range(KT):
                    if k % 4 == 0:
                        act.wait_ge(nrm_done, 4 * which + k // 4 + 1)
                    g, b = LNP[:, 2 * which, k:k + 1], LNP[:, 2 * which + 1, k:k + 1]
                    if which == 0:
                        nc.scalar.activation(X1H[:, k, :], U[:, k, :], ACT.Identity, scale=g, bias=b).then_inc(x1h_done, 1)
                        act.wait_ge(x1h_done, k + 1)
                    nc.scalar.activation(U[:, k, :], U[:, k, :], ACT.Identity, scale=g, bias=b).then_inc(y_done, 1)

            norm(0)
            for half in range(2):
                def ffn_in(i, half=half):
                    ph = PH_F1[half]
                    for k in range(8):
                        split(ph, i, k)
                    n = 22 * half + 2 * i
                    for j in range(2):
                        which, value = ph.tile_done(i, 0, j, 6)
                        act.wait_ge((tile_ready, chunk_used)[which], value)
                        src = bank[j]
                        nc.scalar.activation(SG[:, j, :], src[:, 0:T], ACT.Sigmoid).then_inc(sg_done, 1)
                    for j in range(2):
                        act.wait_ge(tile_free, ph.tile0 - FREE0 + 4 * i + 2 + j + 1)
                        nc.scalar.activation(HH[:, bass.ds(2 * i + j, 1), :].rearrange("p n t -> p (n t)"), HF[:, j, :],
                                             ACT.Copy).then_inc(hh_done, 1)
                loop(act, PH_F1[half], ffn_in)
                for k in range(44):
                    split(PH_F2[half], 0, k)
                    if half == 1 and k % 11 == 10:
                        squares(1, 4 * (k // 11))
            norm(1)
            for k in range(KT):
                act.wait_ge(yt_pe, k + 1)
                b = bank[6 + k % 2]
                nc.scalar.activation(YT[:, :, k * P:k * P + P], b[:, 0:256].rearrange("p (n f) -> p n f", n=2), ACT.Copy)
                nc.scalar.activation(YTS[:, k * P:k * P + P], b[0:NS, 256:384], ACT.Copy).then_inc(yt_done, 1)

        @block.vector
        def _(dve):
            count = [0]

            def link(ins):
                count[0] += 1
                ins.then_inc(chain, 1)
                dve.wait_ge(chain, count[0])

            def split(ph, i, k):
                c = ph.chunk0 + ph.chunks * i + k + AHEAD
                if isinstance(c, int) and c >= CHUNKS:
                    return
                s = (k + AHEAD) % RING
                dve.wait_ge(hi_done, c + 1)
                nc.vector.tensor_tensor(wlo[s][:, :], raw[s][:, :], whi[s][:, :].bitcast(F32), ALU.subtract).then_inc(lo_done, 1)

            link(nc.vector.memset(ones[:, :], 1.0 / D))
            for k in range(KT):
                dve.wait_ge(xh_done, k + 1)
                nc.vector.tensor_tensor(XL[:, k, :], bank[4 + k % 4][:, 0:T], XH[:, k, :].bitcast(F32),
                                        ALU.subtract).then_inc(xl_done, 1)
                if k >= 7 and k % 4 == 3:
                    c = (k - 7) // 4
                    dve.wait_ge(hi_done, c + 1)
                    nc.vector.tensor_tensor(wlo[c][:, :], raw[c][:, :], whi[c][:, :].bitcast(F32), ALU.subtract).then_inc(lo_done, 1)
            def head_bias():
                dve.wait_ge(setup_pe, 1)
                dve.wait_ge(const_in, 16 * 10)
                nc.vector.tensor_tensor(TZ[:, :], bank[4][0:NH, 0:384], TZ[:, :], ALU.add).then_inc(setup_dve, 1)
                nc.vector.tensor_copy(SINKR[:, :], bank[4][:, 400:402]).then_inc(setup_dve, 1)

            def unit(b, j):
                n = 4 * b + j
                g, t0 = 1 + j // 2, 2 * (j % 2)
                dve.wait_ge(unit_in[j % 2], 64 * b + 32 * (j // 2) + 32)
                if not known_below(n, 1):
                    dve.wait_ge(unit_done, n)
                nc.vector.tensor_tensor(PROD[:, :], KST[:, j % 2].rearrange("p t f -> p (t f)"),
                                        QST[:, j % 2].rearrange("p t f -> p (t f)"), ALU.mult).then_inc(prod_done, 1)
                dve.wait_ge(prod_done, n + 1)
                dst = ST[:, g - 1, bass.ds(32 * b, 32)].rearrange("p (h t) -> p t h", t=DS)[:, t0:t0 + 2, :]
                nc.vector.tensor_reduce(dst, PROD[:, :].rearrange("p (t h d) -> p t h d", t=2, h=BH),
                                        AX, ALU.add).then_inc(unit_done, 1)

            def project(kind, ph, i):
                n0 = ph.tile0 + 4 * i
                b = None if kind == "q" else i + {"k": 0, "v": 3, "qa": 6}[kind]
                for k in range(8):
                    split(ph, i, k)
                    if b is not None and k % 2 == 1:
                        unit(b, k // 2)
                if kind != "v":
                    dst = {"q": QB, "k": KB, "qa": QA}[kind]
                    for m in range(4):
                        dve.wait_ge(ft_ready, n0 + m + 1)
                        d = dst[:, bass.ds(4 * i + m, 1), :].rearrange("p n t -> p (n t)")
                        if kind == "k":
                            nc.vector.tensor_copy(d, FT[:, m, :]).then_inc(ft_copied, 1)
                        else:
                            nc.vector.tensor_copy(d[:, 0:SEQ].rearrange("p (n c) -> p n c", n=2),
                                                  FT[:, m, 0:SEQ].rearrange("p (n c) -> p n c", n=2)[:, :, ::-1])
                            nc.vector.tensor_copy(d[:, SEQ:T], FT[:, m, SEQ:T]).then_inc(ft_copied, 1)
                if known_below(n0, 1):
                    head_bias()

            loop(dve, PH_QB, lambda i: project("q", PH_QB, i))
            loop(dve, PH_KB, lambda i: project("k", PH_KB, i))
            loop(dve, PH_VB, lambda i: project("v", PH_VB, i))
            loop(dve, PH_QA, lambda i: project("qa", PH_QA, i))
            dve.wait_ge(ft_copied, 32)
            for par in range(2):
                if par:
                    dve.wait_ge(qas_in, 16)
                src = QLO[:, :, :] if par else QA[0:64, :, SEQ:T]
                for kv in range(2):
                    nc.vector.tensor_copy(QAS[:, kv, :, par:8:2, :].rearrange("p b g t -> p g b t"),
                                          src[:, 4 * kv:4 * kv + 4, :].rearrange("p g (b t) -> p g b t", t=DS)).then_inc(qas_own, 1)
            for k in range(4):
                split(PH_KVA, 0, k)

            def logits(u):
                blocks, s = UNITS[u], u % 4
                if u >= 4:
                    dve.wait_ge(t_ready, UNITS[u - 4][-1][0] + 1)
                if u == 0:
                    dve.wait_ge(kv_out, 16 * 8)
                if u == 2:
                    dve.wait_ge(unit_done, 32)
                for j, (n, *_) in enumerate(blocks):
                    dve.wait_ge(s_ready, n + 1)
                    dve.wait_ge(bias_in[n % 4], 16 * (n // 4 + 1))
                    b = bank[n % 3]
                    nc.vector.tensor_tensor_reduce(SPS[s][:, j, 0:128], b[:, 0:128], BIAS[:, n % 4, 128:256], 1.0, LOW,
                                                   ALU.add, ALU.max, MX[:, s, 0, j:j + 1]).then_inc(m_ready, 1)
                    nc.vector.tensor_tensor_reduce(SPS[s][:, j, 128:384], b[:, 128:384], BIAS[:, n % 4, :], 1.0, LOW,
                                                   ALU.add, ALU.max, MX[:, s, 1, j:j + 1]).then_inc(s_read, 1)
                dve.wait_ge(m_ready, blocks[-1][0] + 1)
                dve.wait_ge(s_read, blocks[-1][0] + 1)
                if len(blocks) == 1:
                    nc.vector.tensor_scalar(NM[:, s, :], MX[:, s, :, 0], SINKB[:, u:u + 1], -1.0, ALU.max, ALU.mult)\
                        .then_inc(nm_ready, 1)
                else:
                    nc.vector.tensor_reduce(NM[:, s, :], MX[:, s, :, :], AX, ALU.max, negate=True).then_inc(nm_ready, 1)

            def normalise(u):
                blocks, s = UNITS[u], u % 4
                dve.wait_ge(e_ready, 3 * (u + 1) if u < QH else 3 * QH + 2 * (u - QH + 1))
                if len(blocks) == 1:
                    link(nc.vector.tensor_tensor(LS[:, s, :], LS[:, s, :], ES[:, s, :], ALU.add))
                link(nc.vector.reciprocal(RL[:, s, :], LS[:, s, :]))
                for qb in range(2):
                    cols = slice(0, 128) if qb == 0 else slice(128, 384)
                    v = SPS[s][:, 0:len(blocks), cols]
                    ins = nc.vector.tensor_scalar(v, v, RL[:, s, qb:qb + 1], None, ALU.mult)
                    ins.then_inc(p_ready, 1)

            def output(pair):
                dve.wait_ge(pt_used, UNITS[2 * pair + 1][-1][0] + 1)
                nc.vector.tensor_copy(OT[:, pair, 0:SEQ].rearrange("p (n c) -> p n c", n=2),
                                      bank[5 + pair % 2][:, 0:SEQ].rearrange("p (n c) -> p n c", n=2)[:, :, ::-1])\
                    .then_inc(o_read, 1)

            dve.wait_ge(const_in, 16 * 10)
            logits(0)
            logits(1)
            for u in range(len(UNITS)):
                normalise(u)
                if u + 2 < len(UNITS):
                    logits(u + 2)
                if u % 2 == 0 and u:
                    if u == 2:
                        dve.wait_ge(toka_out, 32)
                        dve.wait_ge(tok_out, 16 * 9)
                        dve.wait_ge(kd_in, 64)
                    output(u // 2 - 1)
            output(len(UNITS) // 2 - 1)

            dve.wait_ge(samp_in, 64)
            dve.wait_ge(rowbias_pe, 1)
            for bb in range(2):
                ins = nc.vector.tensor_tensor(BIB[:, bb, :], bank[6][:, 0:NKEY_B], BIB[:, bb, :], ALU.add)
                if bb == 1:
                    ins.then_inc(rowbias_done, 1)
            for bb in range(2):
                ins = nc.vector.tensor_tensor(BIA[:, bb, :, :], bank[7][:, 0:2 * NKEY_A].rearrange("p (k n) -> p k n", k=2),
                                              BIA[:, bb, :, :], ALU.add)
                if bb == 1:
                    ins.then_inc(rowbias_done, 1)
            dve.wait_ge(rowbias_done, 2)
            for bb in range(2):
                dve.wait_ge(rows_ready, 1)
                link(nc.vector.tensor_tensor_reduce(SRB[:, bb, :], bank[bb][:, 0:NKEY_B], BIB[:, bb, :], 1.0, LOW,
                                                    ALU.add, ALU.max, SMX[:, bb:bb + 1]))
                nc.vector.tensor_scalar(SNM[:, bb:bb + 1], SMX[:, bb:bb + 1], -1.0, None, ALU.mult).then_inc(rows_m, 1)
            for r in range(2, 6):
                bb, kv = (r - 2) // 2, r % 2
                link(nc.vector.tensor_tensor_reduce(SRA[:, bb, kv, :], bank[2 + bb][:, kv * NKEY_A:kv * NKEY_A + NKEY_A],
                                                    BIA[:, bb, kv, :], 1.0, LOW, ALU.add, ALU.max, SMX[:, r:r + 1]))
                nc.vector.tensor_scalar(SNM[:, r:r + 1], SMX[:, r:r + 1], SINKR[:, kv:kv + 1], -1.0, ALU.max, ALU.mult)\
                    .then_inc(rows_m, 1)
            dve.wait_ge(rows_e, 10)
            link(nc.vector.tensor_tensor(SLS[:, 2:6], SLS[:, 2:6], SES[:, 2:6], ALU.add))
            link(nc.vector.reciprocal(SRL[:, :], SLS[:, :]))
            for r in range(6):
                v = SRB[:, r, :] if r < 2 else SRA[:, (r - 2) // 2, r % 2, :]
                nc.vector.tensor_scalar(v, v, SRL[:, r:r + 1], None, ALU.mult).then_inc(rows_p, 1)

            def gates(i):
                for k in range(8):
                    split(PH_GATE, i, k)
            loop(dve, PH_GATE, gates)
            dve.wait_ge(v_used, 16)
            for hf in range(2):
                q = slice(64 * hf, 64 * hf + 64)
                nc.vector.tensor_copy(OT[q, 8:12, SEQ:T], bank[4][q, 0:256].rearrange("p (r h n) -> p r h n", r=4, h=2)[:, :, hf, :])
                ins = nc.vector.tensor_copy(OT[q, 0:8, SEQ:T], bank[5][q, 0:256].rearrange("p (r n) -> p r n", r=8))
            ins.then_inc(os_read, 1)
            for n in range(3):
                dve.wait_ge(oth_done, n + 1)
                nc.vector.tensor_tensor(OTL[:, 4 * n:4 * n + 4, :], OT[:, 4 * n:4 * n + 4, :],
                                        OTH[:, 4 * n:4 * n + 4, :].bitcast(F32), ALU.subtract).then_inc(otl_done, 1)

            def one(buf, n):
                return buf[:, bass.ds(n, 1), :].rearrange("p n t -> p (n t)")

            def merge(i):
                for k in range(12):
                    split(PH_MERGE, i, k)
                    s = k // 6
                    for m in range(4):
                        n = 8 * i + 4 * s + m
                        if k % 6 == 3:
                            which, value = PH_MERGE.tile_done(i, s, m, 6 * s + 3)
                            dve.wait_ge((tile_ready, chunk_used)[which], value)
                            nc.vector.tensor_tensor(MT[:, m, :], bank[m][:, 0:T], one(GT, n), ALU.mult).then_inc(tile_free, 1)
                        if k % 6 == 5:
                            if m < 3:
                                dve.wait_ge(pb_ready, 6 * i + 3 * s + m + 1)
                            else:
                                dve.wait_ge(chunk_used, PH_MERGE.chunk0 + 12 * i + 6 * s + 6)
                            nc.vector.tensor_tensor(MT[:, 4 + m, :], bank[4 + m][:, 0:T], one(GT, n + 16), ALU.mult)\
                                .then_inc(pb_free, 1)
                    if k % 6 == 5:
                        for m in range(4):
                            n = 8 * i + 4 * s + m
                            dve.wait_ge(pb_free, n + 1)
                            nc.vector.tensor_tensor(MT[:, m, :], MT[:, m, :], MT[:, 4 + m, :], ALU.add).then_inc(mix_done, 1)
                        for m in range(4):
                            n = 8 * i + 4 * s + m
                            dve.wait_ge(mh_done, n + 1)
                            nc.vector.tensor_tensor(one(ML, n), MT[:, m, :], one(MH, n).bitcast(F32), ALU.subtract).then_inc(ml_done, 1)
            loop(dve, PH_MERGE, merge)

            def sums(which, n, m):
                u_made(dve, which, n)
                dve.wait_ge(sum_done, 33 * which + 2 * n + 1)
                nc.vector.tensor_tensor(SUMS[:, 0, :], SUMS[:, 0, :], one(U, n), ALU.add).then_inc(sum_done, 1)
                dve.wait_ge(sq_done, KT * which + n + 1)
                nc.vector.tensor_tensor(SUMS[:, 1, :], SUMS[:, 1, :], SQ[:, m, :], ALU.add).then_inc(sum_done, 1)

            nc.vector.memset(SUMS[:, :, :], 0.0).then_inc(sum_done, 1)

            def outp(i):
                for k in range(8):
                    split(PH_OUT, i, k)
                    m = k // 2
                    n = 4 * i + m
                    if k % 2 == 0:
                        nc.vector.tensor_scalar(one(U, n), one(XH, n).bitcast(F32), ALPHA, None, ALU.mult).then_inc(ax_done, 1)
                    else:
                        dve.wait_ge(ax_done, 2 * n + 1)
                        nc.vector.scalar_tensor_tensor(out=one(U, n), in0=one(XL, n).bitcast(F32), scalar=ALPHA,
                                                       in1=one(U, n), op0=ALU.mult, op1=ALU.add).then_inc(ax_done, 1)
                for m in range(4):
                    n = 4 * i + m
                    which, value = PH_OUT.tile_done(i, 0, m, 7)
                    dve.wait_ge((tile_ready, chunk_used)[which], value)
                    dve.wait_ge(ax_done, 2 * n + 2)
                    nc.vector.tensor_tensor(one(U, n), bank[m][:, 0:T], one(U, n), ALU.add).then_inc(tile_free, 1)
                    if m:
                        sums(0, n - 1, m - 1)
                sums(0, 4 * i + 3, 3)
            loop(dve, PH_OUT, outp)

            def norm(which):
                dve.wait_ge(mu_done, 2 * which + 1)
                v = [U[:, 4 * n:4 * n + 4, :] for n in range(4)]

                def centre(n):
                    nc.vector.tensor_tensor(v[n], v[n], MU[:, :].unsqueeze(1).broadcast_to([P, 4, T]), ALU.subtract)\
                        .then_inc(cen_done, 1)

                def scale(n):
                    dve.wait_ge(cen_done, 4 * which + n + 1)
                    nc.vector.tensor_tensor(v[n], v[n], RS[:, :].unsqueeze(1).broadcast_to([P, 4, T]), ALU.mult)\
                        .then_inc(nrm_done, 1)

                def low(n):
                    for k in range(4 * n, 4 * n + 4):
                        dve.wait_ge(y_done, k + 1)
                        nc.vector.tensor_tensor(X1L[:, k, :], U[:, k, :], X1H[:, k, :].bitcast(F32), ALU.subtract)\
                            .then_inc(x1l_done, 1)

                dve.wait_ge(mu_done, 2 * which + 2)
                dve.wait_ge(sum_pe, 2 * which + 2)
                link(nc.vector.tensor_tensor(VAR[:, :], bank[5][:, 0:T], RS[:, :], ALU.subtract))
                nc.vector.tensor_scalar(VAR[:, :], VAR[:, :], 0.0, EPS, ALU.max, ALU.add).then_inc(var_done, 1)
                centre(0)
                dve.wait_ge(sd_done, which + 1)
                nc.vector.reciprocal(RS[:, :], VAR[:, :]).then_inc(var_done, 1)
                dve.wait_ge(var_done, 2 * which + 2)
                scale(0)
                for n in range(1, 4):
                    centre(n)
                    scale(n)
                    if which == 0 and n == 1:
                        low(0)

            dve.wait_ge(setup_pe, 2)
            link(nc.vector.tensor_copy(LNP[:, :, :], bank[7][:, 0:64].rearrange("p (a k) -> p a k", a=4)))
            norm(0)
            for half in range(2):
                def ffn_in(i, half=half):
                    ph = PH_F1[half]
                    for k in range(8):
                        split(ph, i, k)
                    n = 22 * half + 2 * i
                    t0 = ph.tile0 + 4 * i
                    for j in range(2):
                        dve.wait_ge(sg_done, n + j + 1)
                        nc.vector.tensor_tensor(HT[:, j, :], bank[j][:, 0:T], SG[:, j, :], ALU.mult).then_inc(tile_free, 1)
                    for j in range(2):
                        dve.wait_ge(tile_free, t0 - FREE0 + j + 1)
                        which, value = ph.tile_done(i, 1, j, 7)
                        dve.wait_ge((tile_ready, chunk_used)[which], value)
                        nc.vector.tensor_tensor(HF[:, j, :], bank[2 + j][:, 0:T], HT[:, j, :], ALU.mult).then_inc(tile_free, 1)
                    for j in range(2):
                        dve.wait_ge(hh_done, n + j + 1)
                        nc.vector.tensor_tensor(one(HL, 2 * i + j), HF[:, j, :], one(HH, 2 * i + j).bitcast(F32),
                                                ALU.subtract).then_inc(hl_done, 1)
                loop(dve, PH_F1[half], ffn_in)
                if half == 1:
                    nc.vector.memset(SUMS[:, :, :], 0.0).then_inc(sum_done, 1)
                for k in range(44):
                    split(PH_F2[half], 0, k)
                    if k % 11 == 10:
                        j = k // 11
                        for m in range(4):
                            n = 4 * j + m
                            which, value = PH_F2[half].tile_done(0, j, m, k)
                            dve.wait_ge((tile_ready, chunk_used)[which], value)
                            nc.vector.scalar_tensor_tensor(out=U[:, n, :], in0=U[:, n, :], scalar=ALPHA if half == 0 else 1.0,
                                                           in1=bank[m][:, 0:T], op0=ALU.mult, op1=ALU.add).then_inc(tile_free, 1)
                            if half == 1:
                                if m:
                                    sums(1, n - 1, m - 1)
                                if m == 3:
                                    sums(1, n, m)
            norm(1)

        @block.tensor
        def _(pe):
            def mm(out, lhsT, rhs, start, stop, **kw):
                return nc.tensor.matmul(out, lhsT, rhs, start=start, stop=stop, **kw)

            def turn(out, in_, n=P):
                return nc.tensor.transpose(out, in_, ident[0:n, 0:n])

            def chunk_products(ph, i, k, k0, hi, lo, banks, first, last, free_wait=None, after=None, kk=2, m_n=4, ready=None):
                c = ph.chunk0 + ph.chunks * i + k
                s = k % RING
                pe.wait_ge(lo_done, c + 1)
                w = CK // kk
                for m in range(m_n):
                    if first and free_wait:
                        free_wait(m)
                    for q in range(kk):
                        a = whi[s][:, q * w + m * P:q * w + m * P + P]
                        b = wlo[s][:, q * w + m * P:q * w + m * P + P]
                        out = bank[banks + m][:, 0:T]
                        st, sp_ = first and q == 0, last and q == kk - 1
                        mm(out, a, hi[:, k0 + q, :], st, False)
                        mm(out, a, lo[:, k0 + q, :], False, False)
                        ins = mm(out, b, hi[:, k0 + q, :], False, sp_)
                    if last and m < m_n - 1:
                        ins.then_inc(ready or tile_ready, 1)
                    if last and after and m:
                        after(m - 1)
                ins.then_inc(chunk_used, 1)
                if last and after:
                    after(m_n - 1)

            def x_turn(k):
                if k % 4 == 0:
                    pe.wait_ge(x_in[k // 4], 32 if k else 48)
                if k >= 4:
                    pe.wait_ge(xl_done, k - 3)
                b = bank[4 + k % 4]
                turn(b[:, 0:P], xs_p[:, 0, k * P:k * P + P])
                turn(b[:, P:2 * P], xs_p[:, 1, k * P:k * P + P])
                turn(b[:, 2 * P:T], xs_s[:, k * P:k * P + P], NS).then_inc(xt_ready, 1)

            def free_wait(ph, i, s=0):
                def wait(m):
                    n = ph.tile0 + ph.tiles * (ph.sets * i + s) + m
                    if ph.chunk0 < PH_GATE.chunk0:
                        if not known_below(n, 4):
                            pe.wait_ge(ft_ready, n - 3)
                    elif not known_below(n, FREE0 + 4):
                        pe.wait_ge(tile_free, n - FREE0 - 3)
                return wait

            def project(kind, ph, i):
                n0 = ph.tile0 + 4 * i

                def rows(m):
                    pe.wait_ge(ft_ready, n0 + m + 1)
                    if not known_below(n0, 4):
                        pe.wait_ge(tok_ready, n0 + m - 3)
                        if kind == "q":
                            pe.wait_ge(setup_dve, 2)
                    b = bank[4 + m]
                    if kind in ("k", "v"):
                        turn(b[:, 0:P], FT[:, m, 0:P])
                        turn(b[:, P:2 * P], FT[:, m, P:2 * P])
                    turn(b[0:NS, 256:384], FT[:, m, SEQ:T]).then_inc(ft_turned, 1)

                for k in range(8):
                    if known_below(n0, 1):
                        for t in (range(8), range(8, 12), range(12, 16), (), (), (), (), ())[k]:
                            x_turn(t)
                        pe.wait_ge(xl_done, 2 * k + 2)
                    chunk_products(ph, i, k, 2 * k, XH, XL, 0, k == 0, k == 7, free_wait(ph, i),
                                   rows if kind != "qa" else None)
                if known_below(n0, 1):
                    pe.wait_ge(const_in, 16 * 10)
                    pe.wait_ge(tok_ready, 1)
                    mm(bank[4][:, 400:402], ROWSEL[:, :], SINK2[:, :], True, True)
                    mm(bank[4][0:NH, 0:384], REL4[0:32, :], OHP[:, :], True, True).then_inc(setup_pe, 1)

            loop(pe, PH_QB, lambda i: project("q", PH_QB, i))
            loop(pe, PH_KB, lambda i: project("k", PH_KB, i))
            loop(pe, PH_VB, lambda i: project("v", PH_VB, i))
            loop(pe, PH_QA, lambda i: project("qa", PH_QA, i))
            for k in range(4):
                chunk_products(PH_KVA, 0, k, 4 * k, XH, XL, 0, k == 0, k == 3, free_wait(PH_KVA, 0), None, 4, 2)
            for m in range(2):
                pe.wait_ge(ft_ready, 44 + m + 1)
                if m == 0:
                    pe.wait_ge(tok_ready, 36)
                b = bank[4 + m]
                f = KAF[:, :] if m == 0 else FT[:, 0, :]
                turn(b[:, 0:P], f[:, 0:P])
                turn(b[:, P:2 * P], f[:, P:2 * P])
                turn(b[0:NS, 256:384], f[:, SEQ:T]).then_inc(ft_turned, 1)

            def scores(u):
                for n, kind, h, g in UNITS[u]:
                    if n >= 3:
                        pe.wait_ge(s_read, n - 2)
                    q = slice(64 * (h % 2), 64 * (h % 2) + 64)
                    if kind == "a":
                        qt, kt = QA[q, h // 2, :], KD[q, h // 8, :]
                    else:
                        qt, kt = QB[q, 4 * g + h // 2, :], KB[q, 4 * g + h // 2, :]
                    b = bank[n % 3]
                    mm(b[:, 0:128], qt[:, 0:128], kt[:, 0:128], True, True)
                    mm(b[:, 128:384], qt[:, 128:256], kt[:, 0:256], True, True).then_inc(s_ready, 1)

            def turns(u, n, j):
                pe.wait_ge(p_ready, 2 * u + 2)
                if n >= 2:
                    pe.wait_ge(pt_ready, n - 1)
                b, s = bank[3 + n % 2], SPS[u % 4][:, j, :]
                turn(b[:, 0:128], s[:, 0:128])
                turn(b[:, 128:256], s[:, 128:256])
                turn(b[:, 256:384], s[:, 256:384]).then_inc(t_ready, 1)

            def values(u, n, kind, h, g, first, last):
                pe.wait_ge(pt_ready, n + 1)
                pair = u // 2
                if first and u % 2 == 0 and pair >= 2:
                    pe.wait_ge(o_read, pair - 1)
                q = slice(64 * (h % 2), 64 * (h % 2) + 64)
                o = bank[5 + pair % 2]
                if kind == "a":
                    v = [VAT[:, blk, 64 * (h // 8):64 * (h // 8) + 64] for blk in range(2)]
                else:
                    v = [VTOK[:, blk, g, 64 * h:64 * h + 64] for blk in range(2)]
                mm(o[q, 0:256], v[0], PT[:, n % 3, 0:256], first, False, skip_group_check=True)
                ins = mm(o[q, 128:256], v[1], PT[:, n % 3, 256:384], False, last, skip_group_check=True)
                ins.then_inc(pt_used, 1)
                return ins

            pe.wait_ge(kd_in, 64)
            pe.wait_ge(tok_ready, 38)
            pe.wait_ge(ft_copied, 32)
            scores(0)
            scores(1)
            todo = None
            for u in range(len(UNITS)):
                if u + 2 < len(UNITS):
                    scores(u + 2)
                for j, (n, kind, h, g) in enumerate(UNITS[u]):
                    turns(u, n, j)
                    if todo:
                        values(*todo)
                    todo = (u, n, kind, h, g, j == 0, j == len(UNITS[u]) - 1)
            values(*todo)

            pe.wait_ge(samp_in, 64)
            pe.wait_ge(relt_done, 20)
            pe.wait_ge(o_read, 12)
            for g in range(BG):
                mm(bank[6][:, g * P:g * P + P], RELT[:, g, :], OHB[:, g * P:g * P + P], True, True)
                mm(bank[6][:, 3 * P + NS * g:3 * P + NS * g + NS], RELT[:, g, :],
                   OHB[:, 3 * P + NS * g:3 * P + NS * g + NS], True, True)
            for kv in range(2):
                ins = mm(bank[7][:, kv * NKEY_A:kv * NKEY_A + NKEY_A], RELT[:, 3 + kv, :], OHA[:, :], True, True)
            ins.then_inc(rowbias_pe, 1)
            def cached_keys(b):
                pe.wait_ge(ck_in[b % 2], 32 * (b // 2 + 1))
                if b == 1:
                    pe.wait_ge(rowbias_done, 2)
                if b >= 2:
                    pe.wait_ge(kts_ready, b - 1)
                b0 = 4 + 2 * (b % 2)
                for pr in range(4):
                    turn(bank[b0][:, pr * P:pr * P + P], C1[:, b % 2, pr * P:pr * P + P])
                for kv in range(2):
                    ins = turn(bank[b0 + 1][0:64, kv * P:kv * P + P], CA[:, b % 2, 64 * kv:64 * kv + 64])
                ins.then_inc(kts_pe, 1)

            def cached_logits(b):
                pe.wait_ge(kts_ready, b + 1)
                r, bb, kt = slice(32 * (b % 4), 32 * (b % 4) + 32), b // 4, KTS[b % 2]
                for pr in range(4):
                    mm(bank[bb][r, 0:P], QBD[:, 0, pr, b, :], kt[:, 0, pr * P:pr * P + P], pr == 0, pr == 3)
                for kv in range(2):
                    qs = QAS[:, kv, b].rearrange("p g t -> p (g t)")
                    ins = mm(bank[2 + bb][r, kv * NKEY_A:kv * NKEY_A + P], qs, kt[0:64, 1, kv * P:kv * P + P], True, True)
                ins.then_inc(kts_used, 1)

            cached_keys(0)
            pe.wait_ge(qbd_done, 8)
            pe.wait_ge(qas_own, 4)
            for b in range(DB):
                if b + 1 < DB:
                    cached_keys(b + 1)
                cached_logits(b)
            pe.wait_ge(qbd_done, 24)
            pe.wait_ge(unit_done, 32)
            for bb in range(2):
                for g in (1, 2):
                    turn(bank[bb][:, g * P:g * P + P], ST[:, g - 1, P * bb:P * bb + P])
                for g in range(BG):
                    for pr in range(4):
                        mm(bank[bb][:, 3 * P + NS * g:3 * P + NS * g + NS],
                           QBD[:, g, pr, 4 * bb:4 * bb + 4, :].rearrange("p b r -> p (b r)"),
                           KB[:, 4 * g + pr, SEQ:T], pr == 0, pr == 3)
                for kv in range(2):
                    qs = QAS[:, kv, 4 * bb:4 * bb + 4].rearrange("p b g t -> p (b g t)")
                    ins = mm(bank[2 + bb][:, kv * NKEY_A + P:(kv + 1) * NKEY_A], qs, KD[0:64, kv, SEQ:T], True, True)
            ins.then_inc(rows_ready, 1)
            pe.wait_ge(rows_p, 6)
            for bb in range(2):
                for g in range(BG):
                    turn(bank[4 + bb][:, g * P:g * P + P], SRB[:, bb, g * P:g * P + P])
                ins = turn(bank[4 + bb][0:96, 384:512], SRB[:, bb, 384:480])
            ins.then_inc(rt_pe, 1)
            for bb in range(2):
                for kv in range(2):
                    n = 2 * bb + kv
                    turn(bank[6][:, n * P:n * P + P], SRA[:, bb, kv, 0:P])
                    ins = turn(bank[7][0:NS, n * P:n * P + P], SRA[:, bb, kv, P:NKEY_A])
            ins.then_inc(rt_pe, 1)
            pe.wait_ge(rt_done, 1)
            pe.wait_ge(vn_in, 32)
            for pr in range(4):
                mm(bank[4][:, 64 * pr:64 * pr + 64].rearrange("p (h b t) -> p h b t", h=2, t=DS),
                   VN[:, P * pr:P * pr + P],
                   PTN[:, :, :].rearrange("p c (b h t) -> p h (c b) t", b=4, t=DS)[:, 2 * pr:2 * pr + 2],
                   pr == 0, False, skip_group_check=True)
            for par in range(2):
                for kv in range(2):
                    mm(bank[5][64 * par:64 * par + 64, 128 * kv:128 * kv + 128]
                       .rearrange("p (g b t) -> p g b t", g=4, t=DS),
                       VNA[:, 64 * kv:64 * kv + 64],
                       PTNA[:, kv].rearrange("p c (b g t) -> p g (c b) t", b=4, t=DS)[:, par:8:2],
                       kv == 0, False, skip_group_check=True)

            def cached_values(b):
                c, bb, b4 = slice(4 * b, 4 * b + 4), b // 4, b % 4
                pe.wait_ge(cv_in[b % 2], 32 * (b // 2 + 1))
                for pr in range(4):
                    mm(bank[4][:, 64 * pr:64 * pr + 64].rearrange("p (h n) -> p h n", h=2)[:, :, c],
                       C1[:, b % 2, P * pr:P * pr + P],
                       PTB[:, 0, bb, 32 * b4 + 8 * pr:32 * b4 + 8 * pr + 8].rearrange("p (h t) -> p h t", t=DS),
                       False, False, skip_group_check=True)
                for par in range(2):
                    for kv in range(2):
                        ins = mm(bank[5][64 * par:64 * par + 64, 128 * kv:128 * kv + 128].rearrange("p (g n) -> p g n", g=4)[:, :, c],
                                 CA[:, b % 2, 64 * kv:64 * kv + 64],
                                 PTA[:, kv, bb, 32 * b4:32 * b4 + 32].rearrange("p (g t) -> p g t", t=DS)[:, par:8:2],
                                 False, b == DB - 1, skip_group_check=True)
                ins.then_inc(cv_used, 1)
                for g in (1, 2):
                    pe.wait_ge(v_in[g - 1], 16 * (b + 1))
                    for t in range(DS):
                        for pr in range(4):
                            ins = mm(bank[4][:, 64 * pr:64 * pr + 64].rearrange("p (h n) -> p h n", h=2)[:, :, 4 * b + t],
                                     VST[:, g - 1, t, P * pr:P * pr + P],
                                     PTB[:, g, bb, 32 * b4 + 8 * pr:32 * b4 + 8 * pr + 8].rearrange("p (h t) -> p h t", t=DS)[:, :, t],
                                     False, b == DB - 1 and g == 2, skip_group_check=True)
                    ins.then_inc(v_used, 1)

            for i in range(8):
                for k in range(8):
                    chunk_products(PH_GATE, i, k, 2 * k, XH, XL, 0, k == 0, k == 7, free_wait(PH_GATE, i))
                cached_values(i)

            pe.wait_ge(otl_done, 3)

            def merge(i):
                for s in range(2):
                    n0 = 8 * i + 4 * s

                    def pb_wait(m):
                        if not known_below(n0 + m, 4):
                            pe.wait_ge(pb_free, n0 + m - 3)

                    for k in range(4):
                        chunk_products(PH_MERGE, i, 6 * s + k, 2 * k, OTH, OTL, 0, k == 0, k == 3, free_wait(PH_MERGE, i, s))
                    for k in range(2):
                        chunk_products(PH_MERGE, i, 6 * s + 4 + k, 8 + 2 * k, OTH, OTL, 4, k == 0, k == 1, pb_wait,
                                       ready=pb_ready)
            for i in range(2):
                merge(i)

            def outp(i):
                for k in range(8):
                    if not isinstance(i, int) or i == 0:
                        pe.wait_ge(ml_done, 2 * k + 2)
                    chunk_products(PH_OUT, i, k, 2 * k, MH, ML, 0, k == 0, k == 7, free_wait(PH_OUT, i))
            loop(pe, PH_OUT, outp)

            def norm(which):
                pe.wait_ge(sum_done, 33 * (which + 1) - 1)
                mm(bank[4][:, 0:T], ones[:, :], SUMS[:, 0, :], True, True).then_inc(sum_pe, 1)
                pe.wait_ge(sum_done, 33 * (which + 1))
                mm(bank[5][:, 0:T], ones[:, :], SUMS[:, 1, :], True, True).then_inc(sum_pe, 1)

            pe.wait_ge(ln_in, 64)
            turn(bank[7][:, 0:64], lnrow[:, :], 64).then_inc(setup_pe, 1)
            norm(0)
            for half in range(2):
                def ffn_in(i, half=half):
                    for k in range(8):
                        if half == 0 and k % 2 == 0:
                            pe.wait_ge(*((x1l_rest, 2 * k) if k else (x1l_done, 4)))
                        chunk_products(PH_F1[half], i, k, 4 * (k // 2), X1H, X1L, 2 * (k % 2), k < 2, k >= 6,
                                       free_wait(PH_F1[half], i, k % 2), None, 4, 2)
                loop(pe, PH_F1[half], ffn_in)
                pe.wait_ge(hl_done, 22 * half + 22)
                for j in range(4):
                    for k in range(11):
                        chunk_products(PH_F2[half], 0, 11 * j + k, 2 * k, HH, HL, 0, k == 0, k == 10, free_wait(PH_F2[half], 0, j))
            norm(1)
            for k in range(KT):
                pe.wait_ge(y_done, KT + k + 1)
                if k >= 2:
                    pe.wait_ge(yt_done, k - 1)
                b = bank[6 + k % 2]
                turn(b[:, 0:P], U[:, k, 0:P])
                turn(b[:, P:2 * P], U[:, k, P:2 * P])
                turn(b[0:NS, 256:384], U[:, k, SEQ:T]).then_inc(yt_pe, 1)


_INS = ["x_prompt", "x_sample", "cache_a", "cache_b1", "cache_b2", "cache_b3", "rel_bias", "w_in", "a_sink",
        "w_oa", "w_ob", "w_out", "ln1_g", "ln1_b", "w_ffn_in", "w_ffn_out", "ln2_g", "ln2_b"]
_CONSTS = ["ohp", "maskp", "ohb", "oha", "maskb", "maska", "ident", "rowsel"]
_OUTS = [(1, 256, 2048), (8, 4, 2048), (1, 1, 128, 2, 2, 64), (1, 1, 128, 2, 8, 64), (1, 1, 256, 2, 8, 64),
         (1, 1, 256, 2, 8, 64), (1, 8, 128, 2, 2, 64), (1, 8, 128, 2, 8, 64), (1, 8, 512, 2, 8, 64),
         (1, 8, 2048, 2, 8, 64)]


def kernel(**inputs):
    import numpy as _np
    import concourse.bacc as _bacc
    from concourse import mybir as _mybir
    from concourse.bass_utils import run_bass_kernel_spmd as _run

    nc = _bacc.Bacc("TRN2", target_bir_lowering=False, num_devices=1)
    arrays, args = {}, []
    consts = constants()
    for name in _INS + _CONSTS:
        a = _np.ascontiguousarray(consts[name] if name in consts else inputs[name])
        arrays[f"in_{name}_dram"] = a
        args.append(nc.dram_tensor(f"in_{name}_dram", a.shape, _mybir.dt.from_np(a.dtype), kind="ExternalInput").ap())
    for i, shape in enumerate(_OUTS):
        args.append(nc.dram_tensor(f"out_{i}_dram", shape, _mybir.dt.float32, kind="ExternalOutput").ap())
    build(nc, *args)
    r = _run(nc, [arrays], core_ids=[0])
    return tuple(r.results[0][f"out_{i}_dram"] for i in range(len(_OUTS)))
```

```python
import math
from contextlib import ExitStack

import numpy as np

import concourse.bass as bass
from concourse import mybir

F32 = mybir.dt.float32
F32R = mybir.dt.float32r
ALU = mybir.AluOpType
ACT = mybir.ActivationFunctionType
AX = mybir.AxisListType.X

P = 128
D = 2048
SEQ = 256
DB, DS = 8, 4
NS = DB * DS
T = SEQ + NS
KT = D // P
DH = 64
QH = 16
BH, BG = 8, 3
DIL = (1, 4, 16)
WIN = (128, 512, 2048)
FF = 5632
FT_HALF = FF // P // 2
NH = QH + BG * BH
BUCKETS = 32
ALPHA = 2.0 ** 0.25
SCALE = DH ** -0.5
EPS = 1e-5
NEG = -1e30
LOW = -3.0e38
C_QA, C_KVA, C_QB, C_GATE = 0, 1024, 1280, 5888
CK = 1024
RING = 4
AHEAD = 3
NKEY_B = 3 * P + 3 * NS
NKEY_A = P + NS


def bucket(dist):
    d = max(int(dist), 0)
    if d < 16:
        return d
    return min(16 + int(math.log(d / 16) / math.log(2048 / 16) * 16), 31)


def constants():
    ohp = np.zeros((BUCKETS, 384), np.float32)
    maskp = np.full((NH, 384), NEG, np.float32)
    for i in range(384):
        dist = 255 - i
        ohp[bucket(dist), i] = 1
        if 0 <= dist < 128:
            maskp[:QH, i] = 0
        for g in range(BG):
            if 0 <= dist <= WIN[g] and dist % DIL[g] == 0:
                maskp[QH + g * BH:QH + (g + 1) * BH, i] = 0
    ohb = np.zeros((P, NKEY_B), np.float32)
    oha = np.zeros((P, NKEY_A), np.float32)
    maskb = np.zeros((P, 2, NKEY_B), np.float32)
    maska = np.zeros((P, 2, 2, NKEY_A), np.float32)
    for t in range(DS):
        for n in range(P):
            ohb[32 * t + bucket(128 + t - n), n] = 1
            ohb[32 * t + bucket(4 * (128 - n)), P + n] = 1
            ohb[32 * t + bucket(16 * (128 - n)), 2 * P + n] = 1
            oha[32 * t + bucket(128 + t - n), n] = 1
        for k in range(NS):
            oha[32 * t + bucket(t - k % DS), P + k] = 1
            for g in range(BG):
                ohb[32 * t + bucket(t - k % DS), 3 * P + NS * g + k] = 1
    for r in range(P):
        b4, t = r // 32, r % DS
        for bb in range(2):
            b = bb * 4 + b4
            for n in range(P):
                if 128 + t - n > 128:
                    maskb[r, bb, n] = NEG
                if 128 + t - n > 127:
                    maska[r, bb, :, n] = NEG
            for k in range(NS):
                kb, kt = k // DS, k % DS
                if kb != b or kt > t:
                    maska[r, bb, :, P + k] = NEG
                    maskb[r, bb, 3 * P + k] = NEG
                if kb != b or kt != t:
                    maskb[r, bb, 3 * P + NS + k] = NEG
                    maskb[r, bb, 3 * P + 2 * NS + k] = NEG
    return {"ohp": ohp, "maskp": maskp, "ohb": ohb, "oha": oha, "maskb": maskb, "maska": maska,
            "ident": np.eye(P, dtype=np.float32),
            "rowsel": (np.arange(P)[None, :] // DS % 8 == np.arange(8)[:, None]).astype(np.float32)}


class Phase:

    def __init__(self, chunk0, tile0, set0, groups, chunks, tiles=4, sets=1):
        self.chunk0, self.tile0, self.set0, self.groups, self.chunks = chunk0, tile0, set0, groups, chunks
        self.tiles, self.sets = tiles, sets

    def after(self, groups, chunks, tiles=4, sets=1):
        return Phase(self.chunk0 + self.groups * self.chunks, self.tile0 + self.groups * self.tiles * self.sets,
                     self.set0 + self.groups * (self.tiles - 1) * self.sets, groups, chunks, tiles, sets)

    def tile_done(self, i, set_, m, last_chunk):
        if m == self.tiles - 1:
            return 1, self.chunk0 + self.chunks * i + last_chunk + 1
        return 0, self.set0 + (self.tiles - 1) * (self.sets * i + set_) + m + 1


PH_QB = Phase(0, 0, 0, 3, 8)
PH_KB = PH_QB.after(3, 8)
PH_VB = PH_KB.after(3, 8)
PH_QA = PH_VB.after(2, 8)
PH_KVA = PH_QA.after(1, 4, 2)
PH_GATE = PH_KVA.after(8, 8)
PH_MERGE = PH_GATE.after(2, 12, 4, 2)
PH_OUT = PH_MERGE.after(4, 8)
PH_F1 = [PH_OUT.after(11, 8, 2, 2), None]
PH_F2 = [PH_F1[0].after(1, 44, 4, 4), None]
PH_F1[1] = PH_F2[0].after(11, 8, 2, 2)
PH_F2[1] = PH_F1[1].after(1, 44, 4, 4)
CHUNKS = PH_F2[1].chunk0 + 44
FREE0 = PH_GATE.tile0

UNITS = [[(BG * h + g, "b", h, g) for g in range(BG)] for h in range(BH)] + \
        [[(BG * BH + h, "a", h, 0)] for h in range(QH)]
TABLE_ROWS = [QH + BH * g + h for h in range(BH) for g in range(BG)] + [h for h in range(QH)]


def build(nc, x_prompt, x_sample, cache_a, cache_b1, cache_b2, cache_b3, rel_bias, w_in, a_sink, w_oa,
          w_ob, w_out, ln1_g, ln1_b, w_ffn_in, w_ffn_out, ln2_g, ln2_b,
          ohp, maskp, ohb, oha, maskb, maska, ident_in, rowsel,
          y_p, y_s, na_p, nb1_p, nb2_p, nb3_p, na_s, nb1_s, nb2_s, nb3_s):
    caches = (cache_b1, cache_b2, cache_b3)
    nb_p, nb_s = (nb1_p, nb2_p, nb3_p), (nb1_s, nb2_s, nb3_s)
    tok_dram = nc.dram_tensor("tok_scratch", [3, BG, NS, 512], F32, kind="Internal").ap()
    toka_dram = nc.dram_tensor("toka_scratch", [2, NS, P], F32, kind="Internal").ap()
    tz_dram = nc.dram_tensor("bias_scratch", [NH, 384], F32, kind="Internal").ap()

    with ExitStack() as ctx:
        base = (nc.sbuf_base + 63) // 64 * 64

        def at(name, shape, offset, dt=F32):
            return nc.alloc_sbuf_tensor_at(name, shape, dt, offset=base + offset)

        TB = T * 4
        raw = [at(f"raw{s}", [P, CK], 4096 * s) for s in range(RING)]
        whi = [at(f"whi{s}", [P, CK], 16384 + 4096 * s, F32R) for s in range(RING)]
        wlo = [at(f"wlo{s}", [P, CK], 32768 + 4096 * s, F32R) for s in range(RING)]
        XH = at("XH", [P, KT, T], 49152, F32R)
        XL = at("XL", [P, KT, T], 67584, F32R)
        R1 = 86016
        xs_p = at("xs_p", [P, 2, D], R1)
        xs_s = at("xs_s", [NS, D], R1 + 16384)
        QB = at("QB", [P, 12, T], R1)
        KB = at("KB", [P, 12, T], R1 + 12 * TB)
        QA = at("QA", [P, 8, T], R1 + 24 * TB)
        KD = at("KD", [P, 2, T], R1 + 32 * TB)
        GT = at("GT", [P, 32, T], R1)
        R5 = 170240
        R2 = 125184
        VTOK = at("VTOK", [P, 2, BG, 512], R2)
        VAT = at("VAT", [P, 2, P], R2 + 12288)
        PTB = at("PTB", [P, BG, 2, P], R2)
        PTN = at("PTN", [96, 2, P], R2 + 3072)
        PTA = at("PTA", [P, 2, 2, P], R2 + 4096)
        PTNA = at("PTNA", [NS, 2, 2, P], R2 + 6144)
        K1 = at("K1", [P, 6, 512], R2)
        K16 = at("K16", [P, 512], R5 + 14336)
        KA = at("KA", [P, DB, P], R5 + 9728)
        C1 = at("C1", [P, 2, 512], R2 + 8192)
        CA = at("CA", [P, 2, P], R2 + 12288)
        R3 = 138496
        KTOK = at("KTOK", [P, 2, BG, 512], R3)
        KAT = at("KAT", [P, 2, P], R5 + 14336)
        BIAS = at("BIAS", [P, 4, 256], R3)
        SPS = [at(f"SP{s}", [P, BG, 384], o) for s, o in enumerate((R3 + 4096, R3 + 8704, R5 + 5120, R5 + 9728))]
        PT = at("PT", [P, 3, 384], R3 + 13312)
        QBD = at("QBD", [P, BG, 4, DB, 32], R3)
        KTS = [at("KTS0", [P, 2, 512], R3 + 12288), at("KTS1", [P, 2, 512], R5 + 5120)]
        R4 = 156416
        OT = at("OT", [P, 12, T], R4)
        TOKS = at("TOKS", [NS, BG, 512], R4)
        TOKA = at("TOKA", [NS, 2, P], R4 + 6144)
        FT = at("FT", [P, 4, T], R4 + 7168)
        KAF = at("KAF", [P, T], R4 + 7168 + 4 * TB)
        KST = at("KST", [P, 2, 2, 512], R5)
        QST = at("QST", [P, 2, 2, 512], R5 + 8192)
        PROD = at("PROD", [P, 1024], R5 + 16384)
        OHP = at("OHP", [BUCKETS, 384], R5)
        TZ = at("TZ", [NH, 384], R5 + 1536)
        VST = at("VST", [P, 2, DS, 512], R5)
        OHB = at("OHB", [P, NKEY_B], R5)
        OHA = at("OHA", [P, NKEY_A], R5 + 1920)
        RELT = at("RELT", [P, 5, P], R5 + 2560)
        BIB = at("BIB", [P, 2, NKEY_B], R5 + 16384)
        ST = at("ST", [P, 2, 256], 190720)
        VN = at("VN", [96, 512], 192768)
        VNA = at("VNA", [NS, P], 194816)
        QAS = at("QAS", [64, 2, DB, 8, DS], 195328)
        SRB = at("SRB", [P, 2, NKEY_B], 197376)
        SRA = at("SRA", [P, 2, 2, NKEY_A], 201216)
        BIA = at("BIA", [P, 2, 2, NKEY_A], 203776)
        PV = at("PV", [P, DS, 512], 195328)
        ONECOL = at("ONECOL", [P, 2 * NS - 1], 203776)
        OROW = at("OROW", [NS, 512], 204288)
        OTH = at("OTH", [P, 12, T], R3, F32R)
        OTL = at("OTL", [P, 12, T], R4, F32R)
        MT = at("MT", [P, 8, T], R2)
        MH = at("MH", [P, KT, T], R5, F32R)
        ML = at("ML", [P, KT, T], R5 + 18432, F32R)
        U = at("U", [P, KT, T], R1)
        SUMS = at("SUMS", [P, 2, T], R1 + 18432)
        MU = at("MU", [P, T], R1 + 20736)
        RS = at("RS", [P, T], R1 + 21888)
        VAR = at("VAR", [P, T], R1 + 23040)
        SQ = at("SQ", [P, 4, T], R1 + 24192)
        X1H = at("X1H", [P, KT, T], 49152, F32R)
        X1L = at("X1L", [P, KT, T], 67584, F32R)
        HH = at("HH", [P, FT_HALF, T], R2, F32R)
        HL = at("HL", [P, FT_HALF, T], R2 + 25344, F32R)
        SG = at("SG", [P, 2, T], R2 + 50688)
        HT = at("HT", [P, 2, T], R2 + 52992)
        HF = at("HF", [P, 2, T], R2 + 55296)
        YT = at("YT", [P, 2, D], R2)
        YTS = at("YTS", [NS, D], R2 + 16384)
        R6 = 208704
        ident = at("ident", [P, P], R6)
        ones = at("ones", [P, P], R6 + 512)
        LNP = at("LNP", [P, 4, KT], R6 + 1024)
        REL4 = at("REL4", [P, NH], R6 + 1280)
        SINKB = at("SINKB", [P, QH], R6 + 1440)
        SINKR = at("SINKR", [P, 2], R6 + 1504)
        NM = at("NM", [P, 4, 2], R6 + 1536)
        MX = at("MX", [P, 4, 2, BG], R6 + 2976)
        LS = at("LS", [P, 4, 2], R6 + 1632)
        ES = at("ES", [P, 4, 2], R6 + 1664)
        RL = at("RL", [P, 4, 2], R6 + 1696)
        SMX = at("SMX", [P, 6], R6 + 1728)
        SNM = at("SNM", [P, 6], R6 + 1760)
        SLS = at("SLS", [P, 6], R6 + 1792)
        SES = at("SES", [P, 6], R6 + 1824)
        SRL = at("SRL", [P, 6], R6 + 1856)
        WARM = at("WARM", [P, 1], R6 + 1888)
        lnrow = at("lnrow", [64, P], R6 + 1920)
        ROWSEL = at("ROWSEL", [8, P], R6 + 2432)
        QLO = at("QLO", [64, 8, NS], R6 + 3072)
        SINK2 = at("SINK2", [8, 2], R6 + 2944)

        bank = [ctx.enter_context(nc.psum_tensor(f"bank{i}", [P, 512], F32)) for i in range(8)]

        def sem(name):
            return ctx.enter_context(nc.semaphore(name))

        x_in = [sem(f"x_in{q}") for q in range(4)]; const_in = sem("const_in"); ln_in = sem("ln_in")
        raw_in = [sem(f"raw_in{s}") for s in range(RING)]
        hi_done, lo_done, chunk_used = sem("hi_done"), sem("lo_done"), sem("chunk_used")
        tile_ready, tile_free = sem("tile_ready"), sem("tile_free")
        pb_ready, pb_free = sem("pb_ready"), sem("pb_free")
        xt_ready, xh_done, xl_done = sem("xt_ready"), sem("xh_done"), sem("xl_done")
        setup_pe, setup_dve = sem("setup_pe"), sem("setup_dve")
        tz_out = sem("tz_out")
        ft_ready, ft_turned, ft_copied, tok_ready = sem("ft_ready"), sem("ft_turned"), sem("ft_copied"), sem("tok_ready")
        tok_out = sem("tok_out"); toka_out = sem("toka_out"); kv_out = sem("kv_out")
        new_out = sem("new_out"); copy_out = sem("copy_out")
        unit_in = [sem("unit_in0"), sem("unit_in1")]
        unit_done = sem("unit_done"); prod_done = sem("prod_done")
        kd_in = sem("kd_in"); qas_in = sem("qas_in"); qas_own = sem("qas_own")
        bias_in = [sem(f"bias_in{i}") for i in range(4)]
        s_ready, s_read, m_ready, nm_ready, e_ready, p_ready = (
            sem("s_ready"), sem("s_read"), sem("m_ready"), sem("nm_ready"), sem("e_ready"), sem("p_ready"))
        t_ready, pt_ready, pt_used, o_read = sem("t_ready"), sem("pt_ready"), sem("pt_used"), sem("o_read")
        chain = sem("chain")
        relt_zero, relt_done, qbd_zero, qbd_done = sem("relt_zero"), sem("relt_done"), sem("qbd_zero"), sem("qbd_done")
        samp_in = sem("samp_in"); vn_in = sem("vn_in")
        rowbias_pe, rowbias_done = sem("rowbias_pe"), sem("rowbias_done")
        ck_in = [sem(f"ck_in{i}") for i in range(4)]
        kts_pe = sem("kts_pe"); kts_ready = sem("kts_ready"); kts_used = sem("kts_used")
        rows_ready, rows_m, rows_e, rows_p = sem("rows_ready"), sem("rows_m"), sem("rows_e"), sem("rows_p")
        rt_pe, rt_done = sem("rt_pe"), sem("rt_done")
        v_in = [sem("v_in0"), sem("v_in1")]
        vp_done, pv_ready, pv_used, orow_done, os_ready = (
            sem("vp_done"), sem("pv_ready"), sem("pv_used"), sem("orow_done"), sem("os_ready"))
        cv_in = [sem("cv_in0"), sem("cv_in1")]; cv_used = sem("cv_used")
        os_read = sem("os_read"); onecol_done = sem("onecol_done")
        oth_done, otl_done = sem("oth_done"), sem("otl_done")
        mix_done, mh_done, ml_done = sem("mix_done"), sem("mh_done"), sem("ml_done")
        ax_done, sq_done, sum_done, sum_pe, mu_done, cen_done, cen_rest, var_done, sd_done, nrm_done, y_done, x1h_done, x1l_done, x1l_rest = (
            sem("ax_done"), sem("sq_done"), sem("sum_done"), sem("sum_pe"), sem("mu_done"), sem("cen_done"), sem("cen_rest"), sem("var_done"),
            sem("sd_done"), sem("nrm_done"), sem("y_done"), sem("x1h_done"), sem("x1l_done"), sem("x1l_rest"))
        b_added = sem("b_added")
        sg_done, hh_done, hl_done = sem("sg_done"), sem("hh_done"), sem("hl_done")
        yt_pe, yt_even, yt_odd, y_out = sem("yt_pe"), sem("yt_even"), sem("yt_odd"), sem("y_out")

        block = ctx.enter_context(nc.Block())

        def loop(eng, ph, body):
            start = 0
            if ph.chunk0 == 0:
                body(0)
                start = 1
            if ph.groups - start == 1:
                body(start)
            else:
                with eng.Fori(start, ph.groups) as i:
                    body(i)

        def u_made(eng, which, n):
            eng.wait_ge(tile_free, (PH_OUT, PH_F2[1])[which].tile0 - FREE0 + n + 1)

        def known_below(value, limit):
            return isinstance(value, int) and value < limit

        @block.sync
        def _(sp):
            def x_piece(q):
                c = slice(512 * q, 512 * q + 512)
                sp.dma_start(xs_p[:, :, c], x_prompt[0].rearrange("(n p) d -> p n d", p=P)[:, :, c]).then_inc(x_in[q], 16)
                sp.dma_start(xs_s[:, c], x_sample.rearrange("b t d -> (b t) d")[:, c]).then_inc(x_in[q], 16)

            sp.dma_start(ident[:, :], ident_in).then_inc(x_in[0], 16)
            x_piece(0)

            def chunk(ph, i, k, src, shape=None):
                c = ph.chunk0 + ph.chunks * i + k
                if not known_below(c, RING):
                    sp.wait_ge(lo_done, c - RING + 1)
                dst = raw[k % RING][:, :]
                if shape:
                    dst = dst.rearrange(*shape[0], **shape[1])
                sp.dma_start(dst, src).then_inc(raw_in[k % RING], 16)

            def rows(w):
                return w.rearrange("(k p) e -> p k e", p=P)

            two = (("p (k e) -> p k e",), {"k": 2})
            four = (("p (k e) -> p k e",), {"k": 4})
            win = rows(w_in[0])
            for ph, col in ((PH_QB, C_QB), (PH_KB, C_QB + 1536), (PH_VB, C_QB + 3072), (PH_QA, C_QA)):
                def body(i, ph=ph, col=col):
                    for k in range(8):
                        if known_below(ph.chunk0 + ph.chunks * i, 1) and k in (1, 2, 3):
                            x_piece(k)
                        chunk(ph, i, k, win[:, 2 * k:2 * k + 2, bass.ds(col + 512 * i, 512)], two)
                loop(sp, ph, body)
            for k in range(4):
                chunk(PH_KVA, 0, k, win[:, 4 * k:4 * k + 4, C_KVA:C_KVA + 256], four)
                if k == 0:
                    sp.dma_start(lnrow[0:16, :], ln1_g[0].rearrange("(k p) -> k p", p=P)).then_inc(ln_in, 16)
                    sp.dma_start(lnrow[16:32, :], ln1_b[0].rearrange("(k p) -> k p", p=P)).then_inc(ln_in, 16)
                    sp.dma_start(lnrow[32:48, :], ln2_g[0].rearrange("(k p) -> k p", p=P)).then_inc(ln_in, 16)
                    sp.dma_start(lnrow[48:64, :], ln2_b[0].rearrange("(k p) -> k p", p=P)).then_inc(ln_in, 16)

            def gates(i):
                for k in range(8):
                    chunk(PH_GATE, i, k, win[:, 2 * k:2 * k + 2, bass.ds(C_GATE + 512 * i, 512)], two)
            loop(sp, PH_GATE, gates)

            def merge(i):
                for s in range(2):
                    cols = bass.ds(1024 * i + 512 * s, 512)
                    for k in range(4):
                        chunk(PH_MERGE, i, 6 * s + k, rows(w_oa[0])[:, 2 * k:2 * k + 2, cols], two)
                    for k in range(2):
                        chunk(PH_MERGE, i, 6 * s + 4 + k, rows(w_ob[0])[:, 2 * k:2 * k + 2, cols], two)
            loop(sp, PH_MERGE, merge)

            def outp(i):
                for k in range(8):
                    chunk(PH_OUT, i, k, rows(w_out[0])[:, 2 * k:2 * k + 2, bass.ds(512 * i, 512)], two)
            loop(sp, PH_OUT, outp)
            f1 = w_ffn_in[0].rearrange("(k p) (u e) -> p k u e", p=P, u=2)
            f2 = rows(w_ffn_out[0])
            for half in range(2):
                def ffn_in(i, half=half):
                    for k in range(8):
                        chunk(PH_F1[half], i, k,
                              f1[:, 4 * (k // 2):4 * (k // 2) + 4, k % 2, bass.ds(FT_HALF * P * half + 256 * i, 256)], four)
                loop(sp, PH_F1[half], ffn_in)
                for j in range(4):
                    for k in range(11):
                        k0 = FT_HALF * half + 2 * k
                        chunk(PH_F2[half], 0, 11 * j + k, f2[:, k0:k0 + 2, 512 * j:512 * j + 512], two)
            for q in range(4):
                c = slice(512 * q, 512 * q + 512)
                sp.wait_ge(yt_even, 2 * q + 2)
                sp.wait_ge(yt_odd, 2 * q + 2)
                sp.dma_start(y_p[0].rearrange("(n p) d -> p n d", p=P)[:, :, c], YT[:, :, c]).then_inc(y_out, 16)
                sp.dma_start(y_s.rearrange("b t d -> (b t) d")[:, c], YTS[:, c]).then_inc(y_out, 16)
            sp.wait_ge(y_out, 128)

        @block.gpsimd
        def _(pool):
            for t in range(DS):
                pool.dma_start(REL4[32 * t:32 * t + 32, :], rel_bias).then_inc(const_in, 16)
            pool.dma_start(OHP[:, :], ohp).then_inc(const_in, 16)
            pool.dma_start(TZ[:, :], maskp).then_inc(const_in, 16)
            pool.dma_start(SINKB[:, :], bass.AP(a_sink.tensor, 0, [[0, P], [1, QH]])).then_inc(const_in, 16)
            pool.dma_start(ROWSEL[:, :], rowsel).then_inc(const_in, 16)
            for kv in range(2):
                pool.dma_start(SINK2[:, kv:kv + 1], bass.AP(a_sink.tensor, 8 * kv, [[1, 8], [1, 1]])).then_inc(const_in, 16)
            pool.wait_ge(setup_dve, 1)
            pool.dma_start(tz_dram, TZ[:, :]).then_inc(tz_out, 16)
            pool.wait_ge(tz_out, 16)

            def token_rows(kind, g):
                pool.dma_start(tok_dram[kind, g], TOKS[:, g, :]).then_inc(tok_out, 16)
                pool.wait_ge(tok_out, 16 * (3 * kind + g + 1))
                if kind:
                    w = WIN[g]
                    pool.dma_start(nb_s[g][0, :, w - 4:w, kind - 1].rearrange("b t h d -> b t (h d)"),
                                   tok_dram[kind, g].rearrange("(b t) f -> b t f", b=DB)).then_inc(new_out, 16)

            def unit_load(b, j):
                g, t0 = 1 + j // 2, 2 * (j % 2)
                if not known_below(4 * b + j, 2):
                    pool.wait_ge(unit_done, 4 * b + j - 1)
                keys = caches[g][0].rearrange("b (n r) k h d -> b n r k (h d)", r=DIL[g])
                pool.dma_start(KST[:, j % 2], keys[b, :, t0:t0 + 2, 0, :]).then_inc(unit_in[j % 2], 16)
                q = tok_dram[0, g, 4 * b + t0:4 * b + t0 + 2, :].rearrange("t f -> (t f)")
                pool.dma_start(QST[:, j % 2].rearrange("p t f -> p (t f)"), q.partition_broadcast(P)
                               ).then_inc(unit_in[j % 2], 16)

            for g in range(BG):
                pool.wait_ge(tok_ready, 4 * (g + 1))
                token_rows(0, g)
            unit_load(0, 0)
            unit_load(0, 1)
            for b in range(8):
                unit_load(b, 2)
                unit_load(b, 3)
                if b < 7:
                    unit_load(b + 1, 0)
                    unit_load(b + 1, 1)
                if b < 6:
                    pool.wait_ge(tok_ready, 4 * (b + 4))
                    token_rows(1 + b // 3, b % 3)
                if b == 2 or b == 5:
                    kv, src = (0, KTOK) if b == 2 else (1, VTOK)
                    pool.dma_start(nb1_p[0, 0, :, kv].rearrange("p h d -> p (h d)"), src[:, 1, 0, :]).then_inc(kv_out, 16)
                    for g in (1, 2):
                        pool.dma_start(nb_p[g][0, 0, :, kv].rearrange("(n p) h d -> p n (h d)", p=P),
                                       src[:, :, g, :]).then_inc(kv_out, 16)
            pool.dma_start(VN[:, :], tok_dram[2].rearrange("g n f -> (g n) f")).then_inc(vn_in, 16)
            pool.wait_ge(ft_copied, 32)
            pool.dma_start(QLO[:, :, :], QA[64:128, :, SEQ:T]).then_inc(qas_in, 16)
            def bias_tile(n):
                row = TABLE_ROWS[n]
                if n >= 4:
                    pool.wait_ge(s_read, n - 3)
                pool.dma_start(BIAS[:, n % 4, :], bass.AP(tz_dram.tensor, row * 384, [[1, P], [1, 256]])
                               ).then_inc(bias_in[n % 4], 16)

            pool.wait_ge(kv_out, 16 * 6)
            for n in range(6):
                bias_tile(n)
            pool.wait_ge(ft_ready, 45)
            pool.dma_start(KD[0:64, 1, :], KAF[64:128, :]).then_inc(kd_in, 16)
            pool.dma_start(KD[64:128, 0, :], KAF[0:64, :]).then_inc(kd_in, 16)
            pool.dma_start(KD[0:64, 0, :], KAF[0:64, :]).then_inc(kd_in, 16)
            pool.dma_start(KD[64:128, 1, :], KAF[64:128, :]).then_inc(kd_in, 16)
            for n in range(6, 9):
                bias_tile(n)
            pool.wait_ge(tok_ready, 38)
            for kv, src in ((0, KAT), (1, VAT)):
                pool.dma_start(toka_dram[kv], TOKA[:, kv, :]).then_inc(toka_out, 16)
                pool.dma_start(na_p[0, 0, :, kv].rearrange("p h d -> p (h d)"), src[:, 1, :]).then_inc(kv_out, 16)
            for n in range(9, 16):
                bias_tile(n)
            pool.wait_ge(toka_out, 32)
            for kv in range(2):
                pool.dma_start(na_s[0, :, 124:128, kv].rearrange("b t h d -> b t (h d)"),
                               toka_dram[kv].rearrange("(b t) f -> b t f", b=DB)).then_inc(new_out, 16)
            pool.dma_start(VNA[:, :], toka_dram[1]).then_inc(vn_in, 16)
            for n in range(16, NH):
                bias_tile(n)
            pool.wait_ge(unit_done, 32)
            pool.dma_start(OHB[:, :], ohb).then_inc(samp_in, 16)
            pool.dma_start(OHA[:, :], oha).then_inc(samp_in, 16)
            pool.dma_start(BIB[:, :, :], maskb).then_inc(samp_in, 16)
            pool.dma_start(BIA[:, :, :, :], maska).then_inc(samp_in, 16)
            nc.gpsimd.memset(RELT[:, :, :], 0.0).then_inc(relt_zero, 1)
            pool.wait_ge(relt_zero, 1)
            for s, h0 in enumerate((QH, QH + BH, QH + 2 * BH, 0, BH)):
                for t in range(DS):
                    q = slice(32 * t, 32 * t + 32)
                    dst = RELT[q, s, :].rearrange("p (b h t) -> p b h t", b=4, t=DS)[:, :, :, t]
                    nc.gpsimd.tensor_copy(dst, REL4[q, h0:h0 + 8].unsqueeze(1).broadcast_to([32, 4, 8])
                                          ).then_inc(relt_done, 1)
            pool.wait_ge(relt_done, 20)
            pool.wait_ge(s_read, 40)
            pool.wait_ge(t_ready, UNITS[21][-1][0] + 1)
            for g in range(BG):
                if g:
                    pool.wait_ge(qbd_done, 8 * g)
                nc.gpsimd.memset(QBD[:, g], 0.0).then_inc(qbd_zero, 1)
                pool.wait_ge(qbd_zero, g + 1)
                for pr in range(4):
                    for hf in range(2):
                        q = slice(64 * hf, 64 * hf + 64)
                        h = 2 * pr + hf
                        nc.gpsimd.tensor_copy(QBD[q, g, pr, :, 4 * h:4 * h + 4],
                                              QB[q, 4 * g + pr, SEQ:T].rearrange("p (b t) -> p b t", t=DS)
                                              ).then_inc(qbd_done, 1)
            for b in range(DB):
                if b == 0:
                    pool.wait_ge(rowbias_done, 2)
                    pool.wait_ge(kts_used, 8)
                for g in (1, 2):
                    if b >= 1:
                        pool.wait_ge(pv_ready, b)
                    pool.dma_start(VST[:, g - 1], caches[g][0, b].rearrange("(n r) k h d -> n r k (h d)", r=DIL[g])[:, 0:4, 1, :]
                                   ).then_inc(v_in[g - 1], 16)
                if b >= 2:
                    pool.wait_ge(cv_used, b - 1)
                pool.dma_start(C1[:, b % 2, :], cache_b1[0, b, :, 1].rearrange("p h d -> p (h d)")).then_inc(cv_in[b % 2], 16)
                pool.dma_start(CA[:, b % 2, :], cache_a[0, b, :, 1].rearrange("p h d -> p (h d)")).then_inc(cv_in[b % 2], 16)

            def centre_rest(which):
                pool.wait_ge(mu_done, 2 * which + 1)
                for n in (2, 3):
                    v = U[:, 4 * n:4 * n + 4, :]
                    nc.gpsimd.tensor_tensor(v, v, MU[:, :].unsqueeze(1).broadcast_to([P, 4, T]), ALU.subtract)\
                        .then_inc(cen_rest, 1)

            centre_rest(0)
            for k in range(8, KT):
                pool.wait_ge(x1h_done, k + 1)
                nc.gpsimd.tensor_scalar(U[:, k, :], U[:, k, :], LNP[:, 1, k:k + 1], None, ALU.add).then_inc(b_added, 1)
                pool.wait_ge(b_added, k - 7)
                nc.gpsimd.tensor_tensor(X1L[:, k, :], U[:, k, :], X1H[:, k, :].bitcast(F32), ALU.subtract)\
                    .then_inc(x1l_rest, 1)
            centre_rest(1)
            pool.wait_ge(copy_out, 16 * (1 + 2 + 32 + 28))
            pool.wait_ge(kv_out, 16 * 8)
            pool.wait_ge(new_out, 16 * 8)

        @block.scalar
        def _(act):
            def shift(new, old, first, n, pieces):
                row = old.shape[2] * old.shape[3] * old.shape[4]
                src = old.rearrange("b r k h d -> b (r k h d)")[:, bass.ds(first + DS * row, n)]
                dst = new.rearrange("b r k h d -> b (r k h d)")[:, bass.ds(first, n)]
                act.dma_start(dst.rearrange("b (x y) -> x b y", x=pieces),
                               src.rearrange("b (x y) -> x b y", x=pieces)).then_inc(copy_out, 16)

            def copy_b2(n):
                b = slice(n // 4, n // 4 + 1)
                shift(nb2_s[0, b], cache_b2[0, b], n % 4 * (127 * 1024), 127 * 1024, 16)

            def copy_b1(i):
                b = bass.ds(4 * i, 4)
                shift(nb1_s[0, b], cache_b1[0, b], 0, 124 * 1024, 16)

            def copy_b3(n):
                shift(nb3_s[0], cache_b3[0], n * (73 * 1024), 73 * 1024, 16)

            def split(ph, i, k):
                c = ph.chunk0 + ph.chunks * i + k + AHEAD
                if isinstance(c, int) and c >= CHUNKS:
                    return
                s = (k + AHEAD) % RING
                act.wait_ge(raw_in[s], 16 * (ph.chunk0 // RING + ph.chunks // RING * i + (k + AHEAD) // RING + 1))
                if not known_below(c, RING):
                    act.wait_ge(chunk_used, c - RING + 1)
                nc.scalar.activation(whi[s][:, :], raw[s][:, :], ACT.Copy).then_inc(hi_done, 1)

            for k in range(KT):
                act.wait_ge(xt_ready, k + 1)
                nc.scalar.activation(XH[:, k, :], bank[4 + k % 4][:, 0:T], ACT.Copy).then_inc(xh_done, 1)
                if k < 12 and k % 4 == 3:
                    c = k // 4
                    act.wait_ge(raw_in[c], 16)
                    nc.scalar.activation(whi[c][:, :], raw[c][:, :], ACT.Copy).then_inc(hi_done, 1)

            def tile(ph, i, m):
                which, value = ph.tile_done(i, 0, m, ph.chunks - 1)
                act.wait_ge((tile_ready, chunk_used)[which], value)
                return bank[m]

            def project(kind, ph, i):
                n0 = ph.tile0 + 4 * i

                def evacuate(m):
                    src = tile(ph, i, m)
                    if not known_below(n0 + m, 4):
                        act.wait_ge(ft_turned, 36 if kind == "qa" else n0 + m - 3)
                        act.wait_ge(ft_copied, {"q": n0 + m - 3, "k": n0 + m - 3, "v": 24, "qa": 4 * i + m + 21}[kind])
                    nc.scalar.activation(FT[:, m, :], src[:, 0:T], ACT.Copy,
                                         scale=SCALE if kind in ("q", "qa") else 1.0)\
                        .then_inc(ft_ready, 1)

                def token_rows(m):
                    act.wait_ge(ft_turned, n0 + m + 1)
                    b = bank[4 + m]
                    if kind in ("k", "v"):
                        dst = (KTOK if kind == "k" else VTOK)[:, :, bass.ds(i, 1), m * P:m * P + P]
                        nc.scalar.activation(dst.rearrange("p n g f -> p (n g) f"),
                                             b[:, 0:256].rearrange("p (n f) -> p n f", n=2), ACT.Copy)
                    nc.scalar.activation(TOKS[:, bass.ds(i, 1), m * P:m * P + P].rearrange("p g f -> p (g f)"),
                                         b[0:NS, 256:384], ACT.Copy).then_inc(tok_ready, 1)

                for k in range(8):
                    split(ph, i, k)
                evacuate(0)
                for m in range(1, 4):
                    evacuate(m)
                    if kind != "qa":
                        token_rows(m - 1)
                if kind != "qa":
                    token_rows(3)

            loop(act, PH_QB, lambda i: project("q", PH_QB, i))
            act.wait_ge(tok_out, 16 * 3)
            loop(act, PH_KB, lambda i: project("k", PH_KB, i))
            act.wait_ge(tok_out, 16 * 6)
            loop(act, PH_VB, lambda i: project("v", PH_VB, i))
            loop(act, PH_QA, lambda i: project("qa", PH_QA, i))
            def keys_a():
                tile(PH_KVA, 0, 0)
                nc.scalar.activation(KAF[:, :], bank[6][:, 0:T], ACT.Copy).then_inc(ft_ready, 1)
                tile(PH_KVA, 0, 1)
                act.wait_ge(ft_copied, 29)
                nc.scalar.activation(FT[:, 0, :], bank[7][:, 0:T], ACT.Copy).then_inc(ft_ready, 1)
                act.wait_ge(unit_done, 32)
                for m in range(2):
                    act.wait_ge(ft_turned, 36 + m + 1)
                    nc.scalar.activation((KAT, VAT)[m][:, :, :], bank[4 + m][:, 0:256].rearrange("p (n f) -> p n f", n=2), ACT.Copy)
                    nc.scalar.activation(TOKA[:, m, :], bank[4 + m][0:NS, 256:384], ACT.Copy).then_inc(tok_ready, 1)

            def exponentials(u):
                blocks, s = UNITS[u], u % 4
                act.wait_ge(nm_ready, u + 1)
                for qb in range(2):
                    cols = slice(0, 128) if qb == 0 else slice(128, 384)
                    v = SPS[s][:, 0:len(blocks), cols]
                    nc.scalar.activation(v, v, ACT.Exp, bias=NM[:, s, qb:qb + 1], accum_out=LS[:, s, qb:qb + 1])\
                        .then_inc(e_ready, 1)
                if len(blocks) == 1:
                    h = blocks[0][2]
                    nc.scalar.activation(ES[:, s, :], NM[:, s, :], ACT.Exp, bias=SINKB[:, h:h + 1]).then_inc(e_ready, 1)

            def turned(n):
                act.wait_ge(t_ready, n + 1)
                if n >= 3:
                    act.wait_ge(pt_used, n - 2)
                nc.scalar.activation(PT[:, n % 3, :], bank[3 + n % 2][:, 0:384], ACT.Copy).then_inc(pt_ready, 1)

            split(PH_KVA, 0, 0)
            exponentials(0)
            split(PH_KVA, 0, 1)
            split(PH_KVA, 0, 2)
            exponentials(1)
            split(PH_KVA, 0, 3)
            keys_a()
            for u in range(len(UNITS)):
                for n, *_ in UNITS[u]:
                    turned(n)
                if u + 2 < len(UNITS):
                    exponentials(u + 2)
                copy_b2(u)

            def load_keys(dst, b0, b1, done):
                act.dma_start(dst, cache_b1[0, b0:b1, :, 0].rearrange("b p h d -> p b (h d)")).then_inc(done, 16)

            act.wait_ge(pt_used, 40)
            load_keys(K1[:, 0:2, :], 0, 2, ck_in[0])
            act.dma_start(KA[:, :, :], cache_a[0, :, :, 0].rearrange("b p h d -> p b (h d)")).then_inc(ck_in[0], 16)
            load_keys(K1[:, 2:6, :], 2, 6, ck_in[1])
            act.wait_ge(kv_out, 16 * 8)
            load_keys(K16[:, :].unsqueeze(1), 6, 7, ck_in[2])

            for b in range(DB):
                if b >= 2:
                    copy_b2(22 + b)
                act.wait_ge(kts_pe, b + 1)
                if b == 0:
                    load_keys(K1[:, 0:1, :], 7, 8, ck_in[3])
                if b >= 2:
                    act.wait_ge(kts_used, b - 1)
                kt, b0 = KTS[b % 2], 4 + 2 * (b % 2)
                nc.scalar.activation(kt[:, 0, :], bank[b0][:, 0:512], ACT.Copy)
                nc.scalar.activation(kt[0:64, 1, 0:256], bank[b0 + 1][0:64, 0:256], ACT.Copy).then_inc(kts_ready, 1)
            for r in range(2):
                act.wait_ge(rows_m, r + 1)
                nc.scalar.activation(SRB[:, r, :], SRB[:, r, :], ACT.Exp, bias=SNM[:, r:r + 1],
                                     accum_out=SLS[:, r:r + 1]).then_inc(rows_e, 1)
            copy_b2(30)
            copy_b2(31)
            act.wait_ge(rows_m, 6)
            for r in range(2, 6):
                v = SRA[:, (r - 2) // 2, r % 2, :]
                nc.scalar.activation(v, v, ACT.Exp, bias=SNM[:, r:r + 1], accum_out=SLS[:, r:r + 1]).then_inc(rows_e, 1)
                nc.scalar.activation(SES[:, r:r + 1], SNM[:, r:r + 1], ACT.Exp,
                                     bias=SINKR[:, r % 2:r % 2 + 1]).then_inc(rows_e, 1)

            def rows_turned():
                act.wait_ge(rt_pe, 1)
                nc.scalar.activation(PTB[:, :, 0, :], bank[0][:, 0:384].rearrange("p (g r) -> p g r", g=3), ACT.Copy)
                nc.scalar.activation(PTB[:, :, 1, :], bank[1][:, 0:384].rearrange("p (g r) -> p g r", g=3), ACT.Copy)
                nc.scalar.activation(PTN[:, 0, :], bank[0][0:96, 384:512], ACT.Copy)
                nc.scalar.activation(PTN[:, 1, :], bank[1][0:96, 384:512], ACT.Copy)
                act.wait_ge(rt_pe, 2)
                nc.scalar.activation(PTA[:, :, :, :], bank[2][:, :].rearrange("p (b k r) -> p k b r", b=2, k=2), ACT.Copy)
                nc.scalar.activation(PTNA[:, :, :, :], bank[3][0:NS, :].rearrange("p (b k r) -> p k b r", b=2, k=2),
                                     ACT.Copy).then_inc(rt_done, 1)
                for n in range(3):
                    v = slice(4 * n, 4 * n + 4)
                    nc.scalar.activation(OTH[:, v, 0:SEQ], OT[:, v, 0:SEQ], ACT.Copy).then_inc(oth_done, 1)

            def gates(i):
                copy_b3(i)
                first = known_below(i, 1)
                for k in range(8):
                    split(PH_GATE, i, k)
                    if first and k == 4:
                        rows_turned()
                for m in range(4):
                    src = tile(PH_GATE, i, m)
                    if first:
                        src = bank[4 + m]
                    nc.scalar.activation(GT[:, bass.ds(4 * i + m, 1), :].rearrange("p n t -> p (n t)"), src[:, 0:T],
                                         ACT.Sigmoid).then_inc(tile_free, 1)
            gates(0)
            with act.Fori(1, 8) as i:
                gates(i)

            act.wait_ge(os_read, 1)
            nc.scalar.activation(OTH[:, :, SEQ:T], OT[:, :, SEQ:T], ACT.Copy).then_inc(oth_done, 1)

            shift(na_s[0], cache_a[0], 0, 124 * 256, 16)

            def merge(i):
                copy_b1(i)
                for k in range(12):
                    split(PH_MERGE, i, k)
                    if k % 6 == 5:
                        s = k // 6
                        for m in range(4):
                            n = 8 * i + 4 * s + m
                            act.wait_ge(mix_done, n + 1)
                            nc.scalar.activation(MH[:, bass.ds(n, 1), :].rearrange("p n t -> p (n t)"), MT[:, m, :],
                                                 ACT.Copy).then_inc(mh_done, 1)
            loop(act, PH_MERGE, merge)

            def squares(which, n0):
                for m in range(4):
                    u_made(act, which, n0 + m)
                    nc.scalar.activation(SQ[:, m, :], U[:, bass.ds(n0 + m, 1), :].rearrange("p n t -> p (n t)"), ACT.Square)\
                        .then_inc(sq_done, 1)

            def outp(i):
                copy_b3(8 + i)
                for k in range(8):
                    split(PH_OUT, i, k)
                squares(0, 4 * i)
            loop(act, PH_OUT, outp)

            def norm(which):
                nc.scalar.activation(WARM[:, :], ones[:, 0:1], ACT.Sqrt)
                act.wait_ge(sum_pe, 2 * which + 1)
                nc.scalar.activation(MU[:, :], bank[4][:, 0:T], ACT.Copy).then_inc(mu_done, 1)
                nc.scalar.activation(RS[:, :], bank[4][:, 0:T], ACT.Square).then_inc(mu_done, 1)
                act.wait_ge(var_done, 2 * which + 1)
                nc.scalar.activation(VAR[:, :], VAR[:, :], ACT.Sqrt).then_inc(sd_done, 1)
                for k in range(KT):
                    act.wait_ge(nrm_done, KT * which + k + 1)
                    if which == 0:
                        nc.scalar.activation(X1H[:, k, :], U[:, k, :], ACT.Identity, bias=LNP[:, 1, k:k + 1])\
                            .then_inc(x1h_done, 1)
                    else:
                        add_b(which, k)
                        if k >= 5 and k % 2:
                            y_turned(k - 5)

            def y_turned(k):
                act.wait_ge(yt_pe, k + 1)
                b = bank[k % 8]
                nc.scalar.activation(YT[:, :, k * P:k * P + P], b[:, 0:256].rearrange("p (n f) -> p n f", n=2), ACT.Copy)
                nc.scalar.activation(YTS[:, k * P:k * P + P], b[0:NS, 256:384], ACT.Copy).then_inc(yt_even, 1)

            def add_b(which, k):
                nc.scalar.activation(U[:, k, :], U[:, k, :], ACT.Identity, bias=LNP[:, 2 * which + 1, k:k + 1])\
                    .then_inc(y_done, 1)

            norm(0)
            for half in range(2):
                def ffn_in(i, half=half):
                    ph = PH_F1[half]
                    if half == 0:
                        copy_b3(12 + i)
                    for k in range(8):
                        split(ph, i, k)
                    n = 22 * half + 2 * i
                    for j in range(2):
                        which, value = ph.tile_done(i, 0, j, 6)
                        act.wait_ge((tile_ready, chunk_used)[which], value)
                        src = bank[j]
                        nc.scalar.activation(SG[:, j, :], src[:, 0:T], ACT.Sigmoid).then_inc(sg_done, 1)
                    for j in range(2):
                        act.wait_ge(tile_free, ph.tile0 - FREE0 + 4 * i + 2 + j + 1)
                        nc.scalar.activation(HH[:, bass.ds(2 * i + j, 1), :].rearrange("p n t -> p (n t)"), HF[:, j, :],
                                             ACT.Copy).then_inc(hh_done, 1)
                loop(act, PH_F1[half], ffn_in)
                for k in range(44):
                    if half == 0 and k % 11 == 5:
                        copy_b3(23 + k // 11)
                    if half == 1 and k == 5:
                        copy_b3(27)
                    split(PH_F2[half], 0, k)
                    if half == 0 and k < 8:
                        act.wait_ge(x1l_done, k + 1)
                        add_b(0, k)
                    if half == 1 and k % 11 == 10:
                        squares(1, 4 * (k // 11))
            norm(1)
            for k in range(KT - 4, KT, 2):
                y_turned(k)

        @block.vector
        def _(dve):
            count = [0]

            def link(ins):
                count[0] += 1
                ins.then_inc(chain, 1)
                dve.wait_ge(chain, count[0])

            def split(ph, i, k):
                c = ph.chunk0 + ph.chunks * i + k + AHEAD
                if isinstance(c, int) and c >= CHUNKS:
                    return
                s = (k + AHEAD) % RING
                dve.wait_ge(hi_done, c + 1)
                nc.vector.tensor_tensor(wlo[s][:, :], raw[s][:, :], whi[s][:, :].bitcast(F32), ALU.subtract).then_inc(lo_done, 1)

            link(nc.vector.memset(ones[:, :], 1.0 / D))
            for k in range(KT):
                dve.wait_ge(xh_done, k + 1)
                nc.vector.tensor_tensor(XL[:, k, :], bank[4 + k % 4][:, 0:T], XH[:, k, :].bitcast(F32),
                                        ALU.subtract).then_inc(xl_done, 1)
                if k < 12 and k % 4 == 3:
                    c = k // 4
                    dve.wait_ge(hi_done, c + 1)
                    nc.vector.tensor_tensor(wlo[c][:, :], raw[c][:, :], whi[c][:, :].bitcast(F32), ALU.subtract).then_inc(lo_done, 1)
            def head_bias():
                dve.wait_ge(setup_pe, 1)
                dve.wait_ge(const_in, 16 * 10)
                nc.vector.tensor_tensor(TZ[:, :], bank[4][0:NH, 0:384], TZ[:, :], ALU.add).then_inc(setup_dve, 1)
                nc.vector.tensor_copy(SINKR[:, :], bank[4][:, 400:402]).then_inc(setup_dve, 1)

            def unit(b, j):
                n = 4 * b + j
                g, t0 = 1 + j // 2, 2 * (j % 2)
                dve.wait_ge(unit_in[j % 2], 64 * b + 32 * (j // 2) + 32)
                if not known_below(n, 1):
                    dve.wait_ge(unit_done, n)
                nc.vector.tensor_tensor(PROD[:, :], KST[:, j % 2].rearrange("p t f -> p (t f)"),
                                        QST[:, j % 2].rearrange("p t f -> p (t f)"), ALU.mult).then_inc(prod_done, 1)
                dve.wait_ge(prod_done, n + 1)
                dst = ST[:, g - 1, bass.ds(32 * b, 32)].rearrange("p (h t) -> p t h", t=DS)[:, t0:t0 + 2, :]
                nc.vector.tensor_reduce(dst, PROD[:, :].rearrange("p (t h d) -> p t h d", t=2, h=BH),
                                        AX, ALU.add).then_inc(unit_done, 1)

            def project(kind, ph, i):
                n0 = ph.tile0 + 4 * i
                b = None if kind == "q" else i + {"k": 0, "v": 3, "qa": 6}[kind]
                for k in range(8):
                    split(ph, i, k)
                    if b is not None and k % 2 == 1:
                        unit(b, k // 2)
                if kind != "v":
                    dst = {"q": QB, "k": KB, "qa": QA}[kind]
                    for m in range(4):
                        dve.wait_ge(ft_ready, n0 + m + 1)
                        d = dst[:, bass.ds(4 * i + m, 1), :].rearrange("p n t -> p (n t)")
                        if kind == "k":
                            nc.vector.tensor_copy(d, FT[:, m, :]).then_inc(ft_copied, 1)
                        else:
                            nc.vector.tensor_copy(d[:, 0:SEQ].rearrange("p (n c) -> p n c", n=2),
                                                  FT[:, m, 0:SEQ].rearrange("p (n c) -> p n c", n=2)[:, :, ::-1])
                            nc.vector.tensor_copy(d[:, SEQ:T], FT[:, m, SEQ:T]).then_inc(ft_copied, 1)
                if known_below(n0, 1):
                    head_bias()

            loop(dve, PH_QB, lambda i: project("q", PH_QB, i))
            project("k", PH_KB, 0)
            with dve.Fori(1, 3) as i:
                project("k", PH_KB, i)
            loop(dve, PH_VB, lambda i: project("v", PH_VB, i))
            loop(dve, PH_QA, lambda i: project("qa", PH_QA, i))
            def logits(u):
                blocks, s = UNITS[u], u % 4
                if u >= 4:
                    dve.wait_ge(t_ready, UNITS[u - 4][-1][0] + 1)
                if u == 0:
                    dve.wait_ge(kv_out, 16 * 6)
                if u == 2:
                    dve.wait_ge(unit_done, 32)
                for j, (n, *_) in enumerate(blocks):
                    dve.wait_ge(s_ready, n + 1)
                    dve.wait_ge(bias_in[n % 4], 16 * (n // 4 + 1))
                    b = bank[n % 3]
                    nc.vector.tensor_tensor_reduce(SPS[s][:, j, 0:128], b[:, 0:128], BIAS[:, n % 4, 128:256], 1.0, LOW,
                                                   ALU.add, ALU.max, MX[:, s, 0, j:j + 1]).then_inc(m_ready, 1)
                    nc.vector.tensor_tensor_reduce(SPS[s][:, j, 128:384], b[:, 128:384], BIAS[:, n % 4, :], 1.0, LOW,
                                                   ALU.add, ALU.max, MX[:, s, 1, j:j + 1]).then_inc(s_read, 1)
                dve.wait_ge(m_ready, blocks[-1][0] + 1)
                dve.wait_ge(s_read, blocks[-1][0] + 1)
                if len(blocks) == 1:
                    h = blocks[0][2]
                    nc.vector.tensor_scalar(NM[:, s, :], MX[:, s, :, 0], SINKB[:, h:h + 1], -1.0, ALU.max, ALU.mult)\
                        .then_inc(nm_ready, 1)
                else:
                    nc.vector.tensor_reduce(NM[:, s, :], MX[:, s, :, :], AX, ALU.max, negate=True).then_inc(nm_ready, 1)

            def normalise(u):
                blocks, s = UNITS[u], u % 4
                dve.wait_ge(e_ready, 2 * (u + 1) if u < BH else 2 * BH + 3 * (u - BH + 1))
                if len(blocks) == 1:
                    link(nc.vector.tensor_tensor(LS[:, s, :], LS[:, s, :], ES[:, s, :], ALU.add))
                link(nc.vector.reciprocal(RL[:, s, :], LS[:, s, :]))
                for qb in range(2):
                    cols = slice(0, 128) if qb == 0 else slice(128, 384)
                    v = SPS[s][:, 0:len(blocks), cols]
                    nc.vector.tensor_scalar(v, v, RL[:, s, qb:qb + 1], None, ALU.mult).then_inc(p_ready, 1)

            def output(pair):
                dve.wait_ge(pt_used, UNITS[2 * pair + 1][-1][0] + 1)
                tile = 8 + pair if pair < BH // 2 else pair - BH // 2
                nc.vector.tensor_copy(OT[:, tile, 0:SEQ].rearrange("p (n c) -> p n c", n=2),
                                      bank[5 + pair % 2][:, 0:SEQ].rearrange("p (n c) -> p n c", n=2)[:, :, ::-1])\
                    .then_inc(o_read, 1)

            dve.wait_ge(const_in, 16 * 10)
            split(PH_KVA, 0, 0)
            logits(0)
            split(PH_KVA, 0, 1)
            split(PH_KVA, 0, 2)
            logits(1)
            split(PH_KVA, 0, 3)
            for u in range(len(UNITS)):
                normalise(u)
                if u + 2 < len(UNITS):
                    logits(u + 2)
                if u % 2 == 0 and u:
                    if u == 2:
                        dve.wait_ge(toka_out, 32)
                        dve.wait_ge(tok_out, 16 * 9)
                        dve.wait_ge(kd_in, 64)
                    output(u // 2 - 1)
            output(len(UNITS) // 2 - 1)
            dve.wait_ge(ft_copied, 32)
            for par in range(2):
                if par:
                    dve.wait_ge(qas_in, 16)
                src = QLO[:, :, :] if par else QA[0:64, :, SEQ:T]
                for kv in range(2):
                    nc.vector.tensor_copy(QAS[:, kv, :, par:8:2, :].rearrange("p b g t -> p g b t"),
                                          src[:, 4 * kv:4 * kv + 4, :].rearrange("p g (b t) -> p g b t", t=DS)).then_inc(qas_own, 1)

            dve.wait_ge(samp_in, 64)
            dve.wait_ge(rowbias_pe, 1)
            for bb in range(2):
                ins = nc.vector.tensor_tensor(BIB[:, bb, :], bank[6][:, 0:NKEY_B], BIB[:, bb, :], ALU.add)
                if bb == 1:
                    ins.then_inc(rowbias_done, 1)
            for bb in range(2):
                ins = nc.vector.tensor_tensor(BIA[:, bb, :, :], bank[7][:, 0:2 * NKEY_A].rearrange("p (k n) -> p k n", k=2),
                                              BIA[:, bb, :, :], ALU.add)
                if bb == 1:
                    ins.then_inc(rowbias_done, 1)
            dve.wait_ge(rowbias_done, 2)
            for bb in range(2):
                dve.wait_ge(rows_ready, 1)
                link(nc.vector.tensor_tensor_reduce(SRB[:, bb, :], bank[bb][:, 0:NKEY_B], BIB[:, bb, :], 1.0, LOW,
                                                    ALU.add, ALU.max, SMX[:, bb:bb + 1]))
                nc.vector.tensor_scalar(SNM[:, bb:bb + 1], SMX[:, bb:bb + 1], -1.0, None, ALU.mult).then_inc(rows_m, 1)
            for r in range(2, 6):
                bb, kv = (r - 2) // 2, r % 2
                link(nc.vector.tensor_tensor_reduce(SRA[:, bb, kv, :], bank[2 + bb][:, kv * NKEY_A:kv * NKEY_A + NKEY_A],
                                                    BIA[:, bb, kv, :], 1.0, LOW, ALU.add, ALU.max, SMX[:, r:r + 1]))
                nc.vector.tensor_scalar(SNM[:, r:r + 1], SMX[:, r:r + 1], SINKR[:, kv:kv + 1], -1.0, ALU.max, ALU.mult)\
                    .then_inc(rows_m, 1)
            dve.wait_ge(rows_e, 10)
            link(nc.vector.tensor_tensor(SLS[:, 2:6], SLS[:, 2:6], SES[:, 2:6], ALU.add))
            link(nc.vector.reciprocal(SRL[:, :], SLS[:, :]))
            for r in range(6):
                v = SRB[:, r, :] if r < 2 else SRA[:, (r - 2) // 2, r % 2, :]
                nc.vector.tensor_scalar(v, v, SRL[:, r:r + 1], None, ALU.mult).then_inc(rows_p, 1)

            def outputs_low():
                for n in range(3):
                    v = slice(4 * n, 4 * n + 4)
                    dve.wait_ge(oth_done, n + 1)
                    nc.vector.tensor_tensor(OTL[:, v, 0:SEQ], OT[:, v, 0:SEQ], OTH[:, v, 0:SEQ].bitcast(F32), ALU.subtract)\
                        .then_inc(otl_done, 1)
                nc.vector.memset(ONECOL[:, :], 0.0).then_inc(onecol_done, 1)
                dve.wait_ge(onecol_done, 1)
                nc.vector.memset(ONECOL[:, NS - 1:NS], 1.0).then_inc(onecol_done, 1)

            def value_products(b, loads, par, step):
                def p(g):
                    return PTB[:, g].rearrange("p c r -> p (c r)")[:, bass.ds(32 * b, 32)]\
                        .rearrange("p (h t) -> p t h", t=DS).unsqueeze(3).broadcast_to([P, DS, BH, DH])

                def heads(v):
                    return v.rearrange("p t (h d) -> p t h d", h=BH)

                if step < 2:
                    dve.wait_ge(v_in[step], 16 * b + 16)
                    nc.vector.tensor_tensor(heads(VST[:, step]), heads(VST[:, step]), p(1 + step), ALU.mult).then_inc(vp_done, 1)
                elif step == 2:
                    dve.wait_ge(vp_done, 4 * b + 2)
                    nc.vector.tensor_tensor(VST[:, 0], VST[:, 0], VST[:, 1], ALU.add).then_inc(vp_done, 1)
                elif step == 3:
                    dve.wait_ge(cv_in[par], 32 * loads)
                    if not known_below(b, 1):
                        dve.wait_ge(pv_used, b)
                    v = C1[:, par].rearrange("p (h d) -> p h d", h=BH).unsqueeze(1).broadcast_to([P, DS, BH, DH])
                    nc.vector.tensor_tensor(heads(PV[:, :, :]), v, p(0), ALU.mult).then_inc(vp_done, 1)
                else:
                    dve.wait_ge(vp_done, 4 * b + 4)
                    nc.vector.tensor_tensor(PV[:, :, :], PV[:, :, :], VST[:, 0], ALU.add).then_inc(pv_ready, 1)

            for k in range(8):
                split(PH_GATE, 0, k)
                if k == 4:
                    outputs_low()
                    dve.wait_ge(rt_done, 1)
                for step in ((), (), (), (), (), (0,), (1, 2), (3, 4))[k]:
                    value_products(0, 1, 0, step)

            def gates(b, loads, par):
                for k in range(8):
                    split(PH_GATE, b, k)
                    if 2 <= k < 7:
                        value_products(b, loads, par, k - 2)
            with dve.Fori(0, 3) as j:
                gates(2 * j + 1, j + 1, 1)
                gates(2 * j + 2, j + 2, 0)
            gates(7, 4, 1)
            dve.wait_ge(pv_used, DB)
            nc.vector.tensor_copy(OROW[:, :], bank[6][0:NS, :]).then_inc(orow_done, 1)
            dve.wait_ge(os_ready, 1)
            for hf in range(2):
                q = slice(64 * hf, 64 * hf + 64)
                nc.vector.tensor_copy(OT[q, 8:12, SEQ:T], bank[4][q, 0:256].rearrange("p (r h n) -> p r h n", r=4, h=2)[:, :, hf, :])
                ins = nc.vector.tensor_copy(OT[q, 0:8, SEQ:T], bank[5][q, 0:256].rearrange("p (r n) -> p r n", r=8))
            ins.then_inc(os_read, 1)
            dve.wait_ge(oth_done, 4)
            nc.vector.tensor_tensor(OTL[:, :, SEQ:T], OT[:, :, SEQ:T], OTH[:, :, SEQ:T].bitcast(F32), ALU.subtract)\
                .then_inc(otl_done, 1)

            def one(buf, n):
                return buf[:, bass.ds(n, 1), :].rearrange("p n t -> p (n t)")

            def merge(i):
                for k in range(12):
                    split(PH_MERGE, i, k)
                    s = k // 6
                    for m in range(4):
                        n = 8 * i + 4 * s + m
                        if k % 6 == 3:
                            which, value = PH_MERGE.tile_done(i, s, m, 6 * s + 3)
                            dve.wait_ge((tile_ready, chunk_used)[which], value)
                            nc.vector.tensor_tensor(MT[:, m, :], bank[m][:, 0:T], one(GT, n), ALU.mult).then_inc(tile_free, 1)
                        if k % 6 == 5:
                            if m < 3:
                                dve.wait_ge(pb_ready, 6 * i + 3 * s + m + 1)
                            else:
                                dve.wait_ge(chunk_used, PH_MERGE.chunk0 + 12 * i + 6 * s + 6)
                            nc.vector.tensor_tensor(MT[:, 4 + m, :], bank[4 + m][:, 0:T], one(GT, n + 16), ALU.mult)\
                                .then_inc(pb_free, 1)
                    if k % 6 == 5:
                        for m in range(4):
                            n = 8 * i + 4 * s + m
                            dve.wait_ge(pb_free, n + 1)
                            nc.vector.tensor_tensor(MT[:, m, :], MT[:, m, :], MT[:, 4 + m, :], ALU.add).then_inc(mix_done, 1)
                        for m in range(4):
                            n = 8 * i + 4 * s + m
                            dve.wait_ge(mh_done, n + 1)
                            nc.vector.tensor_tensor(one(ML, n), MT[:, m, :], one(MH, n).bitcast(F32), ALU.subtract).then_inc(ml_done, 1)
            loop(dve, PH_MERGE, merge)

            def sums(which, n, m):
                u_made(dve, which, n)
                dve.wait_ge(sum_done, 33 * which + 2 * n + 1)
                nc.vector.tensor_tensor(SUMS[:, 0, :], SUMS[:, 0, :], one(U, n), ALU.add).then_inc(sum_done, 1)
                dve.wait_ge(sq_done, KT * which + n + 1)
                nc.vector.tensor_tensor(SUMS[:, 1, :], SUMS[:, 1, :], SQ[:, m, :], ALU.add).then_inc(sum_done, 1)

            nc.vector.memset(SUMS[:, :, :], 0.0).then_inc(sum_done, 1)

            def outp(i):
                for k in range(8):
                    split(PH_OUT, i, k)
                    m = k // 2
                    n = 4 * i + m
                    if k % 2 == 0:
                        nc.vector.tensor_scalar(one(U, n), one(XH, n).bitcast(F32), ALPHA, None, ALU.mult).then_inc(ax_done, 1)
                    else:
                        dve.wait_ge(ax_done, 2 * n + 1)
                        nc.vector.scalar_tensor_tensor(out=one(U, n), in0=one(XL, n).bitcast(F32), scalar=ALPHA,
                                                       in1=one(U, n), op0=ALU.mult, op1=ALU.add).then_inc(ax_done, 1)
                for m in range(4):
                    n = 4 * i + m
                    which, value = PH_OUT.tile_done(i, 0, m, 7)
                    dve.wait_ge((tile_ready, chunk_used)[which], value)
                    dve.wait_ge(ax_done, 2 * n + 2)
                    nc.vector.tensor_tensor(one(U, n), bank[m][:, 0:T], one(U, n), ALU.add).then_inc(tile_free, 1)
                    if m:
                        sums(0, n - 1, m - 1)
                sums(0, 4 * i + 3, 3)
            loop(dve, PH_OUT, outp)

            def norm(which):
                dve.wait_ge(mu_done, 2 * which + 1)
                v = [U[:, 4 * n:4 * n + 4, :] for n in range(4)]

                def centre(n):
                    nc.vector.tensor_tensor(v[n], v[n], MU[:, :].unsqueeze(1).broadcast_to([P, 4, T]), ALU.subtract)\
                        .then_inc(cen_done, 1)

                def scale(n):
                    if n < 2:
                        dve.wait_ge(cen_done, 2 * which + n + 1)
                    else:
                        dve.wait_ge(cen_rest, 2 * which + n - 1)
                    for k in range(4 * n, 4 * n + 4):
                        nc.vector.scalar_tensor_tensor(out=U[:, k, :], in0=U[:, k, :], scalar=LNP[:, 2 * which, k:k + 1],
                                                       in1=RS[:, :], op0=ALU.mult, op1=ALU.mult).then_inc(nrm_done, 1)

                def low(n):
                    for k in range(4 * n, 4 * n + 4):
                        dve.wait_ge(x1h_done, k + 1)
                        nc.vector.scalar_tensor_tensor(out=X1L[:, k, :], in0=U[:, k, :], scalar=LNP[:, 1, k:k + 1],
                                                       in1=X1H[:, k, :].bitcast(F32), op0=ALU.add, op1=ALU.subtract)\
                            .then_inc(x1l_done, 1)

                dve.wait_ge(mu_done, 2 * which + 2)
                dve.wait_ge(sum_pe, 2 * which + 2)
                link(nc.vector.tensor_tensor(VAR[:, :], bank[5][:, 0:T], RS[:, :], ALU.subtract))
                nc.vector.tensor_scalar(VAR[:, :], VAR[:, :], 0.0, EPS, ALU.max, ALU.add).then_inc(var_done, 1)
                centre(0)
                dve.wait_ge(sd_done, which + 1)
                nc.vector.reciprocal(RS[:, :], VAR[:, :]).then_inc(var_done, 1)
                dve.wait_ge(var_done, 2 * which + 2)
                scale(0)
                if which == 0:
                    low(0)
                centre(1)
                scale(1)
                if which == 0:
                    low(1)
                scale(2)
                scale(3)
                if which == 1:
                    for k in range(1, KT, 2):
                        dve.wait_ge(yt_pe, k + 1)
                        b = bank[k % 8]
                        nc.vector.tensor_copy(YT[:, :, k * P:k * P + P], b[:, 0:256].rearrange("p (n f) -> p n f", n=2))
                        nc.vector.tensor_copy(YTS[:, k * P:k * P + P], b[0:NS, 256:384]).then_inc(yt_odd, 1)

            dve.wait_ge(setup_pe, 2)
            link(nc.vector.tensor_copy(LNP[:, :, :], bank[7][:, 0:64].rearrange("p (a k) -> p a k", a=4)))
            norm(0)
            for half in range(2):
                def ffn_in(i, half=half):
                    ph = PH_F1[half]
                    for k in range(8):
                        split(ph, i, k)
                    n = 22 * half + 2 * i
                    t0 = ph.tile0 + 4 * i
                    for j in range(2):
                        dve.wait_ge(sg_done, n + j + 1)
                        nc.vector.tensor_tensor(HT[:, j, :], bank[j][:, 0:T], SG[:, j, :], ALU.mult).then_inc(tile_free, 1)
                    for j in range(2):
                        dve.wait_ge(tile_free, t0 - FREE0 + j + 1)
                        which, value = ph.tile_done(i, 1, j, 7)
                        dve.wait_ge((tile_ready, chunk_used)[which], value)
                        nc.vector.tensor_tensor(HF[:, j, :], bank[2 + j][:, 0:T], HT[:, j, :], ALU.mult).then_inc(tile_free, 1)
                    for j in range(2):
                        dve.wait_ge(hh_done, n + j + 1)
                        nc.vector.tensor_tensor(one(HL, 2 * i + j), HF[:, j, :], one(HH, 2 * i + j).bitcast(F32),
                                                ALU.subtract).then_inc(hl_done, 1)
                loop(dve, PH_F1[half], ffn_in)
                if half == 1:
                    nc.vector.memset(SUMS[:, :, :], 0.0).then_inc(sum_done, 1)
                for k in range(44):
                    split(PH_F2[half], 0, k)
                    if k % 11 == 10:
                        j = k // 11
                        for m in range(4):
                            n = 4 * j + m
                            which, value = PH_F2[half].tile_done(0, j, m, k)
                            dve.wait_ge((tile_ready, chunk_used)[which], value)
                            if half == 0 and m == 0:
                                dve.wait_ge(*((y_done, n + 4) if n < 8 else (x1l_rest, n - 4)))
                            nc.vector.scalar_tensor_tensor(out=U[:, n, :], in0=U[:, n, :], scalar=ALPHA if half == 0 else 1.0,
                                                           in1=bank[m][:, 0:T], op0=ALU.mult, op1=ALU.add).then_inc(tile_free, 1)
                            if half == 1:
                                if m:
                                    sums(1, n - 1, m - 1)
                                if m == 3:
                                    sums(1, n, m)
            norm(1)

        @block.tensor
        def _(pe):
            def mm(out, lhsT, rhs, start, stop, **kw):
                return nc.tensor.matmul(out, lhsT, rhs, start=start, stop=stop, **kw)

            def turn(out, in_, n=P):
                return nc.tensor.transpose(out, in_, ident[0:n, 0:n])

            def chunk_products(ph, i, k, k0, hi, lo, banks, first, last, free_wait=None, after=None, kk=2, m_n=4, ready=None):
                c = ph.chunk0 + ph.chunks * i + k
                s = k % RING
                pe.wait_ge(lo_done, c + 1)
                w = CK // kk
                for m in range(m_n):
                    if first and free_wait:
                        free_wait(m)
                    for q in range(kk):
                        a = whi[s][:, q * w + m * P:q * w + m * P + P]
                        b = wlo[s][:, q * w + m * P:q * w + m * P + P]
                        out = bank[banks + m][:, 0:T]
                        st, sp_ = first and q == 0, last and q == kk - 1
                        mm(out, a, hi[:, k0 + q, :], st, False)
                        mm(out, a, lo[:, k0 + q, :], False, False)
                        ins = mm(out, b, hi[:, k0 + q, :], False, sp_)
                    if last and m < m_n - 1:
                        ins.then_inc(ready or tile_ready, 1)
                    if last and after and m:
                        after(m - 1)
                ins.then_inc(chunk_used, 1)
                if last and after:
                    after(m_n - 1)

            def x_turn(k):
                if k % 4 == 0:
                    pe.wait_ge(x_in[k // 4], 32 if k else 48)
                if k >= 4:
                    pe.wait_ge(xl_done, k - 3)
                b = bank[4 + k % 4]
                turn(b[:, 0:P], xs_p[:, 0, k * P:k * P + P])
                turn(b[:, P:2 * P], xs_p[:, 1, k * P:k * P + P])
                turn(b[:, 2 * P:T], xs_s[:, k * P:k * P + P], NS).then_inc(xt_ready, 1)

            def free_wait(ph, i, s=0):
                def wait(m):
                    n = ph.tile0 + ph.tiles * (ph.sets * i + s) + m
                    if ph.chunk0 < PH_GATE.chunk0:
                        if not known_below(n, 4):
                            pe.wait_ge(ft_ready, n - 3)
                    elif not known_below(n, FREE0 + 4):
                        pe.wait_ge(tile_free, n - FREE0 - 3)
                return wait

            def project(kind, ph, i):
                n0 = ph.tile0 + 4 * i

                def rows(m):
                    pe.wait_ge(ft_ready, n0 + m + 1)
                    if not known_below(n0, 4):
                        pe.wait_ge(tok_ready, n0 + m - 3)
                        if kind == "q":
                            pe.wait_ge(setup_dve, 2)
                    b = bank[4 + m]
                    if kind in ("k", "v"):
                        turn(b[:, 0:P], FT[:, m, 0:P])
                        turn(b[:, P:2 * P], FT[:, m, P:2 * P])
                    turn(b[0:NS, 256:384], FT[:, m, SEQ:T]).then_inc(ft_turned, 1)

                for k in range(8):
                    if known_below(n0, 1):
                        for t in (range(8), range(8, 12), range(12, 16), (), (), (), (), ())[k]:
                            x_turn(t)
                        pe.wait_ge(xl_done, 2 * k + 2)
                    chunk_products(ph, i, k, 2 * k, XH, XL, 0, k == 0, k == 7, free_wait(ph, i),
                                   rows if kind != "qa" else None)
                if known_below(n0, 1):
                    pe.wait_ge(const_in, 16 * 10)
                    pe.wait_ge(tok_ready, 1)
                    mm(bank[4][:, 400:402], ROWSEL[:, :], SINK2[:, :], True, True)
                    mm(bank[4][0:NH, 0:384], REL4[0:32, :], OHP[:, :], True, True).then_inc(setup_pe, 1)

            loop(pe, PH_QB, lambda i: project("q", PH_QB, i))
            loop(pe, PH_KB, lambda i: project("k", PH_KB, i))
            loop(pe, PH_VB, lambda i: project("v", PH_VB, i))
            loop(pe, PH_QA, lambda i: project("qa", PH_QA, i))
            def keys_a(k):
                chunk_products(PH_KVA, 0, k, 4 * k, XH, XL, 6, k == 0, k == 3, None, None, 4, 2)
                if k < 3:
                    return
                for m in range(2):
                    pe.wait_ge(ft_ready, 44 + m + 1)
                    b = bank[4 + m]
                    f = KAF[:, :] if m == 0 else FT[:, 0, :]
                    turn(b[:, 0:P], f[:, 0:P])
                    turn(b[:, P:2 * P], f[:, P:2 * P])
                    turn(b[0:NS, 256:384], f[:, SEQ:T]).then_inc(ft_turned, 1)

            def scores(u):
                for n, kind, h, g in UNITS[u]:
                    if n >= 3:
                        pe.wait_ge(s_read, n - 2)
                    q = slice(64 * (h % 2), 64 * (h % 2) + 64)
                    if kind == "a":
                        qt, kt = QA[q, h // 2, :], KD[q, h // 8, :]
                    else:
                        qt, kt = QB[q, 4 * g + h // 2, :], KB[q, 4 * g + h // 2, :]
                    b = bank[n % 3]
                    mm(b[:, 0:128], qt[:, 0:128], kt[:, 0:128], True, True)
                    mm(b[:, 128:384], qt[:, 128:256], kt[:, 0:256], True, True).then_inc(s_ready, 1)

            def turns(u, n, j):
                pe.wait_ge(p_ready, 2 * u + 2)
                if n >= 2:
                    pe.wait_ge(pt_ready, n - 1)
                b, s = bank[3 + n % 2], SPS[u % 4][:, j, :]
                turn(b[:, 0:128], s[:, 0:128])
                turn(b[:, 128:256], s[:, 128:256])
                turn(b[:, 256:384], s[:, 256:384]).then_inc(t_ready, 1)

            def values(u, n, kind, h, g, first, last):
                pe.wait_ge(pt_ready, n + 1)
                pair = u // 2
                if first and u % 2 == 0 and pair >= 2:
                    pe.wait_ge(o_read, pair - 1)
                q = slice(64 * (h % 2), 64 * (h % 2) + 64)
                o = bank[5 + pair % 2]
                if kind == "a":
                    v = [VAT[:, blk, 64 * (h // 8):64 * (h // 8) + 64] for blk in range(2)]
                else:
                    v = [VTOK[:, blk, g, 64 * h:64 * h + 64] for blk in range(2)]
                mm(o[q, 0:256], v[0], PT[:, n % 3, 0:256], first, False, skip_group_check=True)
                ins = mm(o[q, 128:256], v[1], PT[:, n % 3, 256:384], False, last, skip_group_check=True)
                ins.then_inc(pt_used, 1)
                return ins

            pe.wait_ge(tok_ready, 36)
            pe.wait_ge(ft_copied, 24)
            pe.wait_ge(ft_ready, 44)
            scores(0)
            keys_a(0)
            keys_a(1)
            scores(1)
            keys_a(2)
            keys_a(3)
            todo = None
            for u in range(len(UNITS)):
                if u == 0:
                    pe.wait_ge(tok_ready, 38)
                if u + 2 == BH:
                    pe.wait_ge(kd_in, 64)
                    pe.wait_ge(ft_copied, 32)
                if u + 2 < len(UNITS):
                    scores(u + 2)
                for j, (n, kind, h, g) in enumerate(UNITS[u]):
                    turns(u, n, j)
                    if todo:
                        values(*todo)
                    todo = (u, n, kind, h, g, j == 0, j == len(UNITS[u]) - 1)
            values(*todo)

            pe.wait_ge(samp_in, 64)
            pe.wait_ge(relt_done, 20)
            pe.wait_ge(o_read, 12)
            for g in range(BG):
                mm(bank[6][:, g * P:g * P + P], RELT[:, g, :], OHB[:, g * P:g * P + P], True, True)
                mm(bank[6][:, 3 * P + NS * g:3 * P + NS * g + NS], RELT[:, g, :],
                   OHB[:, 3 * P + NS * g:3 * P + NS * g + NS], True, True)
            for kv in range(2):
                ins = mm(bank[7][:, kv * NKEY_A:kv * NKEY_A + NKEY_A], RELT[:, 3 + kv, :], OHA[:, :], True, True)
            ins.then_inc(rowbias_pe, 1)
            def cached_keys(b):
                if b in (0, 2, 6, 7):
                    pe.wait_ge(*{0: (ck_in[0], 32), 2: (ck_in[1], 16), 6: (ck_in[2], 16), 7: (ck_in[3], 16)}[b])
                k1 = K16[:, :] if b == 6 else K1[:, b % 7, :]
                if b == 1:
                    pe.wait_ge(rowbias_done, 2)
                if b >= 2:
                    pe.wait_ge(kts_ready, b - 1)
                b0 = 4 + 2 * (b % 2)
                for pr in range(4):
                    turn(bank[b0][:, pr * P:pr * P + P], k1[:, pr * P:pr * P + P])
                for kv in range(2):
                    ins = turn(bank[b0 + 1][0:64, kv * P:kv * P + P], KA[:, b, 64 * kv:64 * kv + 64])
                ins.then_inc(kts_pe, 1)

            def cached_logits(b):
                pe.wait_ge(kts_ready, b + 1)
                r, bb, kt = slice(32 * (b % 4), 32 * (b % 4) + 32), b // 4, KTS[b % 2]
                for pr in range(4):
                    mm(bank[bb][r, 0:P], QBD[:, 0, pr, b, :], kt[:, 0, pr * P:pr * P + P], pr == 0, pr == 3)
                for kv in range(2):
                    qs = QAS[:, kv, b].rearrange("p g t -> p (g t)")
                    ins = mm(bank[2 + bb][r, kv * NKEY_A:kv * NKEY_A + P], qs, kt[0:64, 1, kv * P:kv * P + P], True, True)
                ins.then_inc(kts_used, 1)

            pe.wait_ge(unit_done, 32)
            pe.wait_ge(qas_own, 4)
            for bb in range(2):
                for g in (1, 2):
                    turn(bank[bb][:, g * P:g * P + P], ST[:, g - 1, P * bb:P * bb + P])
                for kv in range(2):
                    qs = QAS[:, kv, 4 * bb:4 * bb + 4].rearrange("p b g t -> p (b g t)")
                    mm(bank[2 + bb][:, kv * NKEY_A + P:(kv + 1) * NKEY_A], qs, KD[0:64, kv, SEQ:T], True, True)
            cached_keys(0)
            pe.wait_ge(qbd_done, 8)
            for b in range(DB):
                if b + 1 < DB:
                    cached_keys(b + 1)
                cached_logits(b)
            pe.wait_ge(qbd_done, 24)
            for bb in range(2):
                for g in range(BG):
                    for pr in range(4):
                        ins = mm(bank[bb][:, 3 * P + NS * g:3 * P + NS * g + NS],
                                 QBD[:, g, pr, 4 * bb:4 * bb + 4, :].rearrange("p b r -> p (b r)"),
                                 KB[:, 4 * g + pr, SEQ:T], pr == 0, pr == 3)
            ins.then_inc(rows_ready, 1)
            def rows_turn():
                pe.wait_ge(rows_p, 6)
                for bb in range(2):
                    for g in range(BG):
                        turn(bank[bb][:, g * P:g * P + P], SRB[:, bb, g * P:g * P + P])
                    ins = turn(bank[bb][0:96, 384:512], SRB[:, bb, 384:480])
                ins.then_inc(rt_pe, 1)
                for bb in range(2):
                    for kv in range(2):
                        n = 2 * bb + kv
                        turn(bank[2][:, n * P:n * P + P], SRA[:, bb, kv, 0:P])
                        ins = turn(bank[3][0:NS, n * P:n * P + P], SRA[:, bb, kv, P:NKEY_A])
                ins.then_inc(rt_pe, 1)

            def new_values():
                pe.wait_ge(tile_free, 4)
                pe.wait_ge(vn_in, 32)
                pe.wait_ge(onecol_done, 2)
                for pr in range(4):
                    mm(bank[4][:, 64 * pr:64 * pr + 64].rearrange("p (h b t) -> p h b t", h=2, t=DS),
                       VN[:, P * pr:P * pr + P],
                       PTN[:, :, :].rearrange("p c (b h t) -> p h (c b) t", b=4, t=DS)[:, 2 * pr:2 * pr + 2],
                       pr == 0, False, skip_group_check=True)
                for par in range(2):
                    for kv in range(2):
                        mm(bank[5][64 * par:64 * par + 64, 128 * kv:128 * kv + 128]
                           .rearrange("p (g b t) -> p g b t", g=4, t=DS),
                           VNA[:, 64 * kv:64 * kv + 64],
                           PTNA[:, kv].rearrange("p c (b g t) -> p g (c b) t", b=4, t=DS)[:, par:8:2],
                           kv == 0, False, skip_group_check=True)

            def cached_values(b):
                c, bb, b4 = slice(4 * b, 4 * b + 4), b // 4, b % 4
                pe.wait_ge(cv_in[b % 2], 32 * (b // 2 + 1))
                for par in range(2):
                    for kv in range(2):
                        ins = mm(bank[5][64 * par:64 * par + 64, 128 * kv:128 * kv + 128].rearrange("p (g n) -> p g n", g=4)[:, :, c],
                                 CA[:, b % 2, 64 * kv:64 * kv + 64],
                                 PTA[:, kv, bb, 32 * b4:32 * b4 + 32].rearrange("p (g t) -> p g t", t=DS)[:, par:8:2],
                                 False, b == DB - 1, skip_group_check=True)
                ins.then_inc(cv_used, 1)
                pe.wait_ge(pv_ready, b + 1)
                for t in range(DS):
                    row = DS * b + t
                    ins = mm(bank[6][0:NS, :], ONECOL[:, NS - 1 - row:2 * NS - 1 - row], PV[:, t, :],
                             row == 0, row == NS - 1)
                ins.then_inc(pv_used, 1)

            for i in range(8):
                for k in range(8):
                    if i == 1 and k == 0:
                        pe.wait_ge(rt_done, 1)
                    chunk_products(PH_GATE, i, k, 2 * k, XH, XL, 0 if i else 4, k == 0, k == 7,
                                   free_wait(PH_GATE, i) if i else None)
                    if i == 0 and k == 3:
                        rows_turn()
                    if i == 1 and k == 1:
                        new_values()
                    if i and k == 2:
                        cached_values(i - 1)
            cached_values(DB - 1)
            pe.wait_ge(orow_done, 1)
            for pr in range(4):
                ins = mm(bank[4][:, 64 * pr:64 * pr + 64].rearrange("p (h n) -> p h n", h=2),
                         OROW[:, P * pr:P * pr + P], ident[0:NS, 0:NS].unsqueeze(1).broadcast_to([NS, 2, NS]),
                         False, pr == 3, skip_group_check=True)
            ins.then_inc(os_ready, 1)

            pe.wait_ge(otl_done, 4)

            def merge(i):
                for s in range(2):
                    n0 = 8 * i + 4 * s

                    def pb_wait(m):
                        if not known_below(n0 + m, 4):
                            pe.wait_ge(pb_free, n0 + m - 3)

                    for k in range(4):
                        chunk_products(PH_MERGE, i, 6 * s + k, 2 * k, OTH, OTL, 0, k == 0, k == 3, free_wait(PH_MERGE, i, s))
                    for k in range(2):
                        chunk_products(PH_MERGE, i, 6 * s + 4 + k, 8 + 2 * k, OTH, OTL, 4, k == 0, k == 1, pb_wait,
                                       ready=pb_ready)
            for i in range(2):
                merge(i)

            def outp(i):
                for k in range(8):
                    if not isinstance(i, int) or i == 0:
                        pe.wait_ge(ml_done, 2 * k + 2)
                    chunk_products(PH_OUT, i, k, 2 * k, MH, ML, 0, k == 0, k == 7, free_wait(PH_OUT, i))
            loop(pe, PH_OUT, outp)

            def norm(which):
                pe.wait_ge(sum_done, 33 * (which + 1) - 1)
                mm(bank[4][:, 0:T], ones[:, :], SUMS[:, 0, :], True, True).then_inc(sum_pe, 1)
                pe.wait_ge(sum_done, 33 * (which + 1))
                mm(bank[5][:, 0:T], ones[:, :], SUMS[:, 1, :], True, True).then_inc(sum_pe, 1)

            pe.wait_ge(ln_in, 64)
            turn(bank[7][:, 0:64], lnrow[:, :], 64).then_inc(setup_pe, 1)
            norm(0)
            for half in range(2):
                def ffn_in(i, half=half):
                    for k in range(8):
                        if half == 0 and k % 2 == 0:
                            pe.wait_ge(*((x1l_done, 2 * k + 4) if k < 4 else (x1l_rest, 2 * k - 4)))
                        chunk_products(PH_F1[half], i, k, 4 * (k // 2), X1H, X1L, 2 * (k % 2), k < 2, k >= 6,
                                       free_wait(PH_F1[half], i, k % 2), None, 4, 2)
                loop(pe, PH_F1[half], ffn_in)
                pe.wait_ge(hl_done, 22 * half + 22)
                for j in range(4):
                    for k in range(11):
                        chunk_products(PH_F2[half], 0, 11 * j + k, 2 * k, HH, HL, 0, k == 0, k == 10, free_wait(PH_F2[half], 0, j))
            norm(1)
            for k in range(KT):
                pe.wait_ge(y_done, 8 + k + 1)
                if k >= 8:
                    pe.wait_ge((yt_even, yt_odd)[k % 2], k // 2 - 3)
                b = bank[k % 8]
                turn(b[:, 0:P], U[:, k, 0:P])
                turn(b[:, P:2 * P], U[:, k, P:2 * P])
                turn(b[0:NS, 256:384], U[:, k, SEQ:T]).then_inc(yt_pe, 1)


_INS = ["x_prompt", "x_sample", "cache_a", "cache_b1", "cache_b2", "cache_b3", "rel_bias", "w_in", "a_sink",
        "w_oa", "w_ob", "w_out", "ln1_g", "ln1_b", "w_ffn_in", "w_ffn_out", "ln2_g", "ln2_b"]
_CONSTS = ["ohp", "maskp", "ohb", "oha", "maskb", "maska", "ident", "rowsel"]
_OUTS = [(1, 256, 2048), (8, 4, 2048), (1, 1, 128, 2, 2, 64), (1, 1, 128, 2, 8, 64), (1, 1, 256, 2, 8, 64),
         (1, 1, 256, 2, 8, 64), (1, 8, 128, 2, 2, 64), (1, 8, 128, 2, 8, 64), (1, 8, 512, 2, 8, 64),
         (1, 8, 2048, 2, 8, 64)]


def kernel(**inputs):
    import numpy as _np
    import concourse.bacc as _bacc
    from concourse import mybir as _mybir
    from concourse.bass_utils import run_bass_kernel_spmd as _run

    nc = _bacc.Bacc("TRN2", target_bir_lowering=False, num_devices=1)
    arrays, args = {}, []
    consts = constants()
    for name in _INS + _CONSTS:
        a = _np.ascontiguousarray(consts[name] if name in consts else inputs[name])
        arrays[f"in_{name}_dram"] = a
        args.append(nc.dram_tensor(f"in_{name}_dram", a.shape, _mybir.dt.from_np(a.dtype), kind="ExternalInput").ap())
    for i, shape in enumerate(_OUTS):
        args.append(nc.dram_tensor(f"out_{i}_dram", shape, _mybir.dt.float32, kind="ExternalOutput").ap())
    build(nc, *args)
    r = _run(nc, [arrays], core_ids=[0])
    return tuple(r.results[0][f"out_{i}_dram"] for i in range(len(_OUTS)))
```
